# Optimizing a Trainium2 kernel written in Bass

```python
import jax
import jax.numpy as jnp
from jax import lax
import numpy as np

D_MODEL = 2048
BATCH = 1
SEQ = 256
DEPTH = 1

HEAD_DIM = 128
ROPE_THETA = 10000.0
NORM_EPS = 1e-6
Q_BLOCK = 128
NEG_INF = -1e30
TINY = 1e-30

NSA_HEADS = 8
NSA_KV_GROUPS = 2
NSA_HPG = NSA_HEADS // NSA_KV_GROUPS
CMP_BLOCK = 32
CMP_STRIDE = 16
CMP_HIDDEN = 256
SEL_BLOCK = 64
SEL_TOPK = 16
SEL_Q_CHUNK = 32
FORCED_SCORE = 1e4
WINDOW = 512

FOX_HEADS = 8

PEER_HEADS = 8
PEER_N_KEYS = 128
PEER_N_EXPERTS = PEER_N_KEYS * PEER_N_KEYS
PEER_KEY_DIM = 256
PEER_HALF = PEER_KEY_DIM // 2
PEER_TOPK = 16
PEER_TOKEN_CHUNK = 128

NSA_Q_W = NSA_HEADS * HEAD_DIM
NSA_KV_W = NSA_KV_GROUPS * HEAD_DIM
NSA_GATE_W = 3 * NSA_HEADS
FOX_W = FOX_HEADS * HEAD_DIM
IN_WIDTHS = (NSA_Q_W, NSA_KV_W, NSA_KV_W, NSA_KV_W, NSA_KV_W, NSA_KV_W, NSA_KV_W, NSA_GATE_W, FOX_W, FOX_W, FOX_W, FOX_HEADS, D_MODEL, D_MODEL)
IN_TOTAL = sum(IN_WIDTHS)

kernel_name = 'nsa_fox_peer_hybrid_block'

def rms_norm(x, g):
    xf = x.astype(jnp.float32)
    y = xf * lax.rsqrt(jnp.mean(xf * xf, axis=-1, keepdims=True) + NORM_EPS)
    return (y * g.astype(jnp.float32)).astype(x.dtype)

def rope_cos_sin(pos):
    inv_freq = ROPE_THETA ** (-jnp.arange(0, HEAD_DIM, 2, dtype=jnp.float32) / HEAD_DIM)
    ang = pos.astype(jnp.float32)[:, None] * inv_freq[None, :]
    return jnp.cos(ang), jnp.sin(ang)

def apply_rope(x, cos, sin):
    half = HEAD_DIM // 2
    xf = x.astype(jnp.float32)
    x1, x2 = xf[..., :half], xf[..., half:]
    c, s = cos[None, :, None, :], sin[None, :, None, :]
    return jnp.concatenate([x1 * c - x2 * s, x2 * c + x1 * s], axis=-1).astype(x.dtype)

def masked_softmax(s, mask):
    s = jnp.where(mask, s.astype(jnp.float32), NEG_INF)
    m = jnp.max(s, axis=-1, keepdims=True)
    e = jnp.where(mask, jnp.exp(s - m), 0.0)
    return e / jnp.maximum(jnp.sum(e, axis=-1, keepdims=True), TINY)

def compress(tok, pos_emb, w1, w2):
    B, S, G, D = tok.shape
    n_chunks = S // CMP_STRIDE
    ratio = CMP_BLOCK // CMP_STRIDE
    n_blk = n_chunks - ratio + 1
    chunks = tok.reshape(B, n_chunks, CMP_STRIDE, G, D)
    blocks = jnp.concatenate([chunks[:, m:m + n_blk] for m in range(ratio)], axis=2)
    blocks = blocks + pos_emb[None, None, :, None, :]
    flat = blocks.transpose(0, 1, 3, 2, 4).reshape(B, n_blk, G, CMP_BLOCK * D)
    return jax.nn.gelu(flat @ w1) @ w2

def nsa_compressed(q, kc, vc):
    S, Nc = q.shape[1], kc.shape[1]
    s = jnp.einsum('bsghd,bngd->bghsn', q, kc) * (HEAD_DIM ** -0.5)
    t = jnp.arange(S)
    end = jnp.arange(Nc) * CMP_STRIDE + CMP_BLOCK - 1
    p = masked_softmax(s, end[None, :] <= t[:, None])
    o = jnp.einsum('bghsn,bngd->bsghd', p.astype(vc.dtype), vc)
    return o, p

def select_blocks(p_cmp):
    S, Nc = p_cmp.shape[3], p_cmp.shape[4]
    Ns = S // SEL_BLOCK
    c_start = np.arange(Nc) * CMP_STRIDE
    s_start = np.arange(Ns) * SEL_BLOCK
    overlap = (c_start[:, None] < s_start[None, :] + SEL_BLOCK) & (s_start[None, :] < c_start[:, None] + CMP_BLOCK)
    imp = jnp.einsum('bghsn,nj->bgsj', p_cmp, jnp.asarray(overlap, jnp.float32))
    t = jnp.arange(S)
    cur = t // SEL_BLOCK
    j = jnp.arange(Ns)
    forced = (j[None, :] == 0) | (j[None, :] == cur[:, None]) | (j[None, :] == cur[:, None] - 1)
    future = j[None, :] * SEL_BLOCK > t[:, None]
    score = jnp.where(forced, FORCED_SCORE, imp)
    score = jnp.where(future, NEG_INF, score)
    _, idx = lax.top_k(score, min(SEL_TOPK, Ns))
    return idx

def nsa_selected(q, k, v, idx):
    B, S, G, Hg, D = q.shape
    Ns = S // SEL_BLOCK
    n = idx.shape[-1]
    kb = k.reshape(B, Ns, SEL_BLOCK, G, D).transpose(0, 3, 1, 2, 4)
    vb = v.reshape(B, Ns, SEL_BLOCK, G, D).transpose(0, 3, 1, 2, 4)
    C = SEL_Q_CHUNK
    nC = S // C
    qc = q.reshape(B, nC, C, G, Hg, D).transpose(1, 0, 2, 3, 4, 5)
    ic = idx.reshape(B, G, nC, C, n).transpose(2, 0, 1, 3, 4)
    gather = jax.vmap(jax.vmap(lambda tab, ix: tab[ix]))
    scale = HEAD_DIM ** -0.5

    def chunk(args):
        qi, ii, c0 = args
        kg = gather(kb, ii)
        vg = gather(vb, ii)
        s = jnp.einsum('bcghd,bgcnkd->bghcnk', qi, kg) * scale
        tq = c0 + jnp.arange(C)
        kpos = ii[..., None] * SEL_BLOCK + jnp.arange(SEL_BLOCK)
        mask = (kpos <= tq[None, None, :, None, None]).reshape(B, G, 1, C, n * SEL_BLOCK)
        p = masked_softmax(s.reshape(B, G, Hg, C, n * SEL_BLOCK), mask).reshape(B, G, Hg, C, n, SEL_BLOCK)
        return jnp.einsum('bghcnk,bgcnkd->bcghd', p.astype(vg.dtype), vg)

    o = lax.map(chunk, (qc, ic, jnp.arange(nC) * C))
    return o.transpose(1, 0, 2, 3, 4, 5).reshape(B, S, G, Hg, D)

def nsa_window(q, k, v):
    B, S, G, Hg, D = q.shape
    nQ = S // Q_BLOCK
    L = Q_BLOCK + WINDOW
    kp = jnp.pad(k, ((0, 0), (WINDOW, 0), (0, 0), (0, 0)))
    vp = jnp.pad(v, ((0, 0), (WINDOW, 0), (0, 0), (0, 0)))
    qb = q.reshape(B, nQ, Q_BLOCK, G, Hg, D).transpose(1, 0, 2, 3, 4, 5)
    scale = HEAD_DIM ** -0.5

    def blk(args):
        qi, i = args
        start = i * Q_BLOCK
        ki = lax.dynamic_slice_in_dim(kp, start, L, axis=1)
        vi = lax.dynamic_slice_in_dim(vp, start, L, axis=1)
        s = jnp.einsum('bqghd,bkgd->bghqk', qi, ki) * scale
        tq = start + jnp.arange(Q_BLOCK)
        spos = start - WINDOW + jnp.arange(L)
        diff = tq[:, None] - spos[None, :]
        mask = (spos[None, :] >= 0) & (diff >= 0) & (diff < WINDOW)
        p = masked_softmax(s, mask)
        return jnp.einsum('bghqk,bkgd->bqghd', p.astype(vi.dtype), vi)

    o = lax.map(blk, (qb, jnp.arange(nQ)))
    return o.transpose(1, 0, 2, 3, 4, 5).reshape(B, S, G, Hg, D)

def fox_attention(q, k, v, log_f):
    B, S, H, D = q.shape
    nQ = S // Q_BLOCK
    c = lax.cumsum(log_f, axis=1).transpose(0, 2, 1)
    qb = q.reshape(B, nQ, Q_BLOCK, H, D).transpose(1, 0, 2, 3, 4)
    cb = c.reshape(B, H, nQ, Q_BLOCK).transpose(2, 0, 1, 3)
    scale = D ** -0.5
    kpos = jnp.arange(S)

    def blk(args):
        qi, ci, i = args
        s = jnp.einsum('bqhd,bkhd->bhqk', qi, k).astype(jnp.float32) * scale + ci[..., None] - c[:, :, None, :]
        tq = i * Q_BLOCK + jnp.arange(Q_BLOCK)
        p = masked_softmax(s, kpos[None, :] <= tq[:, None])
        return jnp.einsum('bhqk,bkhd->bqhd', p.astype(v.dtype), v)

    o = lax.map(blk, (qb, cb, jnp.arange(nQ)))
    return o.transpose(1, 0, 2, 3, 4).reshape(B, S, H, D)

def peer(x, w_query, sub_keys_1, sub_keys_2, expert_down, expert_up):
    B, S, D = x.shape
    T = B * S
    xt = x.reshape(T, D)
    q = (xt @ w_query).reshape(T, PEER_HEADS, PEER_KEY_DIM)
    s1 = jnp.einsum('thd,hkd->thk', q[..., :PEER_HALF], sub_keys_1).astype(jnp.float32)
    s2 = jnp.einsum('thd,hkd->thk', q[..., PEER_HALF:], sub_keys_2).astype(jnp.float32)
    v1, i1 = lax.top_k(s1, PEER_TOPK)
    v2, i2 = lax.top_k(s2, PEER_TOPK)
    cand = (v1[..., :, None] + v2[..., None, :]).reshape(T, PEER_HEADS, PEER_TOPK * PEER_TOPK)
    cand_idx = (i1[..., :, None] * PEER_N_KEYS + i2[..., None, :]).reshape(T, PEER_HEADS, PEER_TOPK * PEER_TOPK)
    top_s, pos = lax.top_k(cand, PEER_TOPK)
    eidx = jnp.take_along_axis(cand_idx, pos, axis=-1)
    g = jax.nn.softmax(top_s, axis=-1)
    C = PEER_TOKEN_CHUNK
    nC = T // C
    HK = PEER_HEADS * PEER_TOPK

    def chunk(args):
        xi, ei, gi = args
        u = expert_down[ei]
        a = jax.nn.gelu(jnp.einsum('cd,ced->ce', xi, u)).astype(jnp.float32)
        w = (a * gi).astype(xi.dtype)
        return jnp.einsum('ce,ced->cd', w, expert_up[ei])

    out = lax.map(chunk, (xt.reshape(nC, C, D), eidx.reshape(nC, C, HK), g.reshape(nC, C, HK)))
    return out.reshape(B, S, D)

def setup_inputs(seed: int = 0) -> dict:
    key = jax.random.key(seed)
    ks = jax.random.split(key, 24)
    f32 = jnp.float32

    def nrm(k, shape, scale):
        return jax.random.normal(k, shape, f32) * scale

    return {
        'x': nrm(ks[0], (BATCH, SEQ, D_MODEL), 1.0),
        'norm_mix_gain': 1.0 + nrm(ks[1], (DEPTH, D_MODEL), 0.05),
        'w_in': nrm(ks[2], (DEPTH, D_MODEL, IN_TOTAL), D_MODEL ** -0.5),
        'nsa_gate_bias': nrm(ks[3], (DEPTH, NSA_GATE_W), 0.1),
        'fox_forget_bias': 3.0 + nrm(ks[4], (DEPTH, FOX_HEADS), 0.5),
        'merge_gate_bias': nrm(ks[5], (DEPTH, 2 * D_MODEL), 0.1),
        'k_cmp_pos': nrm(ks[6], (DEPTH, CMP_BLOCK, HEAD_DIM), 0.1),
        'k_cmp_w1': nrm(ks[7], (DEPTH, CMP_BLOCK * HEAD_DIM, CMP_HIDDEN), (CMP_BLOCK * HEAD_DIM) ** -0.5),
        'k_cmp_w2': nrm(ks[8], (DEPTH, CMP_HIDDEN, HEAD_DIM), CMP_HIDDEN ** -0.5),
        'v_cmp_pos': nrm(ks[9], (DEPTH, CMP_BLOCK, HEAD_DIM), 0.1),
        'v_cmp_w1': nrm(ks[10], (DEPTH, CMP_BLOCK * HEAD_DIM, CMP_HIDDEN), (CMP_BLOCK * HEAD_DIM) ** -0.5),
        'v_cmp_w2': nrm(ks[11], (DEPTH, CMP_HIDDEN, HEAD_DIM), CMP_HIDDEN ** -0.5),
        'w_up_nsa': nrm(ks[12], (DEPTH, NSA_Q_W, D_MODEL), NSA_Q_W ** -0.5),
        'w_up_fox': nrm(ks[13], (DEPTH, FOX_W, D_MODEL), FOX_W ** -0.5),
        'w_out': nrm(ks[14], (DEPTH, D_MODEL, D_MODEL), D_MODEL ** -0.5),
        'norm_ffn_gain': 1.0 + nrm(ks[15], (DEPTH, D_MODEL), 0.05),
        'peer_w_query': nrm(ks[16], (DEPTH, D_MODEL, PEER_HEADS * PEER_KEY_DIM), D_MODEL ** -0.5),
        'peer_sub_keys_1': nrm(ks[17], (DEPTH, PEER_HEADS, PEER_N_KEYS, PEER_HALF), PEER_HALF ** -0.5),
        'peer_sub_keys_2': nrm(ks[18], (DEPTH, PEER_HEADS, PEER_N_KEYS, PEER_HALF), PEER_HALF ** -0.5),
        'peer_expert_down': nrm(ks[19], (DEPTH, PEER_N_EXPERTS, D_MODEL), D_MODEL ** -0.5),
        'peer_expert_up': nrm(ks[20], (DEPTH, PEER_N_EXPERTS, D_MODEL), 0.5),
        'norm_final_gain': 1.0 + nrm(ks[21], (D_MODEL,), 0.05),
    }

def reference(x, norm_mix_gain, w_in, nsa_gate_bias, fox_forget_bias, merge_gate_bias, k_cmp_pos, k_cmp_w1, k_cmp_w2, v_cmp_pos, v_cmp_w1, v_cmp_w2, w_up_nsa, w_up_fox, w_out, norm_ffn_gain, peer_w_query, peer_sub_keys_1, peer_sub_keys_2, peer_expert_down, peer_expert_up, norm_final_gain):
    B, S, _ = x.shape
    cos_t, sin_t = rope_cos_sin(jnp.arange(S))
    n_cmp = S // CMP_STRIDE - CMP_BLOCK // CMP_STRIDE + 1
    cos_c, sin_c = rope_cos_sin(jnp.arange(n_cmp) * CMP_STRIDE + CMP_BLOCK - 1)
    split_at = np.cumsum(np.array(IN_WIDTHS))[:-1].tolist()

    def grp(a):
        return a.reshape(B, S, NSA_KV_GROUPS, HEAD_DIM)

    for l in range(DEPTH):
        h = rms_norm(x, norm_mix_gain[l])
        proj = jnp.einsum('bsd,de->bse', h, w_in[l])
        (q_n, k_c, v_c, k_s, v_s, k_w, v_w, g_n, q_f, k_f, v_f, f_f, g_a, g_b) = jnp.split(proj, split_at, axis=-1)

        q_n = apply_rope(q_n.reshape(B, S, NSA_HEADS, HEAD_DIM), cos_t, sin_t).reshape(B, S, NSA_KV_GROUPS, NSA_HPG, HEAD_DIM)
        kc = apply_rope(compress(grp(k_c), k_cmp_pos[l], k_cmp_w1[l], k_cmp_w2[l]), cos_c, sin_c)
        vc = compress(grp(v_c), v_cmp_pos[l], v_cmp_w1[l], v_cmp_w2[l])
        o_cmp, p_cmp = nsa_compressed(q_n, kc, vc)
        idx = select_blocks(p_cmp)
        o_sel = nsa_selected(q_n, apply_rope(grp(k_s), cos_t, sin_t), grp(v_s), idx)
        o_win = nsa_window(q_n, apply_rope(grp(k_w), cos_t, sin_t), grp(v_w))
        gates = jax.nn.sigmoid(g_n + nsa_gate_bias[l]).reshape(B, S, NSA_KV_GROUPS, NSA_HPG, 3)
        o_nsa = (gates[..., 0:1] * o_cmp + gates[..., 1:2] * o_sel + gates[..., 2:3] * o_win).reshape(B, S, NSA_Q_W)

        log_f = jax.nn.log_sigmoid((f_f + fox_forget_bias[l]).astype(jnp.float32))
        o_fox = fox_attention(q_f.reshape(B, S, FOX_HEADS, HEAD_DIM), k_f.reshape(B, S, FOX_HEADS, HEAD_DIM), v_f.reshape(B, S, FOX_HEADS, HEAD_DIM), log_f).reshape(B, S, FOX_W)

        merged = (jax.nn.sigmoid(g_a + merge_gate_bias[l, :D_MODEL]) * (o_nsa @ w_up_nsa[l])
                  + jax.nn.sigmoid(g_b + merge_gate_bias[l, D_MODEL:]) * (o_fox @ w_up_fox[l]))
        x = x + merged @ w_out[l]

        x = x + peer(rms_norm(x, norm_ffn_gain[l]), peer_w_query[l], peer_sub_keys_1[l], peer_sub_keys_2[l], peer_expert_down[l], peer_expert_up[l])
    return rms_norm(x, norm_final_gain)


_drawn_inputs = setup_inputs


def setup_inputs(seed=0):
    import zlib

    import numpy as np

    out = dict(_drawn_inputs(seed))
    spreads = {}
    factors = {'nsa_gate_bias': 2.92, 'k_cmp_pos': 4.273}
    for name, (base, spread) in spreads.items():
        noise = np.random.default_rng([zlib.crc32(name.encode()), seed]).standard_normal(out[name].shape)
        drawn = base * np.exp(spread * noise) if base else spread * noise
        out[name] = jnp.asarray(drawn.astype(out[name].dtype))
    for name, factor in factors.items():
        out[name] = (out[name] * factor).astype(out[name].dtype)
    return out
```

```python
from contextlib import ExitStack

import numpy as np

import concourse.bass as bass
from concourse import mybir

F32 = mybir.dt.float32
F32R = mybir.dt.float32r
U32 = mybir.dt.uint32
ALU = mybir.AluOpType
ACT = mybir.ActivationFunctionType
AX_X = mybir.AxisListType.X

P = 128
SEQ = 256
D = 2048
HALVES = SEQ // P
HD = 128
ROT = HD // 2
KC = D // P
NSA_H, GROUPS, HPG = 8, 2, 4
FOX_H = 8
CMP_STRIDE, CMP_BLOCK, CMP_HID = 16, 32, 256
NCMP = SEQ // CMP_STRIDE - CMP_BLOCK // CMP_STRIDE + 1
SCALE = float(HD) ** -0.5
EPS = 1e-6
NEG = -1e30
TINY = 1e-30
GELU_C0, GELU_C1 = 0.7978845608028654, 0.044715
PEER_H, NKEYS, TOPK = 8, 128, 16
SLOTS = PEER_H * TOPK
LOWEST = -3.0e38

Q_N, KV_C, KV_S, KV_W, G_N = 0, 1024, 1536, 2048, 2560
Q_F, V_F, F_F, G_A = 2584, 4632, 5656, 5664
NGATE = 3 * NSA_H

CT = {}


def _columns():
    at = 0
    for name, n in (("ident", P), ("tri", P), ("mask", 384), ("cos", HALVES * ROT), ("sin", HALVES * ROT),
                    ("cosc", ROT), ("sinc", ROT), ("c01", HALVES * NCMP), ("cneg", HALVES * NCMP),
                    ("iota", TOPK), ("augsel", FOX_H)):
        CT[name] = (at, at + n)
        at += n
    return at


NCONST = _columns()


def const_table():
    t = np.zeros((P, NCONST), np.float32)

    def put(name, a):
        lo, hi = CT[name]
        t[:a.shape[0], lo:hi] = a.reshape(a.shape[0], -1)

    i = np.arange(P)
    put("ident", np.eye(P, dtype=np.float32))
    put("tri", (i[:, None] <= i[None, :]).astype(np.float32))
    causal = np.where(i[None, :] <= i[:, None], 0.0, NEG)
    put("mask", np.concatenate([causal, np.zeros((P, P)), causal], axis=1))
    freq = np.float32(10000.0) ** (-np.arange(0, HD, 2, dtype=np.float32) / np.float32(HD))
    ang = np.arange(SEQ, dtype=np.float32)[:, None] * freq[None, :]
    put("cos", np.cos(ang).reshape(HALVES, P, ROT).transpose(1, 0, 2))
    put("sin", np.sin(ang).reshape(HALVES, P, ROT).transpose(1, 0, 2))
    end = np.arange(NCMP) * CMP_STRIDE + CMP_BLOCK - 1
    angc = end.astype(np.float32)[:, None] * freq[None, :]
    put("cosc", np.cos(angc))
    put("sinc", np.sin(angc))
    seen = (end[None, None, :] <= (i[:, None, None] + P * np.arange(HALVES)[None, :, None]))
    put("c01", seen.astype(np.float32))
    put("cneg", np.where(seen, 0.0, NEG))
    put("iota", np.tile(np.arange(TOPK), (P, 1)))
    sel = np.zeros((2 * FOX_H, FOX_H))
    for h in range(FOX_H):
        sel[h, h] = sel[FOX_H + h, h] = 1.0
    put("augsel", sel)
    return t


PIECES = 4
KPP = 4
GATES0, UPS0, OUT0, QRY0, NBLK = 11, 19, 23, 27, 31
CMP_AFTER = 4
W_IN_COL = [Q_N, Q_N + 512, KV_C, KV_S, KV_W, Q_F, Q_F + 512, Q_F + 1024, Q_F + 1536, V_F, V_F + 512]
TRANSPOSED = {2, 5, 6, 7, 8}

UNITS = [("fox", h) for h in range(FOX_H)] + [(b, h) for h in range(NSA_H) for b in ("sel", "win")]
NU = len(UNITS)
NSETUP = 12
P_RING = 4

GS = 8
GPH = SLOTS // GS
NG = HALVES * GPH
RING = 4


def build(nc, x, norm_mix_gain, w_in, nsa_gate_bias, fox_forget_bias, merge_gate_bias, k_cmp_pos, k_cmp_w1,
          k_cmp_w2, v_cmp_pos, v_cmp_w1, v_cmp_w2, w_up_nsa, w_up_fox, w_out, norm_ffn_gain, peer_w_query,
          peer_sub_keys_1, peer_sub_keys_2, peer_expert_down, peer_expert_up, norm_final_gain, consts, out):
    with ExitStack() as ctx:
        def sem(name):
            return ctx.enter_context(nc.semaphore(name))

        base = -(-nc.sbuf_base // 512) * 512

        def at(name, shape, kb, dt=F32):
            n = int(np.prod(shape[1:])) * 4
            assert base + kb * 1024 + n <= nc.sbuf_usable_end, name
            return nc.alloc_sbuf_tensor_at(name, shape, dt, offset=int(base + kb * 1024))

        ct = at("ct", [P, NCONST], 0)
        cols = at("cols", [P, P], 4.5)
        rows = at("rows", [64, 2, P], 5)
        ones = at("ones", [P, P], 6)
        small = at("small", [P, 896], 6.5)
        MERGE_B, MIX_G, FFN_G, KPOS, VPOS = 0, 32, 48, 64, 96
        cut = [0]

        def tile(*dims, dt=F32, parts=P):
            n = int(np.prod(dims))
            a = small[0:parts, cut[0]:cut[0] + n]
            cut[0] += n
            assert cut[0] <= 896
            if len(dims) > 1:
                names = "abcd"[:len(dims)]
                a = a.rearrange(f"p ({' '.join(names)}) -> p {' '.join(names)}", **dict(zip(names, dims)))
            return a if dt == F32 else a.bitcast(dt)

        def const(name, parts=P):
            lo, hi = CT[name]
            return ct[0:parts, lo:hi]

        ident = const("ident")
        act_hi = at("act_hi", [P, KC, SEQ], 10, F32R)
        act_lo = at("act_lo", [P, KC, SEQ], 26, F32R)
        raw = at("raw", [P, PIECES, KPP, 512], 42)
        w_hi = at("w_hi", [P, 2, KPP, 512], 74, F32R)
        w_lo = at("w_lo", [P, 2, KPP, 512], 90, F32R)
        qkfT = at("qkfT", [P, 2 * FOX_H, SEQ], 106)
        vf = at("vf", [P, HALVES, 1024], 122)
        kvsw = at("kvsw", [P, HALVES, 2, 4, HD], 130)
        gateT = at("gateT", [P, 32, SEQ], 106)
        keysT = at("keysT", [P, 2 * PEER_H, NKEYS], 106)
        keys = at("keys", [P, 2, PEER_H, HD], 114)
        ffn_row = at("ffn_row", [P, D], 122)
        final_row = at("final_row", [P, D], 130)
        qn = at("qn", [P, HALVES, NSA_H, HD], 138)
        qnT = at("qnT", [P, NSA_H, SEQ], 146)
        kswT = at("kswT", [P, 2, GROUPS, SEQ], 154)
        kvcT = at("kvcT", [P, 2, GROUPS, SEQ], 158)
        pcT = at("pcT", [NCMP, 2, SEQ], 158)
        aug = at("aug", [2 * FOX_H, 2, SEQ], 160)
        xres = at("xres", [P, HALVES, D], 138)
        o_hi = at("o_hi", [P, 16, SEQ], 162, F32R)
        o_lo = at("o_lo", [P, 16, SEQ], 178, F32R)
        x_in = at("x_in", [P, HALVES, D], 162)
        rt = at("rt", [P, 2, HALVES, NSA_H, ROT], 178)
        flat = at("flat", [P, 2, CMP_BLOCK, GROUPS, NCMP], 186)
        xn = at("xn", [P, HALVES, D], 162)
        qT = at("qT", [P, 2 * PEER_H, SEQ], 178)
        prob = at("prob", [P, P_RING, 384], 194)
        pT = at("pT", [P, 2, 384], 200)
        gf_raw = at("gf_raw", [P, KC, 32], 194)
        gf_hi = at("gf_hi", [P, KC, 32], 196, F32R)
        gf_lo = at("gf_lo", [P, KC, 32], 198, F32R)
        abT = at("abT", [2 * FOX_H, 2, SEQ], 203)
        w2 = at("w2", [P, 2, 2, HD], 205)
        up_a = at("up_a", [P, 4, SEQ], 194)
        up_b = at("up_b", [P, 4, SEQ], 198)
        diag = at("diag", [P, GS, P], 194)
        sq = at("sq", [P, HALVES, D], 106)
        down_rows = at("down_rows", [P, RING, D], 42)
        up_rows = at("up_rows", [P, RING, D], 74)
        onehot = at("onehot", [P, PEER_H, TOPK, TOPK], 10)
        cand = at("cand", [P, 2, TOPK, TOPK], 18)
        cand2 = at("cand2", [P, 2, TOPK * TOPK], 20)
        list2 = at("list2", [P, 4, NKEYS], 22)
        TK = 24.0
        val = at("val", [P, HALVES, PEER_H, 2, TOPK], TK)
        ind = at("ind", [P, HALVES, PEER_H, 2, TOPK], TK + 2, U32)
        top = at("top", [P, HALVES, PEER_H, TOPK], TK + 4)
        pos = at("pos", [P, HALVES, PEER_H, TOPK], TK + 5, U32)
        gw = at("gw", [P, HALVES, PEER_H, TOPK], TK + 6)
        eidx = at("eidx", [P, HALVES, SLOTS], TK + 7, U32)
        pab = at("pab", [P, 2, PEER_H, TOPK], TK + 8, U32)
        pabf = at("pabf", [P, 2, PEER_H, TOPK], TK + 9)
        indf = at("indf", [P, PEER_H, 2, TOPK], TK + 10)
        key12 = at("key12", [P, 2, SLOTS], TK + 11)
        eidf = at("eidf", [P, SLOTS], TK + 12)

        ss = tile(3 * HALVES)
        rms = tile(3 * HALVES)
        rstd = tile(3 * HALVES)
        eps = tile(1)
        bias32 = tile(32)
        hbias = tile(32)
        gz = tile(HALVES, 32)
        nz = tile(HALVES, FOX_H)
        az = tile(HALVES, FOX_H)
        ez = tile(HALVES, FOX_H)
        lz = tile(HALVES, FOX_H)
        lf = tile(HALVES, FOX_H)
        tg = tile(HALVES, NGATE)
        gate = tile(HALVES, NGATE)
        ab = tile(2, HALVES, 2 * FOX_H)
        kcT = tile(GROUPS, NCMP)
        negmax = tile(NU, 2)
        psums = tile(NU, 2)
        prec = tile(NU, 2)
        pscale = tile(NU, 2)
        cmx, csum, crec = tile(16), tile(16), tile(16)
        kc = at("kc", [NCMP, GROUPS, HD], 196)
        crt = at("crt", [NCMP, 2, GROUPS, ROT], 197)
        vc = rows[0:NCMP, 0:2, :]
        cg = at("cg", [P, 6, 2, 2, 2 * NCMP], 200)
        cp = at("cp", [P, 4, HALVES, NSA_H, NCMP], 138)
        dots = at("dots", [P, 7, GS], TK + 12.5)
        idx_stage = at("idx_stage", [P, 2, GS], TK + 12.75, U32)
        soft = at("soft", [P, 4, PEER_H, TOPK], TK + 13)

        psum = ctx.enter_context(nc.psum_tensor("psum", [P, 8, 512], F32))

        x_loaded = sem("x_loaded")
        setup_loaded = sem("setup_loaded")
        raw_loaded = [sem(f"raw_loaded{p}") for p in range(PIECES)]
        xres_loaded = sem("xres_loaded")
        keys_loaded = sem("keys_loaded")
        fin_loaded = sem("fin_loaded")
        stored = sem("stored")
        dve_seq = sem("dve_seq")
        act_seq = sem("act_seq")
        pool_seq = sem("pool_seq")
        const_done = sem("const_done")
        cols_ps = sem("cols_ps")
        cols_done = sem("cols_done")
        hbias_done = sem("hbias_done")
        squares = sem("squares")
        normed = sem("normed")
        xT_ps = sem("xT_ps")
        act_hi_done = sem("act_hi_done")
        act_lo_done = sem("act_lo_done")
        gf_hi_done = sem("gf_hi_done")
        gf_lo_done = sem("gf_lo_done")
        gf_ps = sem("gf_ps")
        gz_done = sem("gz_done")
        fx_done = sem("fx_done")
        lf_done = sem("lf_done")
        cum_ps = sem("cum_ps")
        ab_done = sem("ab_done")
        ab_ps = sem("ab_ps")
        abT_done = sem("abT_done")
        flat_done = sem("flat_done")
        cmp_used = sem("cmp_used")
        ga_done = sem("ga_done")
        gt_done = sem("gt_done")
        gy_done = sem("gy_done")
        kvc_ps = sem("kvc_ps")
        kc_done = sem("kc_done")
        vc_done = sem("vc_done")
        kcr_done = sem("kcr_done")
        kcT_ps = sem("kcT_ps")
        kcT_done = sem("kcT_done")
        roped = sem("roped")
        fill_ps = sem("fill_ps")
        fillA = sem("fillA")
        fillD = sem("fillD")
        cs_ps = sem("cs_ps")
        c2_done = sem("c2_done")
        ce_done = sem("ce_done")
        pc_done = sem("pc_done")
        hi_done = sem("hi_done")
        lo_done = sem("lo_done")
        piece_used = sem("piece_used")
        actA = sem("actA")
        dveA = sem("dveA")
        score_ps = sem("score_ps")
        masked = sem("masked")
        exped = sem("exped")
        scl_ready = sem("scl_ready")
        p_ready = sem("p_ready")
        pT_ps = sem("pT_ps")
        pT_done = sem("pT_done")
        pv_done = sem("pv_done")
        o_hi_done = sem("o_hi_done")
        o_lo_done = sem("o_lo_done")
        pcT_ps = sem("pcT_ps")
        pcT_done = sem("pcT_done")
        aug_done = sem("aug_done")
        up_sum = sem("up_sum")
        mer_hi = sem("mer_hi")
        mer_lo = sem("mer_lo")
        keyT_ps = sem("keyT_ps")
        keyT_done = sem("keyT_done")
        xn_scaled = sem("xn_scaled")
        ks_ps = sem("ks_ps")
        topk_read = sem("topk_read")
        soft_in = sem("soft_in")
        soft_exp = sem("soft_exp")
        eidx_done = sem("eidx_done")
        idx_copied = sem("idx_copied")
        turn = sem("turn")
        down_in = [sem(f"down_in{r}") for r in range(RING)]
        up_in = [sem(f"up_in{r}") for r in range(RING)]
        down_used = sem("down_used")
        up_used = sem("up_used")
        gelu_in = sem("gelu_in")
        gelu_tanh = sem("gelu_tanh")
        ge_sq, ge_poly, ge_in = sem("ge_sq"), sem("ge_poly"), sem("ge_in")
        ge_tanh, ge_y = sem("ge_tanh"), sem("ge_y")
        w_ready = sem("w_ready")
        diag_ready = sem("diag_ready")
        x2_done = sem("x2_done")
        y_done = sem("y_done")

        w_in_v = w_in[0].rearrange("(k p) n -> p k n", p=P)
        w_un_v = w_up_nsa[0].rearrange("(k p) n -> p k n", p=P)
        w_uf_v = w_up_fox[0].rearrange("(k p) n -> p k n", p=P)
        w_out_v = w_out[0].rearrange("(k p) n -> p k n", p=P)
        w_q_v = peer_w_query[0].rearrange("(k p) n -> p k n", p=P)
        x_v = x[0].rearrange("(h p) d -> p h d", p=P)
        out_v = out[0].rearrange("(h p) d -> p h d", p=P)

        def f32(a):
            return a.bitcast(F32)

        def bank_of(b):
            if b < UPS0:
                return 2 * (b % 2)
            return 4 * (b % 2)

        def uses(b):
            return b + 1 + 2 * (1 if not isinstance(b, int) or b > CMP_AFTER else 0)

        def kT_of(kind, h):
            return qkfT[:, FOX_H + h, :] if kind == "fox" else kswT[:, ("sel", "win").index(kind), h // HPG, :]

        def q_of(kind, h):
            return qkfT[:, h, :] if kind == "fox" else qnT[:, h, :]

        def v_of(kind, h, kb):
            if kind == "fox":
                return vf[:, kb, h * HD:(h + 1) * HD]
            return kvsw[:, kb, ("sel", "win").index(kind), GROUPS + h // HPG, :]

        def head_slot(kind, h):
            return h if kind == "fox" else FOX_H + h

        def o_place(hs):
            return NSA_H + hs if hs < FOX_H else hs - FOX_H

        def last_unit(hs):
            return hs if hs < FOX_H else FOX_H + 2 * (hs - FOX_H) + 1

        block = ctx.enter_context(nc.Block())

        @block.sync
        def _(sp):
            sp.dma_start(x_in[:], x_v).then_inc(x_loaded, 16)

            def load(b, src, first=False):
                for p in range(PIECES):
                    if not first:
                        sp.wait_ge(lo_done, 4 * (b - 1) + p + 1)
                    sp.dma_start(raw[:, p], src(p)).then_inc(raw_loaded[p], 16)

            def w_in_piece(col):
                return lambda p: w_in_v[:, KPP * p:KPP * p + KPP, col]

            for b in range(GATES0):
                col = W_IN_COL[b]
                if b == CMP_AFTER + 1:
                    for kv, w1 in enumerate((k_cmp_w1, v_cmp_w1)):
                        w1_v = w1[0].rearrange("(r d) h -> d r h", d=HD)
                        for p in range(PIECES):
                            if kv == 0:
                                sp.wait_ge(lo_done, 4 * (b - 1) + p + 1)
                            else:
                                sp.wait_ge(cmp_used, p + 1)
                            sp.dma_start(raw[:, p].rearrange("p k n -> p (k n)").rearrange("p (r h) -> p r h", h=CMP_HID),
                                         w1_v[:, 8 * p:8 * p + 8, :]).then_inc(raw_loaded[p], 16)
                    for p in range(PIECES):
                        sp.wait_ge(cmp_used, PIECES + p + 1)
                        sp.dma_start(raw[:, p], w_in_piece(slice(col, col + 512))(p)).then_inc(raw_loaded[p], 16)
                else:
                    load(b, w_in_piece(slice(col, col + 512)), first=b == 0)
            with sp.Fori(0, UPS0 - GATES0) as i:
                load(i + GATES0, w_in_piece(bass.ds(i * 512 + G_A, 512)))
            for c in range(4):
                cs = slice(512 * c, 512 * c + 512)
                load(UPS0 + c, lambda p: (w_un_v if p < 2 else w_uf_v)[:, KPP * (p % 2):KPP * (p % 2) + KPP, cs])
            sp.wait_ge(o_hi_done, 16)
            sp.dma_start(xres[:], x_v).then_inc(xres_loaded, 16)
            for c in range(4):
                cs = slice(512 * c, 512 * c + 512)
                load(OUT0 + c, lambda p: w_out_v[:, KPP * p:KPP * p + KPP, cs])
            for c in range(4):
                cs = slice(512 * c, 512 * c + 512)
                load(QRY0 + c, lambda p: w_q_v[:, KPP * p:KPP * p + KPP, cs])
            for half in range(HALVES):
                sp.wait_ge(y_done, half + 1)
                sp.dma_start(out_v[:, half, :], xn[:, half, :]).then_inc(stored, 16)
            sp.wait_ge(stored, 16 * HALVES)

        @block.tensor
        def _(pe):
            def mm(*a, **k):
                return nc.tensor.matmul(*a, skip_group_check=True, **k)

            pe.wait_ge(setup_loaded, 16 * NSETUP)
            nc.tensor.transpose(psum[:, 7, 0:64], rows[:, 0, :], ident[0:64, 0:64])
            nc.tensor.transpose(psum[:, 7, 64:128], rows[:, 1, :], ident[0:64, 0:64]).then_inc(cols_ps, 1)

            def transpose_x(src, n0, bank):
                for k in range(KC):
                    if k >= 2:
                        pe.wait_ge(act_lo_done, n0 + k - 1)
                    for half in range(HALVES):
                        ins = nc.tensor.transpose(psum[:, bank + k % 2, half * P:(half + 1) * P],
                                                  src[:, half, k * P:(k + 1) * P], ident)
                    ins.then_inc(xT_ps, 1)

            pe.wait_ge(normed, 2)
            transpose_x(x_in, 0, 4)

            def nat_piece(hi, lo, p, banks, n=512, kpp=KPP, w0=0):
                for k in range(kpp):
                    kk = kpp * p + k
                    for half in range(HALVES):
                        t = slice(half * P, (half + 1) * P)
                        o = banks[half]
                        mm(o, act_hi[:, kk, t], hi[:, k, :], start=kk == 0, stop=False)
                        mm(o, act_hi[:, kk, t], lo[:, k, :], start=False, stop=False)
                        last = mm(o, act_lo[:, kk, t], hi[:, k, :], start=False, stop=kk == KC - 1)
                return last

            def tr_piece(hi, lo, ahi, alo, k0, bank, nk):
                for k in range(KPP):
                    kk = k0 + k
                    for c in range(4):
                        o = psum[:, bank + c // 2, (c % 2) * SEQ:(c % 2 + 1) * SEQ]
                        cs = slice(c * P, (c + 1) * P)
                        first = kk == 0 and c % 2 == 0
                        mm(o, hi[:, k, cs], ahi[:, kk, :], start=first, stop=False)
                        mm(o, hi[:, k, cs], alo[:, kk, :], start=False, stop=False)
                        last = mm(o, lo[:, k, cs], ahi[:, kk, :], start=False, stop=kk == nk - 1)
                return last

            def weight_block(b, par, kind):
                bank = (2 if kind in ("nat", "tr") else 4) * par
                for p in range(PIECES):
                    pe.wait_ge(lo_done, b * 4 + (p + 1))
                    hi, lo = w_hi[:, p % 2], w_lo[:, p % 2]
                    if kind in ("nat", "out"):
                        last = nat_piece(hi, lo, p, [psum[:, bank, :], psum[:, bank + 1, :]])
                    elif kind in ("tr", "qry"):
                        last = tr_piece(hi, lo, act_hi, act_lo, KPP * p, bank, KC)
                    else:
                        fox = p // 2
                        last = tr_piece(hi, lo, o_hi[:, 8 * fox:8 * fox + 8], o_lo[:, 8 * fox:8 * fox + 8],
                                        KPP * (p % 2), bank + 2 * fox, 2 * KPP)
                    last.then_inc(piece_used, 1)

            def after(b):
                if b == 1:
                    pe.wait_ge(gf_lo_done, 1)
                    pe.wait_ge(cols_done, 1)
                    for half in range(HALVES):
                        t = slice(half * P, (half + 1) * P)
                        o = psum[:, 7, half * 32:half * 32 + 32]
                        for k in range(KC):
                            mm(o, act_hi[:, k, t], gf_hi[:, k, :], start=k == 0, stop=False)
                            mm(o, act_hi[:, k, t], gf_lo[:, k, :], start=False, stop=False)
                            last = mm(o, act_lo[:, k, t], gf_hi[:, k, :], start=False, stop=k == KC - 1)
                    last.then_inc(gf_ps, 1)
                if b == 3:
                    pe.wait_ge(lf_done, 1)
                    tri = const("tri")
                    mm(psum[:, 5, 0:8], tri, lf[:, 0, :], start=True, stop=True)
                    mm(psum[:, 5, 8:16], ones[:], lf[:, 0, :], start=True, stop=False)
                    mm(psum[:, 5, 8:16], tri, lf[:, 1, :], start=False, stop=True).then_inc(cum_ps, 1)
                if b == 4:
                    pe.wait_ge(ab_done, 1)
                    for x_ in range(2):
                        for half in range(HALVES):
                            ins = nc.tensor.transpose(psum[0:16, 4, x_ * SEQ + half * P:x_ * SEQ + (half + 1) * P],
                                                      ab[:, x_, half, :], ident)
                    ins.then_inc(ab_ps, 1)
                    pe.wait_ge(flat_done, 1)
                    pe.wait_ge(gz_done, 1)
                    for kv in range(2):
                        for p in range(PIECES):
                            pe.wait_ge(raw_loaded[p], 16 * (CMP_AFTER + 2 + kv))
                            w1 = raw[:, p].rearrange("p k n -> p (k n)").rearrange("p (r h) -> p r h", h=CMP_HID)
                            for r in range(8):
                                for hc in range(2):
                                    last = mm(psum[:, 6 + kv, hc * 30:hc * 30 + 30], w1[:, r, hc * P:(hc + 1) * P],
                                              flat[:, kv, 8 * p + r, :, :], start=p == 0 and r == 0 and hc == 0,
                                              stop=p == PIECES - 1 and r == 7)
                            last.then_inc(cmp_used, 1)
                if b == 6:
                    pe.wait_ge(gy_done, 1)
                    for kv in range(2):
                        for g in range(GROUPS):
                            for hc in range(2):
                                last = mm(psum[0:NCMP, 6, kv * 256 + g * HD:kv * 256 + (g + 1) * HD],
                                          cg[:, 5, kv, hc, g * NCMP:(g + 1) * NCMP], w2[:, kv, hc, :],
                                          start=hc == 0, stop=hc == 1)
                    last.then_inc(kvc_ps, 1)
                if b == 8:
                    pe.wait_ge(roped, 1)
                    pe.wait_ge(ab_ps, 1)
                    pe.wait_ge(abT_done, 1)
                    pe.wait_ge(ab_done, 1)
                    pe.wait_ge(kc_done, 1)
                    pe.wait_ge(vc_done, 1)
                    pe.wait_ge(ga_done, 2)
                    for f in range(4):
                        for hh in range(2):
                            for half in range(HALVES):
                                ins = nc.tensor.transpose(
                                    psum[:, 4 + f, hh * SEQ + half * P:hh * SEQ + (half + 1) * P],
                                    qn[:, half, 2 * f + hh, :], ident)
                        ins.then_inc(fill_ps, 1)
                if b == 9:
                    pe.wait_ge(roped, 3)
                    for f in range(2):
                        pe.wait_ge(fillA, 2)
                        for g in range(GROUPS):
                            for half in range(HALVES):
                                ins = nc.tensor.transpose(
                                    psum[:, 4 + f, g * SEQ + half * P:g * SEQ + (half + 1) * P],
                                    kvsw[:, half, f, g, :], ident)
                        ins.then_inc(fill_ps, 1)
                    pe.wait_ge(kcr_done, 1)
                    pe.wait_ge(fillD, 2)
                    for g in range(GROUPS):
                        ins = nc.tensor.transpose(psum[:, 6, g * NCMP:(g + 1) * NCMP], kc[:, g, :],
                                                  ident[0:NCMP, 0:NCMP])
                    ins.then_inc(kcT_ps, 1)
                if b == 10:
                    pe.wait_ge(kcT_done, 1)
                    pe.wait_ge(fillA, 3)
                    pe.wait_ge(fillD, 3)
                    for half in range(HALVES):
                        for h in range(NSA_H):
                            last = mm(psum[:, 7, (half * NSA_H + h) * 16:(half * NSA_H + h) * 16 + NCMP],
                                      qnT[:, h, half * P:(half + 1) * P], kcT[:, h // HPG, :],
                                      start=half == 0 and h == 0, stop=True)
                    last.then_inc(cs_ps, 1)

            pe.wait_ge(act_lo_done, KC)
            for b in range(GATES0):
                if b >= 2:
                    pe.wait_ge(actA, b - 1)
                    pe.wait_ge(dveA, b - 1)
                weight_block(b, b % 2, "tr" if b in TRANSPOSED else "nat")
                after(b)

            def score(u):
                kind, h = UNITS[u]
                if u >= 2:
                    pe.wait_ge(masked, u - 1)
                q, k = q_of(kind, h), kT_of(kind, h)
                if kind == "fox":
                    pe.wait_ge(aug_done, h + 1)
                S = psum[:, u % 2, :]
                for half in range(HALVES):
                    n = P * (half + 1)
                    o = S[:, P * half:P * half + n]
                    last = mm(o, q[:, half * P:(half + 1) * P], k[:, 0:n], start=True, stop=kind != "fox")
                    if kind == "fox":
                        last = mm(o, aug[:, h % 2, half * P:(half + 1) * P], abT[:, 1, 0:n], start=False, stop=True)
                last.then_inc(score_ps, 1)

            def trans(u):
                pe.wait_ge(p_ready, u + 1)
                if u >= 2:
                    pe.wait_ge(pT_done, u - 1)
                for j in range(3):
                    ins = nc.tensor.transpose(psum[:, 2 + u % 2, j * P:(j + 1) * P],
                                              prob[:, u % P_RING, j * P:(j + 1) * P], ident)
                ins.then_inc(pT_ps, 1)

            def cmp_trans(h):
                if h == 0:
                    pe.wait_ge(pc_done, 1)
                if h >= 1:
                    pe.wait_ge(pcT_done, h)
                for half in range(HALVES):
                    ins = nc.tensor.transpose(psum[0:NCMP, 6, half * P:(half + 1) * P],
                                              cp[:, 3, half, h, :], ident)
                ins.then_inc(pcT_ps, 1)

            def pv(u):
                kind, h = UNITS[u]
                hs = head_slot(kind, h)
                o = psum[:, 4 + hs % 2, 0:SEQ]
                begins = kind != "win"
                if begins and hs >= 2:
                    pe.wait_ge(o_lo_done, hs - 1)
                if kind == "sel":
                    pe.wait_ge(pcT_done, h + 1)
                    mm(o, vc[:, h // HPG, :], pcT[:, h % 2, :], start=True, stop=False)
                pe.wait_ge(pT_done, u + 1)
                pt = pT[:, u % 2, :]
                mm(o, v_of(kind, h, 0), pt[:, 0:SEQ], start=kind == "fox", stop=False)
                mm(o[:, P:SEQ], v_of(kind, h, 1), pt[:, SEQ:SEQ + P], start=False,
                   stop=kind != "sel").then_inc(pv_done, 1)

            pe.wait_ge(actA, GATES0)
            pe.wait_ge(dveA, GATES0)
            pe.wait_ge(abT_done, 1)
            for t in range(NU + 3):
                if t < NU:
                    score(t)
                    kind, h = UNITS[t]
                    if kind == "sel":
                        cmp_trans(h)
                if 2 <= t < NU + 2:
                    trans(t - 2)
                if t >= 3:
                    pv(t - 3)

            pe.wait_ge(masked, NU)
            pe.wait_ge(pT_done, NU)
            with pe.Fori(0, (UPS0 - GATES0) // 2) as i:
                for q in range(2):
                    b = i * 2 + (GATES0 + q)
                    pe.wait_ge(actA, i * 2 + (GATES0 + q - 1))
                    weight_block(b, (GATES0 + q) % 2, "tr")
            pe.wait_ge(o_lo_done, 16)
            pe.wait_ge(actA, UPS0)
            with pe.Fori(0, 2) as i:
                for q in range(2):
                    pe.wait_ge(dveA, i * 2 + (UPS0 + q - 9))
                    weight_block(i * 2 + (UPS0 + q), (UPS0 + q) % 2, "ups")
            pe.wait_ge(mer_lo, 4)
            with pe.Fori(0, 2) as i:
                for q in range(2):
                    pe.wait_ge(dveA, i * 2 + (OUT0 + q - 9))
                    weight_block(i * 2 + (OUT0 + q), (OUT0 + q) % 2, "out")

            pe.wait_ge(keys_loaded, 32)
            pe.wait_ge(dveA, UPS0 + 2 - 7)
            for f in range(4):
                if f >= 2:
                    pe.wait_ge(keyT_done, f - 1)
                for c in range(4):
                    j = 4 * f + c
                    ins = nc.tensor.transpose(psum[:, 6 + f % 2, c * P:(c + 1) * P], keys[:, j % 2, j // 2, :], ident)
                ins.then_inc(keyT_ps, 1)

            pe.wait_ge(normed, 4)
            pe.wait_ge(keyT_done, 4)
            transpose_x(xn, KC, 6)
            pe.wait_ge(act_lo_done, 2 * KC)
            with pe.Fori(0, 2) as i:
                for q in range(2):
                    pe.wait_ge(dveA, i * 2 + (QRY0 + q - 9))
                    pe.wait_ge(actA, i * 2 + (QRY0 + q - 9))
                    weight_block(i * 2 + (QRY0 + q), (QRY0 + q) % 2, "qry")
            pe.wait_ge(actA, NBLK - 8)
            pe.wait_ge(dveA, NBLK - 8)
            for half in range(HALVES):
                for j in range(2 * PEER_H):
                    last = mm(psum[:, 4 * half + j // 4, (j % 4) * NKEYS:(j % 4 + 1) * NKEYS],
                              qT[:, j, half * P:(half + 1) * P], keysT[:, j, :], start=True, stop=True)
                last.then_inc(ks_ps, 1)

            def up_step(G, half, first=False, end=False):
                for s in range(GS):
                    pe.wait_ge(up_in[s % RING], G * 32 + (s // RING + 1) * 16)
                    pe.wait_ge(diag_ready, G * GS + (s + 1))
                    for c in range(4):
                        last = mm(psum[:, 4 * half + c, :], diag[:, s, :], up_rows[:, s % RING, 512 * c:512 * c + 512],
                                  start=first and s == 0, stop=end and s == GS - 1)
                    last.then_inc(up_used, 1)

            pe.wait_ge(topk_read, 1)
            for G in range(1, GPH // 2):
                up_step(G - 1, 0, first=G == 1)
            with pe.Fori(GPH // 2, GPH) as i:
                up_step(i - 1, 0)
            up_step(GPH - 1, 0, end=True)
            pe.wait_ge(topk_read, 2)
            up_step(GPH, 1, first=True)
            with pe.Fori(GPH + 2, NG) as i:
                up_step(i - 1, 1)
            up_step(NG - 1, 1, end=True)

        @block.gpsimd
        def _(pool):
            n = [0]

            def seq(ins):
                ins.then_inc(pool_seq, 1)
                n[0] += 1

            def rope(x1, x2, cos, sin, t1, t2, done, count):
                tt = nc.gpsimd.tensor_tensor
                seq(tt(t1, x1, sin, ALU.mult))
                seq(tt(t2, x2, sin, ALU.mult))
                pool.wait_ge(pool_seq, n[0])
                seq(tt(x1, x1, cos, ALU.mult))
                seq(tt(x2, x2, cos, ALU.mult))
                pool.wait_ge(pool_seq, n[0])
                seq(tt(x1, x1, t2, ALU.subtract))
                pool.wait_ge(pool_seq, n[0])
                tt(x2, x2, t1, ALU.add).then_inc(done, 1)
                pool.wait_ge(done, count)

            def table(name, heads):
                t = const(name).rearrange("p (h r) -> p h r", h=HALVES)
                return t.unsqueeze(2).to_broadcast([P, HALVES, heads, ROT])

            pool.wait_ge(setup_loaded, 16 * NSETUP)
            pool.wait_ge(actA, 2)
            pool.wait_ge(dveA, 2)
            rope(qn[:, :, :, 0:ROT], qn[:, :, :, ROT:HD], table("cos", NSA_H), table("sin", NSA_H),
                 rt[:, 0], rt[:, 1], roped, 1)
            pool.wait_ge(actA, 5)
            pool.wait_ge(dveA, 5)
            for sw in range(2):
                rope(kvsw[:, :, sw, 0:GROUPS, 0:ROT], kvsw[:, :, sw, 0:GROUPS, ROT:HD], table("cos", GROUPS),
                     table("sin", GROUPS), rt[:, 0, :, 0:GROUPS], rt[:, 1, :, 0:GROUPS], roped, sw + 2)

            def ctable(name):
                return const(name, NCMP).unsqueeze(1).to_broadcast([NCMP, GROUPS, ROT])

            pool.wait_ge(kc_done, 1)
            rope(kc[:, :, 0:ROT], kc[:, :, ROT:HD], ctable("cosc"), ctable("sinc"), crt[:, 0], crt[:, 1], kcr_done, 1)

            pool.wait_ge(abT_done, 1)
            asel = const("augsel", 2 * FOX_H)

            def make_aug(h):
                if h >= 2:
                    pool.wait_ge(score_ps, h - 1)
                nc.gpsimd.tensor_scalar(aug[:, h % 2, :], abT[:, 0, :], asel[:, h:h + 1], None, ALU.mult).then_inc(aug_done, 1)

            pool.wait_ge(flat_done, 1)
            make_aug(0)
            make_aug(1)
            for u in range(NU):
                pool.wait_ge(scl_ready, u + 1)
                nc.gpsimd.tensor_scalar(prob[:, u % P_RING, 0:P], prob[:, u % P_RING, 0:P],
                                        pscale[:, u, 0:1], None, ALU.mult)
                nc.gpsimd.tensor_scalar(prob[:, u % P_RING, P:384], prob[:, u % P_RING, P:384],
                                        pscale[:, u, 1:2], None, ALU.mult).then_inc(p_ready, 1)
                if u + 2 < FOX_H:
                    make_aug(u + 2)

            copies = [0]

            def fetch(kind, G, half, j, s, loop):
                used, table_, rows_, landed = ((down_used, peer_expert_down[0], down_rows, down_in) if kind == 0 else
                                               (up_used, peer_expert_up[0], up_rows, up_in))
                if loop or G > 0 or s >= RING:
                    pool.wait_ge(used, G * GS + (s - RING + 1))
                    pool.sem_inc(turn, 1)
                if s % RING == 0:
                    nc.gpsimd.tensor_copy(idx_stage[:, kind, s:s + RING],
                                          eidx[:, half, bass.ds(j * GS + s, RING)] if loop else
                                          eidx[:, half, j * GS + s:j * GS + s + RING]).then_inc(idx_copied, 1)
                return used, table_, rows_, landed

            def gather(kind, s):
                table_, rows_, landed = ((peer_expert_down[0], down_rows, down_in) if kind == 0 else
                                         (peer_expert_up[0], up_rows, up_in))
                nc.gpsimd.indirect_dma_start(
                    rows_[:, s % RING, :], None, table_,
                    bass.IndirectOffsetOnAxis(ap=idx_stage[:, kind, s:s + 1], axis=0)).then_inc(landed[s % RING], 16)

            def step(G, half, j, loop, down=True, up=True, up_half=None, up_j=None):
                for s in range(GS):
                    for kind in ((0,) if down else ()) + ((1,) if up else ()):
                        if kind == 0:
                            fetch(0, G, half, j, s, loop)
                        else:
                            fetch(1, G - 1, up_half, up_j, s, loop)
                        if s % RING == 0:
                            before = (0 if not up else (G * 4 - 2)) if not loop else G * 4 - 2
                            mine = 1 + (s // RING) * (int(down) + int(up)) + (kind if down else 0)
                            pool.wait_ge(idx_copied, before + mine)
                            if loop:
                                pool.sem_inc(turn, 1)
                        gather(kind, s)

            pool.wait_ge(lo_done, 4 * NBLK)
            pool.wait_ge(piece_used, 4 * NBLK)
            pool.wait_ge(eidx_done, 1)
            step(0, 0, 0, False, up=False)
            for G in range(1, GPH // 2):
                step(G, 0, G, False, up_half=0, up_j=G - 1)
            with pool.Fori(GPH // 2, GPH) as i:
                step(i, 0, i, True, up_half=0, up_j=i - 1)
            pool.wait_ge(eidx_done, 2)
            step(GPH, 1, 0, False, up_half=0, up_j=GPH - 1)
            step(GPH + 1, 1, 1, False, up_half=1, up_j=0)
            with pool.Fori(GPH + 2, NG) as i:
                step(i, 1, i - GPH, True, up_half=1, up_j=i - (GPH + 1))
            step(NG, 1, GPH, False, down=False, up_half=1, up_j=GPH - 1)

        @block.scalar
        def _(act):
            A = nc.scalar.activation
            n = [0]

            def seq(ins):
                ins.then_inc(act_seq, 1)
                n[0] += 1

            def ld(dst, src):
                act.dma_start(dst, src).then_inc(setup_loaded, 16)

            ld(ct[:], consts)
            ld(rows[0:32, 0, :], merge_gate_bias[0].rearrange("(c p) -> c p", p=P))
            ld(rows[32:48, 0, :], norm_mix_gain[0].rearrange("(c p) -> c p", p=P))
            ld(rows[48:64, 0, :], norm_ffn_gain[0].rearrange("(c p) -> c p", p=P))
            ld(rows[0:32, 1, :], k_cmp_pos[0])
            ld(rows[32:64, 1, :], v_cmp_pos[0])
            ld(bias32[:, 0:NGATE], nsa_gate_bias.partition_broadcast(P))
            ld(bias32[:, NGATE:32], fox_forget_bias.partition_broadcast(P))
            ld(gf_raw[:, :, 0:NGATE], w_in_v[:, :, G_N:G_N + NGATE])
            ld(gf_raw[:, :, NGATE:32], w_in_v[:, :, F_F:F_F + FOX_H])
            ld(w2[:, 0], k_cmp_w2[0].rearrange("(c p) d -> p c d", p=P))
            ld(w2[:, 1], v_cmp_w2[0].rearrange("(c p) d -> p c d", p=P))

            def norm_stats(src, junk, i0, halves):
                for i, half in enumerate(halves):
                    seq(A(junk(half), src[:, half, :], ACT.Square, accum_out=ss[:, i0 + i:i0 + i + 1]))
                act.wait_ge(act_seq, n[0])
                A(rms[:, i0:i0 + len(halves)], ss[:, i0:i0 + len(halves)], ACT.Sqrt, bias=eps[:, 0:1],
                  scale=1.0 / D).then_inc(squares, 1)

            def split_x(n0, bank, gain):
                for k in range(KC):
                    act.wait_ge(xT_ps, n0 + k + 1)
                    A(act_hi[:, k, :], psum[:, bank + k % 2, 0:SEQ], ACT.Copy,
                      scale=cols[:, gain + k:gain + k + 1]).then_inc(act_hi_done, 1)

            act.wait_ge(x_loaded, 16)
            act.wait_ge(const_done, 1)
            act.wait_ge(setup_loaded, 16 * NSETUP)
            norm_stats(x_in, lambda half: sq[:, half, :], 0, range(HALVES))
            act.wait_ge(cols_ps, 1)
            nc.scalar.copy(cols[:], psum[:, 7, 0:P]).then_inc(cols_done, 1)
            nc.scalar.copy(gf_hi[:], gf_raw[:]).then_inc(gf_hi_done, 1)
            act.wait_ge(cols_done, 1)
            split_x(0, 4, MIX_G)

            def hi_piece(b, p):
                act.wait_ge(raw_loaded[p], uses(b) * 16)
                if not (isinstance(b, int) and b == 0 and p < 2):
                    act.wait_ge(piece_used, b * 4 + (p - 1))
                nc.scalar.copy(w_hi[:, p % 2], raw[:, p]).then_inc(hi_done, 1)

            def evac(b):
                act.wait_ge(piece_used, 4 * (b + 1))
                bank = psum[:, bank_of(b), :]
                two = bank.rearrange("p (c t) -> p c t", t=SEQ)
                if b < 2:
                    dst = qn[:, 0, 4 * b:4 * b + 4, :].rearrange("p h d -> p (h d)")
                elif b == 2:
                    dst, bank = kvcT[:, 0], two
                elif b < 5:
                    dst = kvsw[:, 0, b - 3].rearrange("p h d -> p (h d)")
                elif b < 9:
                    dst, bank = qkfT[:, 4 * (b - 5):4 * (b - 5) + 2, :], two
                elif b < 11:
                    dst = vf[:, 0, 512 * (b - 9):512 * (b - 9) + 512]
                else:
                    c = b - QRY0
                    dst, bank = qT[:, 4 * c:4 * c + 2, :], psum[:, 4 * (b % 2), :].rearrange("p (c t) -> p c t", t=SEQ)
                nc.scalar.copy(dst, bank).then_inc(actA, 1)

            def hook(b):
                if b == 2:
                    act.wait_ge(fx_done, 1)
                    seq(A(ez[:], az[:], ACT.Exp, scale=-1.0))
                    seq(A(tg[:], gz[:, :, 0:NGATE], ACT.Tanh, scale=0.5))
                    act.wait_ge(act_seq, n[0])
                    A(lz[:], ez[:], ACT.Ln, bias=1.0).then_inc(gt_done, 1)
                if b == 5:
                    act.wait_ge(ab_ps, 1)
                    nc.scalar.copy(abT[:].rearrange("p x t -> p (x t)"), psum[0:2 * FOX_H, 4, :]).then_inc(abT_done, 1)
                    act.wait_ge(cmp_used, 8)
                    for kv in range(2):
                        nc.scalar.copy(cg[:, 0, kv].rearrange("p c n -> p (c n)"), psum[:, 6 + kv, 0:60]).then_inc(ga_done, 1)
                if b == 6:
                    act.wait_ge(gelu_in, 1)
                    A(cg[:, 4], cg[:, 3], ACT.Tanh, scale=GELU_C0).then_inc(gelu_tanh, 1)
                if b == 7:
                    act.wait_ge(kvc_ps, 1)
                    nc.scalar.copy(kc[:].rearrange("p g d -> p (g d)"), psum[0:NCMP, 6, 0:256]).then_inc(kc_done, 1)
                if b == 9:
                    for f in range(2):
                        act.wait_ge(fill_ps, f + 1)
                        nc.scalar.copy(qnT[:, 2 * f:2 * f + 2, :].rearrange("p h t -> p (h t)"), psum[:, 4 + f, :]).then_inc(fillA, 1)
                if b == 10:
                    act.wait_ge(fill_ps, 5)
                    nc.scalar.copy(kswT[:, 0].rearrange("p g t -> p (g t)"), psum[:, 4, :]).then_inc(fillA, 1)
                    act.wait_ge(kcT_ps, 1)
                    nc.scalar.copy(kcT.rearrange("p g n -> p (g n)"), psum[:, 6, 0:2 * NCMP]).then_inc(kcT_done, 1)

            for b in range(GATES0):
                hi_piece(b, 0)
                hi_piece(b, 1)
                if b >= 1:
                    evac(b - 1)
                hook(b)
                hi_piece(b, 2)
                hi_piece(b, 3)
            evac(GATES0 - 1)

            def exp_unit(u):
                act.wait_ge(masked, u + 1)
                pr = prob[:, u % P_RING, :]
                A(pr[:, 0:P], pr[:, 0:P], ACT.Exp, bias=negmax[:, u, 0:1], scale=-1.0, accum_out=psums[:, u, 0:1])
                A(pr[:, P:384], pr[:, P:384], ACT.Exp, bias=negmax[:, u, 1:2], scale=-1.0,
                  accum_out=psums[:, u, 1:2]).then_inc(exped, 1)

            def head_hi(hs):
                act.wait_ge(pv_done, last_unit(hs) + 1)
                nc.scalar.copy(o_hi[:, o_place(hs), :], psum[:, 4 + hs % 2, 0:SEQ]).then_inc(o_hi_done, 1)

            done_at = {last_unit(hs) + 3: hs for hs in range(16)}
            for t in range(NU + 4):
                if t < NU:
                    exp_unit(t)
                    kind, h = UNITS[t]
                    if kind == "sel":
                        act.wait_ge(pcT_ps, h + 1)
                        if h >= 2:
                            act.wait_ge(pv_done, FOX_H + 2 * (h - 2) + 1)
                        nc.scalar.copy(pcT[:, h % 2, :], psum[0:NCMP, 6, 0:SEQ]).then_inc(pcT_done, 1)
                if t == 3:
                    act.wait_ge(c2_done, 1)
                    A(cp[:, 1], cp[:, 0], ACT.Exp).then_inc(ce_done, 1)
                if t - 1 in done_at:
                    head_hi(done_at[t - 1])

            def gate_evac(b, par, loop=None):
                g = b - GATES0
                for c in range(4):
                    src = psum[:, 2 * par + c // 2, (c % 2) * SEQ:(c % 2 + 1) * SEQ]
                    if isinstance(b, int):
                        dst, bias = gateT[:, 4 * g + c, :], hbias[:, 4 * g + c:4 * g + c + 1]
                    else:
                        dst = gateT[:, bass.ds(g * 4 + c, 1), :].rearrange("p o t -> p (o t)")
                        bias = hbias[:, bass.ds(g * 4 + c, 1)]
                    ins = A(dst, src, ACT.Tanh, bias=bias, scale=0.5)
                ins.then_inc(actA, 1)

            def hi4(b, middle):
                hi_piece(b, 0)
                hi_piece(b, 1)
                middle()
                hi_piece(b, 2)
                hi_piece(b, 3)

            def gates_block(b, par):
                def middle():
                    act.wait_ge(piece_used, b * 4)
                    gate_evac(b - 1, 1 - par)
                hi4(b, middle)

            act.wait_ge(hbias_done, 1)
            act.wait_ge(pv_done, NU)
            hi4(GATES0, lambda: None)
            with act.Fori(0, (UPS0 - GATES0) // 2 - 1) as i:
                for q in range(2):
                    gates_block(i * 2 + (GATES0 + 1 + q), (GATES0 + 1 + q) % 2)
            gates_block(UPS0 - 1, (UPS0 - 1) % 2)

            def merged_hi(c):
                act.wait_ge(up_sum, c + 1)
                A(act_hi[:, 4 * c:4 * c + 4, :], up_a[:], ACT.Copy, scale=0.5).then_inc(mer_hi, 1)

            for c in range(4):
                b = UPS0 + c
                hi4(b, (lambda: (act.wait_ge(piece_used, b * 4), gate_evac(b - 1, (b - 1) % 2))) if c == 0 else
                    (lambda: merged_hi(c - 1)))
            for c in range(4):
                hi4(OUT0 + c, (lambda: merged_hi(3)) if c == 0 else (lambda: None))
                if c == 0:
                    act.dma_start(keys[:, 0], peer_sub_keys_1[0].rearrange("h k d -> k h d")).then_inc(keys_loaded, 16)
                    act.dma_start(keys[:, 1], peer_sub_keys_2[0].rearrange("h k d -> k h d")).then_inc(keys_loaded, 16)
                    act.dma_start(ffn_row[:], norm_ffn_gain.partition_broadcast(P)).then_inc(fin_loaded, 16)
                    act.dma_start(final_row[:], norm_final_gain.unsqueeze(0).partition_broadcast(P)).then_inc(fin_loaded, 16)
            for f in range(4):
                act.wait_ge(keyT_ps, f + 1)
                nc.scalar.copy(keysT[:, 4 * f:4 * f + 4, :].rearrange("p j k -> p (j k)"), psum[:, 6 + f % 2, :]).then_inc(keyT_done, 1)
            act.wait_ge(dveA, QRY0 - 8)
            norm_stats(xres, lambda half: xn[:, half, :], HALVES, range(HALVES))
            hi_piece(QRY0, 0)
            split_x(KC, 6, FFN_G)
            for c in range(4):
                b = QRY0 + c
                if c > 0:
                    hi_piece(b, 0)
                hi_piece(b, 1)
                if c > 0:
                    evac(b - 1)
                hi_piece(b, 2)
                hi_piece(b, 3)
            evac(NBLK - 1)

            def soft_half(half):
                act.wait_ge(soft_in, half + 1)
                A(soft[:, 1], soft[:, 0], ACT.Exp).then_inc(soft_exp, 1)

            def step(G, loop=False, middle=None):
                act.wait_ge(ge_in, G + 1)
                A(dots[:, 4, :], dots[:, 3, :], ACT.Tanh, scale=GELU_C0).then_inc(ge_tanh, 1)
                if middle:
                    middle()
                act.wait_ge(w_ready, G + 1)
                for s in range(GS):
                    if loop or G > 0:
                        act.wait_ge(up_used, G * GS + (s + 1 - GS))
                    A(diag[:, s, :], ident, ACT.Copy, scale=dots[:, 6, s:s + 1]).then_inc(diag_ready, 1)

            def final_stats(half):
                act.wait_ge(x2_done, half + 1)
                norm_stats(xres, lambda h: xn[:, h, :], 2 * HALVES + half, [half])

            soft_half(0)
            for G in range(GPH // 2):
                step(G)
            soft_half(1)
            with act.Fori(GPH // 2, GPH) as i:
                step(i, True)
            step(GPH)
            step(GPH + 1, middle=lambda: final_stats(0))
            with act.Fori(GPH + 2, NG) as i:
                step(i, True)
            final_stats(1)

        @block.vector
        def _(dve):
            V = nc.vector
            tt, ts, stt = V.tensor_tensor, V.tensor_scalar, V.scalar_tensor_tensor
            n = [0]

            def seq(ins):
                ins.then_inc(dve_seq, 1)
                n[0] += 1

            def settle():
                dve.wait_ge(dve_seq, n[0])

            V.memset(ones[:], 1.0)
            V.memset(ab[:, 0, :, FOX_H:], 1.0)
            V.memset(ab[:, 1, :, 0:FOX_H], 1.0)
            V.memset(eps, EPS).then_inc(const_done, 1)

            def scale_rows(dst, src, i0, count):
                dve.wait_ge(squares, count)
                seq(V.reciprocal(rstd[:, i0:i0 + HALVES], rms[:, i0:i0 + HALVES]))
                settle()
                for half in range(HALVES):
                    ts(dst[:, half, :], src[:, half, :], rstd[:, i0 + half:i0 + half + 1], None, ALU.mult).then_inc(normed, 1)

            def lo_x(n0, bank, gain):
                for k in range(KC):
                    dve.wait_ge(act_hi_done, n0 + k + 1)
                    stt(act_lo[:, k, :], psum[:, bank + k % 2, 0:SEQ], cols[:, gain + k:gain + k + 1],
                        f32(act_hi[:, k, :]), ALU.mult, ALU.subtract).then_inc(act_lo_done, 1)

            scale_rows(x_in, x_in, 0, 1)
            dve.wait_ge(cols_done, 1)
            ts(hbias, cols[:, MERGE_B:MERGE_B + 32], 0.5, None, ALU.mult).then_inc(hbias_done, 1)
            dve.wait_ge(gf_hi_done, 1)
            tt(gf_lo[:], gf_raw[:], f32(gf_hi[:]), ALU.subtract).then_inc(gf_lo_done, 1)
            lo_x(0, 4, MIX_G)

            def lo_piece(b, p):
                dve.wait_ge(hi_done, b * 4 + (p + 1))
                tt(w_lo[:, p % 2], raw[:, p], f32(w_hi[:, p % 2]), ALU.subtract).then_inc(lo_done, 1)

            def evac(b):
                dve.wait_ge(piece_used, 4 * (b + 1))
                bank = psum[:, bank_of(b) + 1, :]
                two = bank.rearrange("p (c t) -> p c t", t=SEQ)
                if b < 2:
                    dst = qn[:, 1, 4 * b:4 * b + 4, :].rearrange("p h d -> p (h d)")
                elif b == 2:
                    dst, bank = kvcT[:, 1], two
                elif b < 5:
                    dst = kvsw[:, 1, b - 3].rearrange("p h d -> p (h d)")
                elif b < 9:
                    dst, bank = qkfT[:, 4 * (b - 5) + 2:4 * (b - 5) + 4, :], two
                elif b < 11:
                    dst = vf[:, 1, 512 * (b - 9):512 * (b - 9) + 512]
                elif b < QRY0:
                    c = b - OUT0
                    if c == 0:
                        dve.wait_ge(xres_loaded, 16)
                    for half in range(HALVES):
                        o = xres[:, half, 512 * c:512 * c + 512]
                        ins = tt(o, psum[:, bank_of(b) + half, :], o, ALU.add)
                    ins.then_inc(dveA, 1)
                    return
                else:
                    c = b - QRY0
                    dst, bank = qT[:, 4 * c + 2:4 * c + 4, :], two
                V.tensor_copy(dst, bank).then_inc(dveA, 1)

            def hook(b):
                if b == 2:
                    dve.wait_ge(gf_ps, 1)
                    tt(gz[:], psum[:, 7, 0:64].rearrange("p (h c) -> p h c", c=32),
                       bias32.unsqueeze(1).to_broadcast([P, HALVES, 32]), ALU.add).then_inc(gz_done, 1)
                    dve.wait_ge(gz_done, 1)
                    f = gz[:, :, NGATE:32]
                    seq(ts(nz[:], f, -1.0, None, ALU.mult))
                    settle()
                    tt(az[:], f, nz[:], ALU.max).then_inc(fx_done, 1)
                if b == 3:
                    dve.wait_ge(gt_done, 1)
                    stt(lf[:], gz[:, :, NGATE:32], 0.0, lz[:], ALU.min, ALU.subtract).then_inc(lf_done, 1)
                    seq(ts(gate[:], tg[:], 0.5, 0.5, ALU.mult, ALU.add))
                    dve.wait_ge(actA, 3)
                    dve.wait_ge(dveA, 3)
                    for kv, pc0 in ((0, KPOS), (1, VPOS)):
                        tok = kvcT[:, kv].rearrange("p g (n r) -> p r g n", r=CMP_STRIDE)
                        for m in range(2):
                            rs = slice(CMP_STRIDE * m, CMP_STRIDE * (m + 1))
                            pe_ = cols[:, pc0 + CMP_STRIDE * m:pc0 + CMP_STRIDE * (m + 1)]
                            for g in range(GROUPS):
                                ins = tt(flat[:, kv, rs, g, :], tok[:, :, g, m:m + NCMP],
                                         pe_.unsqueeze(2).to_broadcast([P, CMP_STRIDE, NCMP]), ALU.add)
                    ins.then_inc(flat_done, 1)
                if b == 4:
                    dve.wait_ge(cum_ps, 1)
                    c_ = psum[:, 5, 0:16].rearrange("p (h c) -> p h c", c=FOX_H)
                    ts(ab[:, 0, :, 0:FOX_H], c_, 1.0 / SCALE, None, ALU.mult)
                    ts(ab[:, 1, :, FOX_H:], c_, -1.0 / SCALE, None, ALU.mult).then_inc(ab_done, 1)
                if b == 6:
                    dve.wait_ge(ga_done, 2)
                    a = cg[:, 0]
                    seq(tt(cg[:, 1], a, a, ALU.mult))
                    settle()
                    seq(ts(cg[:, 2], cg[:, 1], GELU_C1, 1.0, ALU.mult, ALU.add))
                    settle()
                    tt(cg[:, 3], cg[:, 2], a, ALU.mult).then_inc(gelu_in, 1)
                    dve.wait_ge(gelu_tanh, 1)
                    seq(stt(cg[:, 1], cg[:, 4], 1.0, a, ALU.add, ALU.mult))
                    settle()
                    ts(cg[:, 5], cg[:, 1], 0.5, None, ALU.mult).then_inc(gy_done, 1)
                if b == 7:
                    dve.wait_ge(kc_done, 1)
                    V.tensor_copy(vc.rearrange("p g d -> p (g d)"), psum[0:NCMP, 6, 256:512]).then_inc(vc_done, 1)
                if b == 9:
                    for f in (2, 3):
                        dve.wait_ge(fill_ps, f + 1)
                        V.tensor_copy(qnT[:, 2 * f:2 * f + 2, :].rearrange("p h t -> p (h t)"), psum[:, 4 + f, :]).then_inc(fillD, 1)
                if b == 10:
                    dve.wait_ge(fill_ps, 6)
                    V.tensor_copy(kswT[:, 1].rearrange("p g t -> p (g t)"), psum[:, 5, :]).then_inc(fillD, 1)

            for b in range(GATES0):
                lo_piece(b, 0)
                lo_piece(b, 1)
                if b >= 1:
                    evac(b - 1)
                hook(b)
                lo_piece(b, 2)
                lo_piece(b, 3)
            evac(GATES0 - 1)

            mask = const("mask")

            def mask_unit(u):
                dve.wait_ge(score_ps, u + 1)
                if u >= P_RING:
                    dve.wait_ge(pT_ps, u - P_RING + 1)
                for half in range(HALVES):
                    cs = slice(0, P) if half == 0 else slice(P, 384)
                    ins = V.tensor_tensor_reduce(out=prob[:, u % P_RING, cs], in0=psum[:, u % 2, cs],
                                                 in1=mask[:, 0:P] if half == 0 else mask[:, P:384],
                                                 scale=-SCALE, scalar=-LOWEST, op0=ALU.add, op1=ALU.min,
                                                 accum_out=negmax[:, u, half:half + 1])
                ins.then_inc(masked, 1)

            def scale_unit(u):
                kind, h = UNITS[u]
                dve.wait_ge(exped, u + 1)
                if kind == "fox":
                    V.reciprocal(pscale[:, u, :], psums[:, u, :]).then_inc(scl_ready, 1)
                else:
                    seq(V.reciprocal(prec[:, u, :], psums[:, u, :]))
                    settle()
                    col = 3 * h + 1 + ("sel", "win").index(kind)
                    tt(pscale[:, u, :], prec[:, u, :], gate[:, :, col], ALU.mult).then_inc(scl_ready, 1)

            def pT_out(u):
                dve.wait_ge(pT_ps, u + 1)
                if u >= 2:
                    dve.wait_ge(pv_done, u - 1)
                V.tensor_copy(pT[:, u % 2, :], psum[:, 2 + u % 2, 0:384]).then_inc(pT_done, 1)

            def head_lo(hs):
                dve.wait_ge(o_hi_done, hs + 1)
                o = o_place(hs)
                tt(o_lo[:, o, :], psum[:, 4 + hs % 2, 0:SEQ], f32(o_hi[:, o, :]), ALU.subtract).then_inc(o_lo_done, 1)

            hn = [P, HALVES, NSA_H, NCMP]

            def over_heads(name):
                return const(name).rearrange("p (h n) -> p h n", n=NCMP).unsqueeze(2).to_broadcast(hn)

            def over_blocks(a):
                return a.rearrange("p (h c) -> p h c", c=NSA_H).unsqueeze(3).to_broadcast(hn)

            def cmp_before_exp():
                dve.wait_ge(cs_ps, 1)
                s_ = psum[:, 7, 0:256].rearrange("p (h c n) -> p h c n", h=HALVES, n=16)[:, :, :, 0:NCMP]
                for half in range(HALVES):
                    cn = over_heads("cneg")[:, half]
                    ins = stt(cp[:, 1, half], s_[:, half], SCALE, cn, ALU.mult, ALU.add)
                seq(ins)
                settle()
                seq(V.tensor_reduce(cmx, cp[:, 1], AX_X, ALU.max))
                settle()
                tt(cp[:, 0], cp[:, 1], over_blocks(cmx), ALU.subtract).then_inc(c2_done, 1)

            def cmp_after_exp():
                dve.wait_ge(ce_done, 1)
                seq(tt(cp[:, 2], cp[:, 1], over_heads("c01"), ALU.mult))
                settle()
                seq(V.tensor_reduce(csum, cp[:, 2], AX_X, ALU.add))
                settle()
                seq(ts(cmx, csum, TINY, None, ALU.max))
                settle()
                seq(V.reciprocal(csum, cmx))
                settle()
                seq(tt(crec.rearrange("p (h c) -> p h c", c=NSA_H), csum.rearrange("p (h c) -> p h c", c=NSA_H),
                       gate[:].rearrange("p h (c b) -> p h c b", b=3)[:, :, :, 0], ALU.mult))
                settle()
                tt(cp[:, 3], cp[:, 2], over_blocks(crec), ALU.mult).then_inc(pc_done, 1)

            done_at = {last_unit(hs) + 4: hs for hs in range(16)}
            for t in range(NU + 4):
                if t < NU:
                    mask_unit(t)
                if 1 <= t <= NU:
                    scale_unit(t - 1)
                if t == 1:
                    cmp_before_exp()
                if t == 5:
                    cmp_after_exp()
                if 2 <= t < NU + 2:
                    pT_out(t - 2)
                if t in done_at:
                    head_lo(done_at[t])

            with dve.Fori(0, UPS0 - GATES0) as i:
                for p in range(PIECES):
                    lo_piece(i + GATES0, p)

            def up_out(c):
                b = UPS0 + c
                dve.wait_ge(piece_used, 4 * (b + 1))
                dve.wait_ge(actA, UPS0)
                bank = bank_of(b)
                for x_, o in ((0, up_a), (1, up_b)):
                    ps = psum[:, bank + 2 * x_:bank + 2 * x_ + 2, :].rearrange("p k t -> p (k t)")
                    g = gateT[:, 16 * x_ + 4 * c:16 * x_ + 4 * c + 4, :].rearrange("p k t -> p (k t)")
                    last = stt(o[:].rearrange("p k t -> p (k t)"), g, 1.0, ps, ALU.add, ALU.mult)
                last.then_inc(dveA, 1)
                dve.wait_ge(dveA, b - 7)
                tt(up_a[:], up_a[:], up_b[:], ALU.add).then_inc(up_sum, 1)

            def merged_lo(c):
                dve.wait_ge(mer_hi, c + 1)
                stt(act_lo[:, 4 * c:4 * c + 4, :], up_a[:], 0.5, f32(act_hi[:, 4 * c:4 * c + 4, :]),
                    ALU.mult, ALU.subtract).then_inc(mer_lo, 1)
                dve.wait_ge(mer_lo, c + 1)

            def lo4(b, middle=None):
                lo_piece(b, 0)
                lo_piece(b, 1)
                if middle:
                    middle()
                lo_piece(b, 2)
                lo_piece(b, 3)

            def up_all(c):
                up_out(c)
                merged_lo(c)

            for c in range(4):
                lo4(UPS0 + c, (lambda: up_all(c - 1)) if c > 0 else None)
            for c in range(4):
                lo4(OUT0 + c, (lambda: up_all(3)) if c == 0 else (lambda: evac(OUT0 + c - 1)))
            evac(QRY0 - 1)

            scale_rows(xn, xres, HALVES, 2)
            lo_piece(QRY0, 0)
            lo_x(KC, 6, FFN_G)
            for c in range(4):
                b = QRY0 + c
                if c > 0:
                    lo_piece(b, 0)
                lo_piece(b, 1)
                if c > 0:
                    evac(b - 1)
                if c == 1:
                    dve.wait_ge(fin_loaded, 32)
                    dve.wait_ge(xT_ps, 2 * KC)
                    for half in range(HALVES):
                        seq(tt(xn[:, half, :], xn[:, half, :], ffn_row[:], ALU.mult))
                lo_piece(b, 2)
                lo_piece(b, 3)
            evac(NBLK - 1)

            def top16(lists):
                for src, scratch, v, ix in lists:
                    seq(V.max(v[:, 0:8], src))
                settle()
                for src, scratch, v, ix in lists:
                    seq(V.max_index(ix[:, 0:8], v[:, 0:8], src))
                    seq(V.match_replace(scratch, v[:, 0:8], src, LOWEST))
                settle()
                for src, scratch, v, ix in lists:
                    seq(V.max(v[:, 8:16], scratch))
                settle()
                for src, scratch, v, ix in lists:
                    seq(V.max_index(ix[:, 8:16], v[:, 8:16], scratch))

            def topk_head(half, h):
                def scores(j):
                    return psum[:, 4 * half + j // 4, (j % 4) * NKEYS:(j % 4 + 1) * NKEYS]
                top16([(scores(2 * h + l), list2[:, 2 * (h % 2) + l, :], val[:, half, h, l, :], ind[:, half, h, l, :])
                       for l in range(2)])
                cd = cand[:, h % 2]
                seq(tt(cd, val[:, half, h, 0, :].unsqueeze(2).to_broadcast([P, TOPK, TOPK]),
                       val[:, half, h, 1, :].unsqueeze(1).to_broadcast([P, TOPK, TOPK]), ALU.add))
                settle()
                top16([(cd.rearrange("p a b -> p (a b)"), cand2[:, h % 2, :], top[:, half, h, :], pos[:, half, h, :])])

            def topk_end(half):
                settle()
                V.sem_inc(topk_read, 1)
                seq(ts(pab[:, 0], pos[:, half], 4, None, ALU.logical_shift_right))
                seq(ts(pab[:, 1], pos[:, half], 15, None, ALU.bitwise_and))
                seq(V.tensor_copy(indf[:], ind[:, half]))
                tt(soft[:, 0], top[:, half], top[:, half, :, 0:1].to_broadcast([P, PEER_H, TOPK]),
                   ALU.subtract).then_inc(soft_in, 1)
                settle()
                seq(V.tensor_copy(pabf[:], pab[:]))
                settle()
                full = [P, PEER_H, TOPK, TOPK]
                iota = const("iota").unsqueeze(1).to_broadcast([P, PEER_H * TOPK, TOPK])
                for l in range(2):
                    oh = onehot[:].rearrange("p h s c -> p (h s) c")
                    seq(tt(oh, pabf[:, l].rearrange("p h s -> p (h s)").unsqueeze(2).to_broadcast([P, SLOTS, TOPK]),
                           iota, ALU.is_equal))
                    settle()
                    seq(tt(onehot[:], onehot[:], indf[:, :, l, :].unsqueeze(2).to_broadcast(full), ALU.mult))
                    settle()
                    seq(V.tensor_reduce(key12[:, l, :], oh, AX_X, ALU.add))
                    settle()
                seq(stt(eidf[:], key12[:, 0, :], float(NKEYS), key12[:, 1, :], ALU.mult, ALU.add))
                settle()
                V.tensor_copy(eidx[:, half, :], eidf[:]).then_inc(eidx_done, 1)
                dve.wait_ge(soft_exp, half + 1)
                seq(V.tensor_reduce(soft[:, 2, :, 0:1], soft[:, 1], AX_X, ALU.add))
                settle()
                seq(V.reciprocal(soft[:, 3, :, 0:1], soft[:, 2, :, 0:1]))
                settle()
                seq(tt(gw[:, half], soft[:, 1], soft[:, 3, :, 0:1].to_broadcast([P, PEER_H, TOPK]), ALU.mult))
                settle()

            dve.wait_ge(ks_ps, 2)
            for h in range(PEER_H):
                topk_head(0, h)
            topk_end(0)

            def step(G, half, j, loop=False):
                for s in range(GS):
                    dve.wait_ge(down_in[s % RING], G * 32 + (s // RING + 1) * 16)
                    V.tensor_tensor_reduce(out=down_rows[:, s % RING, :], in0=down_rows[:, s % RING, :],
                                           in1=xn[:, half, :], scale=1.0, scalar=0.0, op0=ALU.mult, op1=ALU.add,
                                           accum_out=dots[:, 0, s:s + 1]).then_inc(down_used, 1)
                a = dots[:, 0, :]
                dve.wait_ge(down_used, G * GS + GS)
                tt(dots[:, 1, :], a, a, ALU.mult).then_inc(ge_sq, 1)
                dve.wait_ge(ge_sq, G + 1)
                ts(dots[:, 2, :], dots[:, 1, :], GELU_C1, 1.0, ALU.mult, ALU.add).then_inc(ge_poly, 1)
                dve.wait_ge(ge_poly, G + 1)
                tt(dots[:, 3, :], dots[:, 2, :], a, ALU.mult).then_inc(ge_in, 1)
                if loop or G > 0:
                    dve.wait_ge(w_ready, G)
                dve.wait_ge(ge_tanh, G + 1)
                stt(dots[:, 5, :], dots[:, 4, :], 1.0, a, ALU.add, ALU.mult).then_inc(ge_y, 1)
                if loop or G > 0:
                    dve.wait_ge(diag_ready, G * GS)
                dve.wait_ge(ge_y, G + 1)
                g = gw[:, half].rearrange("p h s -> p (h s)")
                g = g[:, bass.ds(j * GS, GS)] if loop else g[:, j * GS:j * GS + GS]
                stt(dots[:, 6, :], dots[:, 5, :], 0.5, g, ALU.mult, ALU.mult).then_inc(w_ready, 1)

            def residual(half):
                dve.wait_ge(up_used, SLOTS * (half + 1))
                tt(xres[:, half, :], psum[:, 4 * half:4 * half + 4, :].rearrange("p k n -> p (k n)"),
                   xres[:, half, :], ALU.add).then_inc(x2_done, 1)

            def final(half):
                dve.wait_ge(squares, 3 + half)
                i = 2 * HALVES + half
                seq(V.reciprocal(rstd[:, i:i + 1], rms[:, i:i + 1]))
                settle()
                stt(xn[:, half, :], xres[:, half, :], rstd[:, i:i + 1], final_row[:], ALU.mult, ALU.mult).then_inc(y_done, 1)

            for G in range(GPH // 2):
                step(G, 0, G)
                topk_head(1, G)
            topk_end(1)
            with dve.Fori(GPH // 2, GPH) as i:
                step(i, 0, i, True)
            step(GPH, 1, 0)
            step(GPH + 1, 1, 1)
            residual(0)
            final(0)
            with dve.Fori(GPH + 2, NG) as i:
                step(i, 1, i - GPH, True)
            residual(1)
            final(1)


_INS = ['x', 'norm_mix_gain', 'w_in', 'nsa_gate_bias', 'fox_forget_bias', 'merge_gate_bias', 'k_cmp_pos', 'k_cmp_w1',
        'k_cmp_w2', 'v_cmp_pos', 'v_cmp_w1', 'v_cmp_w2', 'w_up_nsa', 'w_up_fox', 'w_out', 'norm_ffn_gain',
        'peer_w_query', 'peer_sub_keys_1', 'peer_sub_keys_2', 'peer_expert_down', 'peer_expert_up',
        'norm_final_gain']


def kernel(**inputs):
    import concourse.bacc as _bacc
    from concourse.bass_utils import run_bass_kernel_spmd as _run

    nc = _bacc.Bacc("TRN2", target_bir_lowering=False, num_devices=1)
    arrays, args = {}, []
    for name in _INS:
        a = np.ascontiguousarray(inputs[name])
        arrays[f"in_{name}_dram"] = a
        args.append(nc.dram_tensor(f"in_{name}_dram", a.shape, mybir.dt.from_np(a.dtype), kind="ExternalInput").ap())
    table = const_table()
    arrays["in_consts_dram"] = table
    args.append(nc.dram_tensor("in_consts_dram", table.shape, F32, kind="ExternalInput").ap())
    args.append(nc.dram_tensor("out_0_dram", (1, SEQ, D), F32, kind="ExternalOutput").ap())
    build(nc, *args)
    r = _run(nc, [arrays], core_ids=[0])
    return r.results[0]["out_0_dram"]
```

```python
from contextlib import ExitStack

import numpy as np

import concourse.bass as bass
from concourse import mybir

F32 = mybir.dt.float32
F32R = mybir.dt.float32r
U32 = mybir.dt.uint32
ALU = mybir.AluOpType
ACT = mybir.ActivationFunctionType
AX_X = mybir.AxisListType.X

P = 128
SEQ = 256
D = 2048
HALVES = SEQ // P
HD = 128
ROT = HD // 2
KC = D // P
NSA_H, GROUPS, HPG = 8, 2, 4
FOX_H = 8
CMP_STRIDE, CMP_BLOCK, CMP_HID = 16, 32, 256
NCMP = SEQ // CMP_STRIDE - CMP_BLOCK // CMP_STRIDE + 1
SCALE = float(HD) ** -0.5
EPS = 1e-6
NEG = -1e30
TINY = 1e-30
GELU_C0, GELU_C1 = 0.7978845608028654, 0.044715
PEER_H, NKEYS, TOPK = 8, 128, 16
SLOTS = PEER_H * TOPK
LOWEST = -3.0e38

Q_N, KV_C, KV_S, KV_W, G_N = 0, 1024, 1536, 2048, 2560
Q_F, V_F, F_F, G_A = 2584, 4632, 5656, 5664
NGATE = 3 * NSA_H

CT = {}


def _columns():
    at = 0
    for name, n in (("ident", P), ("tri", P), ("mask", 384), ("cos", HALVES * ROT), ("sin", HALVES * ROT),
                    ("cosc", ROT), ("sinc", ROT), ("c01", HALVES * NCMP), ("cneg", HALVES * NCMP),
                    ("iota", TOPK), ("augsel", FOX_H)):
        CT[name] = (at, at + n)
        at += n
    return at


NCONST = _columns()


def const_table():
    t = np.zeros((P, NCONST), np.float32)

    def put(name, a):
        lo, hi = CT[name]
        t[:a.shape[0], lo:hi] = a.reshape(a.shape[0], -1)

    i = np.arange(P)
    put("ident", np.eye(P, dtype=np.float32))
    put("tri", (i[:, None] <= i[None, :]).astype(np.float32))
    causal = np.where(i[None, :] <= i[:, None], 0.0, NEG)
    put("mask", np.concatenate([causal, np.zeros((P, P)), causal], axis=1))
    freq = np.float32(10000.0) ** (-np.arange(0, HD, 2, dtype=np.float32) / np.float32(HD))
    ang = np.arange(SEQ, dtype=np.float32)[:, None] * freq[None, :]
    put("cos", np.cos(ang).reshape(HALVES, P, ROT).transpose(1, 0, 2))
    put("sin", np.sin(ang).reshape(HALVES, P, ROT).transpose(1, 0, 2))
    end = np.arange(NCMP) * CMP_STRIDE + CMP_BLOCK - 1
    angc = end.astype(np.float32)[:, None] * freq[None, :]
    put("cosc", np.cos(angc))
    put("sinc", np.sin(angc))
    seen = (end[None, None, :] <= (i[:, None, None] + P * np.arange(HALVES)[None, :, None]))
    put("c01", seen.astype(np.float32))
    put("cneg", np.where(seen, 0.0, NEG))
    put("iota", np.tile(np.arange(TOPK), (P, 1)))
    sel = np.zeros((2 * FOX_H, FOX_H))
    for h in range(FOX_H):
        sel[h, h] = sel[FOX_H + h, h] = 1.0
    put("augsel", sel)
    return t


PIECES = 4
KPP = 4
GATES0, UPS0, OUT0, QRY0, NBLK = 11, 19, 23, 27, 31
CMP_AFTER = 4
W_IN_COL = [Q_N, Q_N + 512, KV_C, KV_S, KV_W, Q_F, Q_F + 512, Q_F + 1024, Q_F + 1536, V_F, V_F + 512]
TRANSPOSED = {2, 5, 6, 7, 8}

UNITS = [("fox", h) for h in range(FOX_H)] + [(b, h) for h in range(NSA_H) for b in ("sel", "win")]
NU = len(UNITS)
NSETUP, NLATE = 6, 6
P_RING = 4

GS = 8
GPH = SLOTS // GS
NG = HALVES * GPH
RING = 4


def build(nc, x, norm_mix_gain, w_in, nsa_gate_bias, fox_forget_bias, merge_gate_bias, k_cmp_pos, k_cmp_w1,
          k_cmp_w2, v_cmp_pos, v_cmp_w1, v_cmp_w2, w_up_nsa, w_up_fox, w_out, norm_ffn_gain, peer_w_query,
          peer_sub_keys_1, peer_sub_keys_2, peer_expert_down, peer_expert_up, norm_final_gain, consts, out):
    with ExitStack() as ctx:
        def sem(name):
            return ctx.enter_context(nc.semaphore(name))

        base = -(-nc.sbuf_base // 512) * 512

        def at(name, shape, kb, dt=F32):
            n = int(np.prod(shape[1:])) * 4
            assert base + kb * 1024 + n <= nc.sbuf_usable_end, name
            return nc.alloc_sbuf_tensor_at(name, shape, dt, offset=int(base + kb * 1024))

        ct = at("ct", [P, NCONST], 0)
        cols = at("cols", [P, P], 4.5)
        rows = at("rows", [64, 2, P], 5)
        ones = at("ones", [P, P], 6)
        small = at("small", [P, 896], 6.5)
        MERGE_B, MIX_G, FFN_G, KPOS, VPOS = 0, 32, 48, 64, 96
        cut = [0]

        def tile(*dims, dt=F32, parts=P):
            n = int(np.prod(dims))
            a = small[0:parts, cut[0]:cut[0] + n]
            cut[0] += n
            assert cut[0] <= 896
            if len(dims) > 1:
                names = "abcd"[:len(dims)]
                a = a.rearrange(f"p ({' '.join(names)}) -> p {' '.join(names)}", **dict(zip(names, dims)))
            return a if dt == F32 else a.bitcast(dt)

        def const(name, parts=P):
            lo, hi = CT[name]
            return ct[0:parts, lo:hi]

        ident = const("ident")
        act_hi = at("act_hi", [P, KC, SEQ], 10, F32R)
        act_lo = at("act_lo", [P, KC, SEQ], 26, F32R)
        raw = at("raw", [P, PIECES, KPP, 512], 42)
        w_hi = at("w_hi", [P, 2, KPP, 512], 74, F32R)
        w_lo = at("w_lo", [P, 2, KPP, 512], 90, F32R)
        qkfT = at("qkfT", [P, 2 * FOX_H, SEQ], 106)
        vf = at("vf", [P, HALVES, 1024], 122)
        kvsw = at("kvsw", [P, HALVES, 2, 4, HD], 130)
        gateT = at("gateT", [P, 32, SEQ], 106)
        keysT = at("keysT", [P, 2 * PEER_H, NKEYS], 106)
        keys = at("keys", [P, 2, PEER_H, HD], 114)
        ffn_row = at("ffn_row", [P, D], 122)
        final_row = at("final_row", [P, D], 130)
        qn = at("qn", [P, HALVES, NSA_H, HD], 138)
        qnT = at("qnT", [P, NSA_H, SEQ], 146)
        kswT = at("kswT", [P, 2, GROUPS, SEQ], 154)
        kvcT = at("kvcT", [P, 2, GROUPS, SEQ], 158)
        pcT = at("pcT", [NCMP, 2, SEQ], 158)
        xres = at("xres", [P, HALVES, D], 138)
        o_hi = at("o_hi", [P, 16, SEQ], 162, F32R)
        o_lo = at("o_lo", [P, 16, SEQ], 178, F32R)
        x_in = at("x_in", [P, HALVES, D], 162)
        rt = at("rt", [P, 2, HALVES, NSA_H, ROT], 178)
        flat = at("flat", [P, 2, CMP_BLOCK, GROUPS, NCMP], 186)
        aug = at("aug", [2 * FOX_H, FOX_H, SEQ], 186)
        xn = at("xn", [P, HALVES, D], 162)
        qT = at("qT", [P, 2 * PEER_H, SEQ], 178)
        prob = at("prob", [P, P_RING, 384], 194)
        pT = at("pT", [P, 2, 384], 200)
        gf_raw = at("gf_raw", [P, KC, 32], 194)
        gf_hi = at("gf_hi", [P, KC, 32], 196, F32R)
        gf_lo = at("gf_lo", [P, KC, 32], 198, F32R)
        gfT = at("gfT", [32, SEQ], 200)
        abT = at("abT", [2 * FOX_H, 2, SEQ], 203)
        w2 = at("w2", [P, 2, 2, HD], 205)
        up_a = at("up_a", [P, 4, SEQ], 194)
        up_b = at("up_b", [P, 4, SEQ], 198)
        diag = at("diag", [P, GS, P], 194)
        sq = at("sq", [P, HALVES, D], 106)
        down_rows = at("down_rows", [P, RING, D], 42)
        up_rows = at("up_rows", [P, RING, D], 74)
        onehot = at("onehot", [P, PEER_H, TOPK, TOPK], 114)
        cand = at("cand", [P, 2, TOPK, TOPK], 154)
        cand2 = at("cand2", [P, 2, TOPK * TOPK], 156)
        list2 = at("list2", [P, 4, NKEYS], 158)
        val = at("val", [P, HALVES, PEER_H, 2, TOPK], 160)
        ind = at("ind", [P, HALVES, PEER_H, 2, TOPK], 198, U32)
        top = at("top", [P, HALVES, PEER_H, TOPK], 200)
        pos = at("pos", [P, HALVES, PEER_H, TOPK], 201, U32)
        gw = at("gw", [P, HALVES, PEER_H, TOPK], 202)
        eidx = at("eidx", [P, HALVES, SLOTS], 203, U32)
        pab = at("pab", [P, 2, PEER_H, TOPK], 204, U32)
        pabf = at("pabf", [P, 2, PEER_H, TOPK], 205)
        indf = at("indf", [P, PEER_H, 2, TOPK], 206)
        dots = at("dots", [P, 7, GS], 207)
        idx_stage = at("idx_stage", [P, 2, GS], 207.25, U32)
        key12 = at("key12", [P, 2, SLOTS], 5)
        eidf = at("eidf", [P, SLOTS], 6)

        ss = tile(3 * HALVES)
        ss4 = tile(HALVES, 4)
        wsum = tile(2, PEER_H)
        rms = tile(3 * HALVES)
        rstd = tile(3 * HALVES)
        eps = tile(1)
        bias32 = tile(32)
        hbias = tile(32)
        gz = tile(HALVES, 32)
        nz = tile(HALVES, FOX_H)
        az = tile(HALVES, FOX_H)
        ez = tile(HALVES, FOX_H)
        lz = tile(HALVES, FOX_H)
        lf = tile(HALVES, FOX_H)
        tg = tile(HALVES, NGATE)
        gate = tile(HALVES, NGATE)
        ab = tile(2, HALVES, 2 * FOX_H)
        kcT = tile(GROUPS, NCMP)
        negmax = tile(NU, 2)
        psums = tile(NU, 2)
        prec = tile(NU, 2)
        pscale = tile(NU, 2)
        cmx, csum, crec = tile(16), tile(16), tile(16)
        kc = at("kc", [NCMP, GROUPS, HD], 196)
        crt = at("crt", [NCMP, 2, GROUPS, ROT], 197)
        vc = rows[0:NCMP, 0:2, :]
        hid = at("hid", [GROUPS * NCMP, 2, CMP_HID], 194)
        hid1 = at("hid1", [GROUPS * NCMP, 2, CMP_HID], 198)
        hid2 = at("hid2", [GROUPS * NCMP, 2, CMP_HID], 200)
        hidT = at("hidT", [P, 2, 2, GROUPS * NCMP], 202)
        cp = at("cp", [P, 4, HALVES, NSA_H, NCMP], 138)

        psum = ctx.enter_context(nc.psum_tensor("psum", [P, 8, 512], F32))

        x_loaded = [sem(f"x_loaded{half}") for half in range(HALVES)]
        setup_loaded = sem("setup_loaded")
        late_loaded = sem("late_loaded")
        raw_loaded = [sem(f"raw_loaded{p}") for p in range(PIECES)]
        xres_loaded = sem("xres_loaded")
        keys_loaded = sem("keys_loaded")
        fin_loaded = sem("fin_loaded")
        stored = sem("stored")
        dve_seq = sem("dve_seq")
        act_seq = sem("act_seq")
        pool_seq = sem("pool_seq")
        const_done = sem("const_done")
        cols_ps = sem("cols_ps")
        cols_done = sem("cols_done")
        hbias_done = sem("hbias_done")
        half_sum = sem("half_sum")
        part_sums = sem("part_sums")
        ms_done = sem("ms_done")
        squares = sem("squares")
        normed = sem("normed")
        xT_ps = sem("xT_ps")
        act_hi_done = sem("act_hi_done")
        act_lo_done = sem("act_lo_done")
        gf_hi_done = sem("gf_hi_done")
        gf_lo_done = sem("gf_lo_done")
        gf_ps = sem("gf_ps")
        gfT_done = sem("gfT_done")
        gfz_ps = sem("gfz_ps")
        gz_done = sem("gz_done")
        fx_done = sem("fx_done")
        lf_done = sem("lf_done")
        cum_ps = sem("cum_ps")
        ab_done = sem("ab_done")
        ab_ps = sem("ab_ps")
        abT_done = sem("abT_done")
        flat_done = sem("flat_done")
        cmp_used = sem("cmp_used")
        ga_done = sem("ga_done")
        gt_done = sem("gt_done")
        gy_done = sem("gy_done")
        hidT_ps = sem("hidT_ps")
        hidT_done = sem("hidT_done")
        kvc_ps = sem("kvc_ps")
        kc_done = sem("kc_done")
        vc_done = sem("vc_done")
        kcr_done = sem("kcr_done")
        kcT_ps = sem("kcT_ps")
        kcT_done = sem("kcT_done")
        roped = sem("roped")
        fill_ps = sem("fill_ps")
        fillA = sem("fillA")
        fillD = sem("fillD")
        cs_ps = sem("cs_ps")
        c2_done = sem("c2_done")
        ce_done = sem("ce_done")
        pc_done = sem("pc_done")
        hi_done = sem("hi_done")
        lo_done = sem("lo_done")
        piece_used = sem("piece_used")
        actA = sem("actA")
        dveA = sem("dveA")
        score_ps = sem("score_ps")
        masked = sem("masked")
        exped = sem("exped")
        p_ready = sem("p_ready")
        pT_ps = sem("pT_ps")
        pT_done = sem("pT_done")
        pv_done = sem("pv_done")
        o_hi_done = sem("o_hi_done")
        o_lo_done = sem("o_lo_done")
        pcT_ps = sem("pcT_ps")
        pcT_done = sem("pcT_done")
        aug_done = sem("aug_done")
        up_sum = sem("up_sum")
        mer_hi = sem("mer_hi")
        mer_lo = sem("mer_lo")
        keyT_ps = sem("keyT_ps")
        keyT_done = sem("keyT_done")
        xn_scaled = sem("xn_scaled")
        ks_ps = sem("ks_ps")
        topk_read = sem("topk_read")
        soft_in = sem("soft_in")
        soft_exp = sem("soft_exp")
        eidx_done = sem("eidx_done")
        idx_copied = sem("idx_copied")
        turn = sem("turn")
        down_in = [sem(f"down_in{r}") for r in range(RING)]
        up_in = [sem(f"up_in{r}") for r in range(RING)]
        down_used = sem("down_used")
        up_used = sem("up_used")
        gelu_in = sem("gelu_in")
        gelu_tanh = sem("gelu_tanh")
        ge_sq, ge_poly, ge_in = sem("ge_sq"), sem("ge_poly"), sem("ge_in")
        ge_tanh, ge_y = sem("ge_tanh"), sem("ge_y")
        w_ready = sem("w_ready")
        diag_ready = sem("diag_ready")
        x2_done = sem("x2_done")
        y_done = sem("y_done")

        w_in_v = w_in[0].rearrange("(k p) n -> p k n", p=P)
        w_un_v = w_up_nsa[0].rearrange("(k p) n -> p k n", p=P)
        w_uf_v = w_up_fox[0].rearrange("(k p) n -> p k n", p=P)
        w_out_v = w_out[0].rearrange("(k p) n -> p k n", p=P)
        w_q_v = peer_w_query[0].rearrange("(k p) n -> p k n", p=P)
        x_v = x[0].rearrange("(h p) d -> p h d", p=P)
        out_v = out[0].rearrange("(h p) d -> p h d", p=P)

        def f32(a):
            return a.bitcast(F32)

        def bank_of(b):
            if b < UPS0:
                return 2 * (b % 2)
            return 4 * (b % 2)

        X_BANKS = ((2, 3, 4, 5), (2, 3, 6, 7))
        SCORE_BANKS = ((2, 3, 6, 7), (4, 5, 6, 7))

        def uses(b):
            return b + 1 + 2 * (1 if not isinstance(b, int) or b > CMP_AFTER else 0)

        def kT_of(kind, h):
            return qkfT[:, FOX_H + h, :] if kind == "fox" else kswT[:, ("sel", "win").index(kind), h // HPG, :]

        def q_of(kind, h):
            return qkfT[:, h, :] if kind == "fox" else qnT[:, h, :]

        def v_of(kind, h, kb):
            if kind == "fox":
                return vf[:, kb, h * HD:(h + 1) * HD]
            return kvsw[:, kb, ("sel", "win").index(kind), GROUPS + h // HPG, :]

        def head_slot(kind, h):
            return h if kind == "fox" else FOX_H + h

        def o_place(hs):
            return NSA_H + hs if hs < FOX_H else hs - FOX_H

        def last_unit(hs):
            return hs if hs < FOX_H else FOX_H + 2 * (hs - FOX_H) + 1

        block = ctx.enter_context(nc.Block())

        @block.sync
        def _(sp):
            sp.dma_start(x_in[:, 0, :], x_v[:, 0, :]).then_inc(x_loaded[0], 16)
            for dst, src in ((rows[0:32, 0, :], merge_gate_bias[0].rearrange("(c p) -> c p", p=P)),
                             (rows[32:48, 0, :], norm_mix_gain[0].rearrange("(c p) -> c p", p=P)),
                             (rows[48:64, 0, :], norm_ffn_gain[0].rearrange("(c p) -> c p", p=P)),
                             (rows[0:32, 1, :], k_cmp_pos[0]), (rows[32:64, 1, :], v_cmp_pos[0])):
                sp.dma_start(dst, src).then_inc(setup_loaded, 16)
            sp.dma_start(x_in[:, 1, :], x_v[:, 1, :]).then_inc(x_loaded[1], 16)

            def load(b, src, first=False):
                for p in range(PIECES):
                    if not first:
                        sp.wait_ge(lo_done, 4 * (b - 1) + p + 1)
                    sp.dma_start(raw[:, p], src(p)).then_inc(raw_loaded[p], 16)

            def w_in_piece(col):
                return lambda p: w_in_v[:, KPP * p:KPP * p + KPP, col]

            for b in range(GATES0):
                col = W_IN_COL[b]
                if b == CMP_AFTER + 1:
                    for kv, w1 in enumerate((k_cmp_w1, v_cmp_w1)):
                        w1_v = w1[0].rearrange("(r d) h -> d r h", d=HD)
                        for p in range(PIECES):
                            if kv == 0:
                                sp.wait_ge(lo_done, 4 * (b - 1) + p + 1)
                            else:
                                sp.wait_ge(cmp_used, p + 1)
                            sp.dma_start(raw[:, p].rearrange("p k n -> p (k n)").rearrange("p (r h) -> p r h", h=CMP_HID),
                                         w1_v[:, 8 * p:8 * p + 8, :]).then_inc(raw_loaded[p], 16)
                    for p in range(PIECES):
                        sp.wait_ge(cmp_used, PIECES + p + 1)
                        sp.dma_start(raw[:, p], w_in_piece(slice(col, col + 512))(p)).then_inc(raw_loaded[p], 16)
                else:
                    load(b, w_in_piece(slice(col, col + 512)), first=b == 0)
            with sp.Fori(0, UPS0 - GATES0) as i:
                load(i + GATES0, w_in_piece(bass.ds(i * 512 + G_A, 512)))
            for c in range(4):
                cs = slice(512 * c, 512 * c + 512)
                load(UPS0 + c, lambda p: (w_un_v if p < 2 else w_uf_v)[:, KPP * (p % 2):KPP * (p % 2) + KPP, cs])
            sp.wait_ge(o_hi_done, 16)
            sp.dma_start(xres[:], x_v).then_inc(xres_loaded, 16)
            for c in range(4):
                cs = slice(512 * c, 512 * c + 512)
                load(OUT0 + c, lambda p: w_out_v[:, KPP * p:KPP * p + KPP, cs])
            for c in range(4):
                cs = slice(512 * c, 512 * c + 512)
                load(QRY0 + c, lambda p: w_q_v[:, KPP * p:KPP * p + KPP, cs])
            for half in range(HALVES):
                sp.wait_ge(y_done, half + 1)
                sp.dma_start(out_v[:, half, :], xn[:, half, :]).then_inc(stored, 16)
            sp.wait_ge(stored, 16 * HALVES)

        @block.tensor
        def _(pe):
            def mm(*a, **k):
                return nc.tensor.matmul(*a, skip_group_check=True, **k)

            pe.wait_ge(setup_loaded, 16 * NSETUP)
            nc.tensor.transpose(psum[:, 7, 0:64], rows[:, 0, :], ident[0:64, 0:64])
            nc.tensor.transpose(psum[:, 7, 64:128], rows[:, 1, :], ident[0:64, 0:64]).then_inc(cols_ps, 1)

            def transpose_x(src, n0, chunks):
                for k in chunks:
                    if k % 4 == 0:
                        pe.wait_ge(normed, (n0 + k) // 4 + 1)
                    if k >= 4:
                        pe.wait_ge(act_lo_done, n0 + k - 3)
                    for half in range(HALVES):
                        ins = nc.tensor.transpose(psum[:, X_BANKS[n0 > 0][k % 4], half * P:(half + 1) * P],
                                                  src[:, half, k * P:(k + 1) * P], ident)
                    ins.then_inc(xT_ps, 1)

            def nat_piece(hi, lo, p, banks, n=512, kpp=KPP, w0=0):
                for k in range(kpp):
                    kk = kpp * p + k
                    for half in range(HALVES):
                        t = slice(half * P, (half + 1) * P)
                        o = banks[half]
                        mm(o, act_hi[:, kk, t], hi[:, k, :], start=kk == 0, stop=False)
                        mm(o, act_hi[:, kk, t], lo[:, k, :], start=False, stop=False)
                        last = mm(o, act_lo[:, kk, t], hi[:, k, :], start=False, stop=kk == KC - 1)
                return last

            def tr_piece(hi, lo, ahi, alo, k0, bank, nk):
                for k in range(KPP):
                    kk = k0 + k
                    for c in range(4):
                        o = psum[:, bank + c // 2, (c % 2) * SEQ:(c % 2 + 1) * SEQ]
                        cs = slice(c * P, (c + 1) * P)
                        first = kk == 0 and c % 2 == 0
                        mm(o, hi[:, k, cs], ahi[:, kk, :], start=first, stop=False)
                        mm(o, hi[:, k, cs], alo[:, kk, :], start=False, stop=False)
                        last = mm(o, lo[:, k, cs], ahi[:, kk, :], start=False, stop=kk == nk - 1)
                return last

            def weight_block(b, par, kind, before=None, behind=None):
                bank = (2 if kind in ("nat", "tr") else 4) * par
                for p in range(PIECES):
                    if before:
                        before(p)
                    pe.wait_ge(lo_done, b * 4 + (p + 1))
                    if kind == "out" and p == PIECES - 1:
                        pe.wait_ge(mer_lo, 4)
                    hi, lo = w_hi[:, p % 2], w_lo[:, p % 2]
                    if kind in ("nat", "out"):
                        last = nat_piece(hi, lo, p, [psum[:, bank, :], psum[:, bank + 1, :]])
                    elif kind in ("tr", "qry"):
                        last = tr_piece(hi, lo, act_hi, act_lo, KPP * p, bank, KC)
                    else:
                        fox = p // 2
                        last = tr_piece(hi, lo, o_hi[:, 8 * fox:8 * fox + 8], o_lo[:, 8 * fox:8 * fox + 8],
                                        KPP * (p % 2), bank + 2 * fox, 2 * KPP)
                    last.then_inc(piece_used, 1)
                    if behind:
                        behind(p)

            def beside_norm(src, n0):
                def before(p):
                    transpose_x(src, n0, range(0, 8) if p == 0 else range(4 * p + 4, 4 * p + 8) if p < 3 else ())
                    pe.wait_ge(act_lo_done, n0 + KPP * (p + 1))
                return before

            def after(b):
                if b == 1:
                    pe.wait_ge(gf_lo_done, 1)
                    pe.wait_ge(cols_done, 1)
                    o = psum[0:32, 7, 0:SEQ]
                    for k in range(KC):
                        mm(o, gf_hi[:, k, :], act_hi[:, k, :], start=k == 0, stop=False)
                        mm(o, gf_hi[:, k, :], act_lo[:, k, :], start=False, stop=False)
                        last = mm(o, gf_lo[:, k, :], act_hi[:, k, :], start=False, stop=k == KC - 1)
                    last.then_inc(gf_ps, 1)
                if b == 2:
                    pe.wait_ge(gfT_done, 1)
                    for half in range(HALVES):
                        ins = nc.tensor.transpose(psum[:, 7, half * 32:half * 32 + 32], gfT[:, half * P:(half + 1) * P],
                                                  ident[0:32, 0:32])
                    ins.then_inc(gfz_ps, 1)
                if b == 4:
                    pe.wait_ge(lf_done, 1)
                    tri = const("tri")
                    mm(psum[:, 5, 0:8], tri, lf[:, 0, :], start=True, stop=True)
                    mm(psum[:, 5, 8:16], ones[:], lf[:, 0, :], start=True, stop=False)
                    mm(psum[:, 5, 8:16], tri, lf[:, 1, :], start=False, stop=True).then_inc(cum_ps, 1)
                    pe.wait_ge(flat_done, 1)
                    pe.wait_ge(gz_done, 1)
                    for kv in range(2):
                        for p in range(PIECES):
                            pe.wait_ge(raw_loaded[p], 16 * (CMP_AFTER + 2 + kv))
                            w1 = raw[:, p].rearrange("p k n -> p (k n)").rearrange("p (r h) -> p r h", h=CMP_HID)
                            for r in range(8):
                                last = mm(psum[0:GROUPS * NCMP, 6 + kv, 0:CMP_HID],
                                          flat[:, kv, 8 * p + r, :, :].rearrange("p g n -> p (g n)"), w1[:, r, :],
                                          start=p == 0 and r == 0, stop=p == PIECES - 1 and r == 7)
                            last.then_inc(cmp_used, 1)
                if b == 5:
                    pe.wait_ge(ab_done, 1)
                    for x_ in range(2):
                        for half in range(HALVES):
                            ins = nc.tensor.transpose(psum[0:16, 4, x_ * SEQ + half * P:x_ * SEQ + (half + 1) * P],
                                                      ab[:, x_, half, :], ident)
                    ins.then_inc(ab_ps, 1)
                if b == 6:
                    pe.wait_ge(gy_done, 1)
                    for kv in range(2):
                        for hc in range(2):
                            c = (2 * kv + hc) * GROUPS * NCMP
                            ins = nc.tensor.transpose(psum[:, 7, c:c + GROUPS * NCMP], hid2[:, kv, hc * P:(hc + 1) * P],
                                                      ident[0:GROUPS * NCMP, 0:GROUPS * NCMP])
                    ins.then_inc(hidT_ps, 1)
                if b == 7:
                    pe.wait_ge(hidT_done, 1)
                    pe.wait_ge(late_loaded, 16 * NLATE)
                    for kv in range(2):
                        for g in range(GROUPS):
                            for hc in range(2):
                                last = mm(psum[0:NCMP, 6, kv * 256 + g * HD:kv * 256 + (g + 1) * HD],
                                          hidT[:, kv, hc, g * NCMP:(g + 1) * NCMP], w2[:, kv, hc, :],
                                          start=hc == 0, stop=hc == 1)
                    last.then_inc(kvc_ps, 1)
                if b == 8:
                    pe.wait_ge(roped, 1)
                    pe.wait_ge(ab_ps, 1)
                    pe.wait_ge(abT_done, 1)
                    pe.wait_ge(ab_done, 1)
                    pe.wait_ge(kc_done, 1)
                    pe.wait_ge(vc_done, 1)
                    pe.wait_ge(hidT_done, 1)
                    for f in range(4):
                        for hh in range(2):
                            for half in range(HALVES):
                                ins = nc.tensor.transpose(
                                    psum[:, 4 + f, hh * SEQ + half * P:hh * SEQ + (half + 1) * P],
                                    qn[:, half, 2 * f + hh, :], ident)
                        ins.then_inc(fill_ps, 1)
                if b == 9:
                    pe.wait_ge(roped, 3)
                    for f in range(2):
                        pe.wait_ge(fillA, 2)
                        for g in range(GROUPS):
                            for half in range(HALVES):
                                ins = nc.tensor.transpose(
                                    psum[:, 4 + f, g * SEQ + half * P:g * SEQ + (half + 1) * P],
                                    kvsw[:, half, f, g, :], ident)
                        ins.then_inc(fill_ps, 1)
                    pe.wait_ge(kcr_done, 1)
                    pe.wait_ge(fillD, 2)
                    for g in range(GROUPS):
                        ins = nc.tensor.transpose(psum[:, 6, g * NCMP:(g + 1) * NCMP], kc[:, g, :],
                                                  ident[0:NCMP, 0:NCMP])
                    ins.then_inc(kcT_ps, 1)
                if b == 10:
                    pe.wait_ge(kcT_done, 1)
                    pe.wait_ge(fillA, 3)
                    pe.wait_ge(fillD, 3)
                    for half in range(HALVES):
                        for h in range(NSA_H):
                            last = mm(psum[:, 7, (half * NSA_H + h) * 16:(half * NSA_H + h) * 16 + NCMP],
                                      qnT[:, h, half * P:(half + 1) * P], kcT[:, h // HPG, :],
                                      start=half == 0 and h == 0, stop=True)
                    last.then_inc(cs_ps, 1)

            for b in range(GATES0):
                if b >= 2:
                    pe.wait_ge(actA, b - 1)
                    pe.wait_ge(dveA, b - 1)
                weight_block(b, b % 2, "tr" if b in TRANSPOSED else "nat",
                             before=beside_norm(x_in, 0) if b == 0 else None)
                after(b)

            def score(u):
                kind, h = UNITS[u]
                if u >= 2:
                    pe.wait_ge(masked, u - 1)
                q, k = q_of(kind, h), kT_of(kind, h)
                if kind == "fox":
                    pe.wait_ge(aug_done, h + 1)
                S = psum[:, u % 2, :]
                for half in range(HALVES):
                    n = P * (half + 1)
                    o = S[:, P * half:P * half + n]
                    last = mm(o, q[:, half * P:(half + 1) * P], k[:, 0:n], start=True, stop=kind != "fox")
                    if kind == "fox":
                        last = mm(o, aug[:, h, half * P:(half + 1) * P], abT[:, 1, 0:n], start=False, stop=True)
                last.then_inc(score_ps, 1)

            def trans(u):
                pe.wait_ge(p_ready, u + 1)
                if u >= 2:
                    pe.wait_ge(pT_done, u - 1)
                for j in range(3):
                    ins = nc.tensor.transpose(psum[:, 2 + u % 2, j * P:(j + 1) * P],
                                              prob[:, u % P_RING, j * P:(j + 1) * P], ident)
                ins.then_inc(pT_ps, 1)

            def cmp_trans(h):
                if h == 0:
                    pe.wait_ge(pc_done, 1)
                if h >= 1:
                    pe.wait_ge(pcT_done, h)
                for half in range(HALVES):
                    ins = nc.tensor.transpose(psum[0:NCMP, 6, half * P:(half + 1) * P],
                                              cp[:, 3, half, h, :], ident)
                ins.then_inc(pcT_ps, 1)

            def pv(u):
                kind, h = UNITS[u]
                hs = head_slot(kind, h)
                o = psum[:, 4 + hs % 2, 0:SEQ]
                begins = kind != "win"
                if begins and hs >= 2:
                    pe.wait_ge(o_lo_done, hs - 1)
                if kind == "sel":
                    pe.wait_ge(pcT_done, h + 1)
                    mm(o, vc[:, h // HPG, :], pcT[:, h % 2, :], start=True, stop=False)
                pe.wait_ge(pT_done, u + 1)
                pt = pT[:, u % 2, :]
                mm(o, v_of(kind, h, 0), pt[:, 0:SEQ], start=kind == "fox", stop=False)
                mm(o[:, P:SEQ], v_of(kind, h, 1), pt[:, SEQ:SEQ + P], start=False,
                   stop=kind != "sel").then_inc(pv_done, 1)

            pe.wait_ge(actA, GATES0)
            pe.wait_ge(dveA, GATES0)
            pe.wait_ge(abT_done, 1)
            for t in range(NU + 3):
                if t < NU:
                    score(t)
                    kind, h = UNITS[t]
                    if kind == "sel":
                        cmp_trans(h)
                if 2 <= t < NU + 2:
                    trans(t - 2)
                if t >= 3:
                    pv(t - 3)

            pe.wait_ge(masked, NU)
            pe.wait_ge(pT_done, NU)
            with pe.Fori(0, (UPS0 - GATES0) // 2) as i:
                for q in range(2):
                    b = i * 2 + (GATES0 + q)
                    pe.wait_ge(actA, i * 2 + (GATES0 + q - 1))
                    weight_block(b, (GATES0 + q) % 2, "tr")
            pe.wait_ge(o_lo_done, 16)
            with pe.Fori(0, 2) as i:
                for q in range(2):
                    if q == 1:
                        pe.wait_ge(actA, UPS0)
                    pe.wait_ge(dveA, i * 2 + (UPS0 + q - 9))
                    weight_block(i * 2 + (UPS0 + q), (UPS0 + q) % 2, "ups")
            pe.wait_ge(mer_lo, 3)
            with pe.Fori(0, 2) as i:
                for q in range(2):
                    pe.wait_ge(dveA, i * 2 + (OUT0 + q - 9))
                    weight_block(i * 2 + (OUT0 + q), (OUT0 + q) % 2, "out")

            pe.wait_ge(keys_loaded, 32)
            pe.wait_ge(dveA, QRY0 - 12)
            for f in range(4):
                if f >= 2:
                    pe.wait_ge(keyT_done, f - 1)
                for c in range(4):
                    j = 4 * f + c
                    ins = nc.tensor.transpose(psum[:, 6 + f % 2, c * P:(c + 1) * P], keys[:, j % 2, j // 2, :], ident)
                ins.then_inc(keyT_ps, 1)

            pe.wait_ge(keyT_done, 4)

            def key_scores(half, pair):
                for j in range(4 * pair, 4 * pair + 4):
                    last = mm(psum[:, SCORE_BANKS[half][pair], (j % 4) * NKEYS:(j % 4 + 1) * NKEYS],
                              qT[:, j, half * P:(half + 1) * P], keysT[:, j, :], start=True, stop=True)
                return last

            def scores_behind(c):
                def behind(p):
                    if p == 0:
                        pe.wait_ge(actA, QRY0 + c - 8)
                        pe.wait_ge(dveA, QRY0 + c - 8)
                        key_scores(0, c - 1).then_inc(ks_ps, 1)
                return behind

            for c in range(4):
                pe.wait_ge(dveA, QRY0 + c - 9)
                if c >= 2:
                    pe.wait_ge(actA, QRY0 + c - 9)
                weight_block(QRY0 + c, (QRY0 + c) % 2, "qry", before=beside_norm(xn, KC) if c == 0 else None,
                             behind=scores_behind(c) if c > 0 else None)
            pe.wait_ge(actA, NBLK - 8)
            pe.wait_ge(dveA, NBLK - 8)
            key_scores(0, 3).then_inc(ks_ps, 1)

            def up_step(G, half, first=False, end=False):
                for s in range(GS):
                    pe.wait_ge(up_in[s % RING], G * 32 + (s // RING + 1) * 16)
                    pe.wait_ge(diag_ready, G * GS + (s + 1))
                    for c in range(4):
                        last = mm(psum[:, 4 * half + c, :], diag[:, s, :], up_rows[:, s % RING, 512 * c:512 * c + 512],
                                  start=first and s == 0, stop=end and s == GS - 1)
                    last.then_inc(up_used, 1)

            pe.wait_ge(topk_read, 2)
            up_step(0, 0, first=True)
            pe.wait_ge(topk_read, 4)
            for pair in range(4):
                last = key_scores(1, pair)
            last.then_inc(ks_ps, 1)
            for G in range(2, GPH // 2):
                up_step(G - 1, 0)
            with pe.Fori(GPH // 2, GPH) as i:
                up_step(i - 1, 0)
            up_step(GPH - 1, 0, end=True)
            pe.wait_ge(topk_read, 5)
            up_step(GPH, 1, first=True)
            with pe.Fori(GPH + 2, NG) as i:
                up_step(i - 1, 1)
            up_step(NG - 1, 1, end=True)

        @block.gpsimd
        def _(pool):
            n = [0]

            def seq(ins):
                ins.then_inc(pool_seq, 1)
                n[0] += 1

            def rope(x1, x2, cos, sin, t1, t2, done, count):
                tt = nc.gpsimd.tensor_tensor
                seq(tt(t1, x1, sin, ALU.mult))
                seq(tt(t2, x2, sin, ALU.mult))
                pool.wait_ge(pool_seq, n[0])
                seq(tt(x1, x1, cos, ALU.mult))
                seq(tt(x2, x2, cos, ALU.mult))
                pool.wait_ge(pool_seq, n[0])
                seq(tt(x1, x1, t2, ALU.subtract))
                pool.wait_ge(pool_seq, n[0])
                tt(x2, x2, t1, ALU.add).then_inc(done, 1)
                pool.wait_ge(done, count)

            def table(name, heads):
                t = const(name).rearrange("p (h r) -> p h r", h=HALVES)
                return t.unsqueeze(2).to_broadcast([P, HALVES, heads, ROT])

            pool.wait_ge(setup_loaded, 16 * NSETUP)
            pool.wait_ge(actA, 2)
            pool.wait_ge(dveA, 2)
            rope(qn[:, :, :, 0:ROT], qn[:, :, :, ROT:HD], table("cos", NSA_H), table("sin", NSA_H),
                 rt[:, 0], rt[:, 1], roped, 1)
            pool.wait_ge(actA, 5)
            pool.wait_ge(dveA, 5)
            for sw in range(2):
                rope(kvsw[:, :, sw, 0:GROUPS, 0:ROT], kvsw[:, :, sw, 0:GROUPS, ROT:HD], table("cos", GROUPS),
                     table("sin", GROUPS), rt[:, 0, :, 0:GROUPS], rt[:, 1, :, 0:GROUPS], roped, sw + 2)

            def ctable(name):
                return const(name, NCMP).unsqueeze(1).to_broadcast([NCMP, GROUPS, ROT])

            pool.wait_ge(kc_done, 1)
            rope(kc[:, :, 0:ROT], kc[:, :, ROT:HD], ctable("cosc"), ctable("sinc"), crt[:, 0], crt[:, 1], kcr_done, 1)

            pool.wait_ge(abT_done, 1)
            pool.wait_ge(cmp_used, 8)
            asel = const("augsel", 2 * FOX_H)
            for h in range(FOX_H):
                nc.gpsimd.tensor_scalar(aug[:, h, :], abT[:, 0, :], asel[:, h:h + 1], None, ALU.mult).then_inc(aug_done, 1)

            def fetch(kind, G, half, j, s, loop):
                used = down_used if kind == 0 else up_used
                if loop or G > 0 or s >= RING:
                    pool.wait_ge(used, G * GS + (s - RING + 1))
                    pool.sem_inc(turn, 1)
                elif kind == 0:
                    pool.wait_ge(lo_done, 4 * (NBLK - 1) + s + 1)
                elif s == 0:
                    pool.wait_ge(piece_used, 4 * NBLK)
                if s % RING == 0:
                    nc.gpsimd.tensor_copy(idx_stage[:, kind, s:s + RING],
                                          eidx[:, half, bass.ds(j * GS + s, RING)] if loop else
                                          eidx[:, half, j * GS + s:j * GS + s + RING]).then_inc(idx_copied, 1)

            def gather(kind, s):
                table_, rows_, landed = ((peer_expert_down[0], down_rows, down_in) if kind == 0 else
                                         (peer_expert_up[0], up_rows, up_in))
                nc.gpsimd.indirect_dma_start(
                    rows_[:, s % RING, :], None, table_,
                    bass.IndirectOffsetOnAxis(ap=idx_stage[:, kind, s:s + 1], axis=0)).then_inc(landed[s % RING], 16)

            def step(G, half, j, loop, down=True, up=True, up_half=None, up_j=None):
                for s in range(GS):
                    for kind in ((0,) if down else ()) + ((1,) if up else ()):
                        if kind == 0:
                            fetch(0, G, half, j, s, loop)
                        else:
                            fetch(1, G - 1, up_half, up_j, s, loop)
                        if s % RING == 0:
                            before = (0 if not up else (G * 4 - 2)) if not loop else G * 4 - 2
                            mine = 1 + (s // RING) * (int(down) + int(up)) + (kind if down else 0)
                            pool.wait_ge(idx_copied, before + mine)
                            if loop:
                                pool.sem_inc(turn, 1)
                        gather(kind, s)

            pool.wait_ge(eidx_done, 1)
            step(0, 0, 0, False, up=False)
            for G in range(1, GPH // 2):
                if G == 4:
                    pool.wait_ge(eidx_done, 2)
                step(G, 0, G, False, up_half=0, up_j=G - 1)
            with pool.Fori(GPH // 2, GPH) as i:
                step(i, 0, i, True, up_half=0, up_j=i - 1)
            pool.wait_ge(eidx_done, 3)
            step(GPH, 1, 0, False, up_half=0, up_j=GPH - 1)
            step(GPH + 1, 1, 1, False, up_half=1, up_j=0)
            with pool.Fori(GPH + 2, NG) as i:
                step(i, 1, i - GPH, True, up_half=1, up_j=i - (GPH + 1))
            step(NG, 1, GPH, False, down=False, up_half=1, up_j=GPH - 1)

        @block.scalar
        def _(act):
            A = nc.scalar.activation
            n = [0]

            def seq(ins):
                ins.then_inc(act_seq, 1)
                n[0] += 1

            act.dma_start(ct[:], consts).then_inc(setup_loaded, 16)

            def norm_stats(src, junk, i, half):
                seq(A(junk[:, half, :], src[:, half, :], ACT.Square, accum_out=ss[:, i:i + 1]))
                act.wait_ge(act_seq, n[0])
                A(rms[:, i:i + 1], ss[:, i:i + 1], ACT.Sqrt, bias=eps[:, 0:1], scale=1.0 / D).then_inc(squares, 1)

            def split_x(n0, gain, q):
                for k in range(4 * q, 4 * q + 4):
                    act.wait_ge(xT_ps, n0 + k + 1)
                    A(act_hi[:, k, :], psum[:, X_BANKS[n0 > 0][k % 4], 0:SEQ], ACT.Copy,
                      scale=cols[:, gain + k:gain + k + 1]).then_inc(act_hi_done, 1)

            act.wait_ge(x_loaded[0], 16)
            seq(A(sq[:, 0, :], x_in[:, 0, :], ACT.Square, accum_out=ss[:, 0:1]))
            def ld(dst, src):
                act.dma_start(dst, src).then_inc(late_loaded, 16)

            ld(bias32[:, 0:NGATE], nsa_gate_bias.partition_broadcast(P))
            ld(bias32[:, NGATE:32], fox_forget_bias.partition_broadcast(P))
            ld(gf_raw[:, :, 0:NGATE], w_in_v[:, :, G_N:G_N + NGATE])
            ld(gf_raw[:, :, NGATE:32], w_in_v[:, :, F_F:F_F + FOX_H])
            ld(w2[:, 0], k_cmp_w2[0].rearrange("(c p) d -> p c d", p=P))
            ld(w2[:, 1], v_cmp_w2[0].rearrange("(c p) d -> p c d", p=P))

            act.wait_ge(const_done, 1)
            act.wait_ge(half_sum, 1)
            act.wait_ge(act_seq, n[0])
            A(rms[:, 0:HALVES], ss[:, 0:HALVES], ACT.Sqrt, bias=eps[:, 0:1], scale=1.0 / D).then_inc(squares, 1)
            act.wait_ge(cols_ps, 1)
            nc.scalar.copy(cols[:], psum[:, 7, 0:P]).then_inc(cols_done, 1)
            act.wait_ge(cols_done, 1)

            def hi_piece(b, p):
                act.wait_ge(raw_loaded[p], uses(b) * 16)
                if not (isinstance(b, int) and b == 0 and p < 2):
                    act.wait_ge(piece_used, b * 4 + (p - 1))
                nc.scalar.copy(w_hi[:, p % 2], raw[:, p]).then_inc(hi_done, 1)

            def evac(b):
                act.wait_ge(piece_used, 4 * (b + 1))
                bank = psum[:, bank_of(b), :]
                two = bank.rearrange("p (c t) -> p c t", t=SEQ)
                if b < 2:
                    dst = qn[:, 0, 4 * b:4 * b + 4, :].rearrange("p h d -> p (h d)")
                elif b == 2:
                    dst, bank = kvcT[:, 0], two
                elif b < 5:
                    dst = kvsw[:, 0, b - 3].rearrange("p h d -> p (h d)")
                elif b < 9:
                    dst, bank = qkfT[:, 4 * (b - 5):4 * (b - 5) + 2, :], two
                elif b < 11:
                    dst = vf[:, 0, 512 * (b - 9):512 * (b - 9) + 512]
                else:
                    c = b - QRY0
                    dst, bank = qT[:, 4 * c:4 * c + 2, :], psum[:, 4 * (b % 2), :].rearrange("p (c t) -> p c t", t=SEQ)
                nc.scalar.copy(dst, bank).then_inc(actA, 1)

            def hook(b):
                if b == 2:
                    act.wait_ge(gf_ps, 1)
                    nc.scalar.copy(gfT[:], psum[0:32, 7, 0:SEQ]).then_inc(gfT_done, 1)
                if b == 3:
                    act.wait_ge(fx_done, 1)
                    seq(A(ez[:], az[:], ACT.Exp, scale=-1.0))
                    seq(A(tg[:], gz[:, :, 0:NGATE], ACT.Tanh, scale=0.5))
                    act.wait_ge(act_seq, n[0])
                    A(lz[:], ez[:], ACT.Ln, bias=1.0).then_inc(gt_done, 1)
                if b == 5:
                    act.wait_ge(cmp_used, 8)
                    for kv in range(2):
                        nc.scalar.copy(hid[:, kv, :], psum[0:GROUPS * NCMP, 6 + kv, 0:CMP_HID]).then_inc(ga_done, 1)
                if b == 6:
                    act.wait_ge(ab_ps, 1)
                    nc.scalar.copy(abT[:].rearrange("p x t -> p (x t)"), psum[0:2 * FOX_H, 4, :]).then_inc(abT_done, 1)
                    act.wait_ge(gelu_in, 1)
                    A(hid2[:], hid1[:], ACT.Tanh, scale=GELU_C0).then_inc(gelu_tanh, 1)
                if b == 7:
                    act.wait_ge(hidT_ps, 1)
                    nc.scalar.copy(hidT[:].rearrange("p v c n -> p (v c n)"), psum[:, 7, 0:4 * GROUPS * NCMP]).then_inc(hidT_done, 1)
                if b == 8:
                    act.wait_ge(kvc_ps, 1)
                    nc.scalar.copy(kc[:].rearrange("p g d -> p (g d)"), psum[0:NCMP, 6, 0:256]).then_inc(kc_done, 1)
                if b == 9:
                    for f in range(2):
                        act.wait_ge(fill_ps, f + 1)
                        nc.scalar.copy(qnT[:, 2 * f:2 * f + 2, :].rearrange("p h t -> p (h t)"), psum[:, 4 + f, :]).then_inc(fillA, 1)
                if b == 10:
                    act.wait_ge(fill_ps, 5)
                    nc.scalar.copy(kswT[:, 0].rearrange("p g t -> p (g t)"), psum[:, 4, :]).then_inc(fillA, 1)
                    act.wait_ge(kcT_ps, 1)
                    nc.scalar.copy(kcT.rearrange("p g n -> p (g n)"), psum[:, 6, 0:2 * NCMP]).then_inc(kcT_done, 1)

            for b in range(GATES0):
                if b == 0:
                    split_x(0, MIX_G, 0)
                hi_piece(b, 0)
                if b == 0:
                    split_x(0, MIX_G, 1)
                hi_piece(b, 1)
                if b >= 1:
                    evac(b - 1)
                hook(b)
                if b == 0:
                    split_x(0, MIX_G, 2)
                hi_piece(b, 2)
                if b == 0:
                    split_x(0, MIX_G, 3)
                hi_piece(b, 3)
                if b == 0:
                    act.wait_ge(late_loaded, 16 * NLATE)
                    nc.scalar.copy(gf_hi[:], gf_raw[:]).then_inc(gf_hi_done, 1)
            evac(GATES0 - 1)

            def exp_unit(u):
                act.wait_ge(masked, u + 1)
                pr = prob[:, u % P_RING, :]
                A(pr[:, 0:P], pr[:, 0:P], ACT.Exp, bias=negmax[:, u, 0:1], scale=-1.0, accum_out=psums[:, u, 0:1])
                A(pr[:, P:384], pr[:, P:384], ACT.Exp, bias=negmax[:, u, 1:2], scale=-1.0,
                  accum_out=psums[:, u, 1:2]).then_inc(exped, 1)

            def pT_out(u):
                act.wait_ge(pT_ps, u + 1)
                if u >= 2:
                    act.wait_ge(pv_done, u - 1)
                nc.scalar.copy(pT[:, u % 2, :], psum[:, 2 + u % 2, 0:384]).then_inc(pT_done, 1)

            def head_hi(hs):
                act.wait_ge(pv_done, last_unit(hs) + 1)
                nc.scalar.copy(o_hi[:, o_place(hs), :], psum[:, 4 + hs % 2, 0:SEQ]).then_inc(o_hi_done, 1)

            done_at = {last_unit(hs) + 3: hs for hs in range(16)}
            hi_piece(GATES0, 0)
            for t in range(NU + 4):
                if 2 <= t < NU + 2:
                    pT_out(t - 2)
                if t == NU:
                    hi_piece(GATES0, 1)
                if t < NU:
                    exp_unit(t)
                    kind, h = UNITS[t]
                    if kind == "sel":
                        act.wait_ge(pcT_ps, h + 1)
                        if h >= 2:
                            act.wait_ge(pv_done, FOX_H + 2 * (h - 2) + 1)
                        nc.scalar.copy(pcT[:, h % 2, :], psum[0:NCMP, 6, 0:SEQ]).then_inc(pcT_done, 1)
                if t == 3:
                    act.wait_ge(c2_done, 1)
                    A(cp[:, 1], cp[:, 0], ACT.Exp).then_inc(ce_done, 1)
                if t - 1 in done_at:
                    head_hi(done_at[t - 1])

            def gate_evac(b, par, loop=None):
                g = b - GATES0
                for c in range(4):
                    src = psum[:, 2 * par + c // 2, (c % 2) * SEQ:(c % 2 + 1) * SEQ]
                    if isinstance(b, int):
                        dst, bias = gateT[:, 4 * g + c, :], hbias[:, 4 * g + c:4 * g + c + 1]
                    else:
                        dst = gateT[:, bass.ds(g * 4 + c, 1), :].rearrange("p o t -> p (o t)")
                        bias = hbias[:, bass.ds(g * 4 + c, 1)]
                    ins = A(dst, src, ACT.Tanh, bias=bias, scale=0.5)
                ins.then_inc(actA, 1)

            def hi4(b, middle):
                hi_piece(b, 0)
                hi_piece(b, 1)
                middle()
                hi_piece(b, 2)
                hi_piece(b, 3)

            def gates_block(b, par):
                def middle():
                    act.wait_ge(piece_used, b * 4)
                    gate_evac(b - 1, 1 - par)
                hi4(b, middle)

            act.wait_ge(hbias_done, 1)
            act.wait_ge(pv_done, NU)
            hi_piece(GATES0, 2)
            hi_piece(GATES0, 3)
            with act.Fori(0, (UPS0 - GATES0) // 2 - 1) as i:
                for q in range(2):
                    gates_block(i * 2 + (GATES0 + 1 + q), (GATES0 + 1 + q) % 2)
            gates_block(UPS0 - 1, (UPS0 - 1) % 2)

            def merged_hi(c):
                act.wait_ge(up_sum, c + 1)
                A(act_hi[:, 4 * c:4 * c + 4, :], up_a[:], ACT.Copy, scale=0.5).then_inc(mer_hi, 1)

            gates_block(UPS0, UPS0 % 2)
            for c in range(1, 5):
                for p in range(3):
                    hi_piece(UPS0 + c, p)
                merged_hi(c - 1)
                hi_piece(UPS0 + c, 3)
            act.dma_start(keys[:, 0], peer_sub_keys_1[0].rearrange("h k d -> k h d")).then_inc(keys_loaded, 16)
            act.dma_start(keys[:, 1], peer_sub_keys_2[0].rearrange("h k d -> k h d")).then_inc(keys_loaded, 16)
            act.dma_start(ffn_row[:], norm_ffn_gain.partition_broadcast(P)).then_inc(fin_loaded, 16)
            act.dma_start(final_row[:], norm_final_gain.unsqueeze(0).partition_broadcast(P)).then_inc(fin_loaded, 16)
            def part_squares(c):
                act.wait_ge(dveA, OUT0 + c - 7)
                for half in range(HALVES):
                    ins = A(xn[:, half, 512 * c:512 * c + 512], xres[:, half, 512 * c:512 * c + 512], ACT.Square,
                            accum_out=ss4[:, half, c:c + 1])
                ins.then_inc(part_sums, 1)

            for c in range(1, 4):
                hi4(OUT0 + c, lambda: None)
                part_squares(c - 1)
            hi_piece(QRY0, 0)
            for f in range(4):
                act.wait_ge(keyT_ps, f + 1)
                nc.scalar.copy(keysT[:, 4 * f:4 * f + 4, :].rearrange("p j k -> p (j k)"), psum[:, 6 + f % 2, :]).then_inc(keyT_done, 1)
            part_squares(3)
            act.wait_ge(ms_done, 1)
            A(rms[:, HALVES:2 * HALVES], ss[:, HALVES:2 * HALVES], ACT.Sqrt, bias=eps[:, 0:1],
              scale=1.0 / D).then_inc(squares, 1)
            hi_piece(QRY0, 1)
            split_x(KC, FFN_G, 0)
            split_x(KC, FFN_G, 1)
            for c in range(4):
                b = QRY0 + c
                if c > 0:
                    hi_piece(b, 0)
                    hi_piece(b, 1)
                    evac(b - 1)
                else:
                    split_x(KC, FFN_G, 2)
                hi_piece(b, 2)
                if c == 0:
                    split_x(KC, FFN_G, 3)
                hi_piece(b, 3)
            evac(NBLK - 1)

            def soft_exp_of(i, half, h0, h1):
                act.wait_ge(soft_in, i)
                A(gw[:, half, h0:h1], gw[:, half, h0:h1], ACT.Exp).then_inc(soft_exp, 1)

            def step(G, loop=False, middle=None):
                act.wait_ge(ge_in, G + 1)
                A(dots[:, 4, :], dots[:, 3, :], ACT.Tanh, scale=GELU_C0).then_inc(ge_tanh, 1)
                if middle:
                    middle()
                act.wait_ge(w_ready, G + 1)
                for s in range(GS):
                    if loop or G > 0:
                        act.wait_ge(up_used, G * GS + (s + 1 - GS))
                    A(diag[:, s, :], ident, ACT.Copy, scale=dots[:, 6, s:s + 1]).then_inc(diag_ready, 1)

            def final_stats(half):
                act.wait_ge(x2_done, half + 1)
                norm_stats(xres, xn, 2 * HALVES + half, half)

            soft_exp_of(1, 0, 0, 2)
            for G in range(GPH // 2):
                step(G)
                if G == 2:
                    soft_exp_of(2, 0, 2, PEER_H)
                if G == 7:
                    soft_exp_of(3, 1, 0, PEER_H)
            with act.Fori(GPH // 2, GPH) as i:
                step(i, True)
            step(GPH)
            step(GPH + 1, middle=lambda: final_stats(0))
            with act.Fori(GPH + 2, NG) as i:
                step(i, True)
            final_stats(1)

        @block.vector
        def _(dve):
            V = nc.vector
            tt, ts, stt = V.tensor_tensor, V.tensor_scalar, V.scalar_tensor_tensor
            n = [0]

            def seq(ins):
                ins.then_inc(dve_seq, 1)
                n[0] += 1

            def settle():
                dve.wait_ge(dve_seq, n[0])

            V.memset(ones[:], 1.0)
            V.memset(ab[:, 0, :, FOX_H:], 1.0)
            V.memset(ab[:, 1, :, 0:FOX_H], 1.0)
            V.memset(eps, EPS).then_inc(const_done, 1)

            def inverse_rms(i0, count):
                dve.wait_ge(squares, count)
                seq(V.reciprocal(rstd[:, i0:i0 + HALVES], rms[:, i0:i0 + HALVES]))
                settle()

            def scale_rows(dst, src, i0, q):
                cs = slice(512 * q, 512 * q + 512)
                for half in range(HALVES):
                    ins = ts(dst[:, half, cs], src[:, half, cs], rstd[:, i0 + half:i0 + half + 1], None, ALU.mult)
                ins.then_inc(normed, 1)

            def lo_x(n0, gain, q):
                for k in range(4 * q, 4 * q + 4):
                    dve.wait_ge(act_hi_done, n0 + k + 1)
                    stt(act_lo[:, k, :], psum[:, X_BANKS[n0 > 0][k % 4], 0:SEQ], cols[:, gain + k:gain + k + 1],
                        f32(act_hi[:, k, :]), ALU.mult, ALU.subtract).then_inc(act_lo_done, 1)

            dve.wait_ge(x_loaded[1], 16)
            V.tensor_tensor_reduce(out=sq[:, 1, :], in0=x_in[:, 1, :], in1=x_in[:, 1, :], scale=1.0, scalar=0.0,
                                   op0=ALU.mult, op1=ALU.add, accum_out=ss[:, 1:2]).then_inc(half_sum, 1)
            inverse_rms(0, 1)
            scale_rows(x_in, x_in, 0, 0)
            scale_rows(x_in, x_in, 0, 1)
            dve.wait_ge(cols_done, 1)
            ts(hbias, cols[:, MERGE_B:MERGE_B + 32], 0.5, None, ALU.mult).then_inc(hbias_done, 1)

            def lo_piece(b, p):
                dve.wait_ge(hi_done, b * 4 + (p + 1))
                tt(w_lo[:, p % 2], raw[:, p], f32(w_hi[:, p % 2]), ALU.subtract).then_inc(lo_done, 1)

            def evac(b):
                dve.wait_ge(piece_used, 4 * (b + 1))
                bank = psum[:, bank_of(b) + 1, :]
                two = bank.rearrange("p (c t) -> p c t", t=SEQ)
                if b < 2:
                    dst = qn[:, 1, 4 * b:4 * b + 4, :].rearrange("p h d -> p (h d)")
                elif b == 2:
                    dst, bank = kvcT[:, 1], two
                elif b < 5:
                    dst = kvsw[:, 1, b - 3].rearrange("p h d -> p (h d)")
                elif b < 9:
                    dst, bank = qkfT[:, 4 * (b - 5) + 2:4 * (b - 5) + 4, :], two
                elif b < 11:
                    dst = vf[:, 1, 512 * (b - 9):512 * (b - 9) + 512]
                elif b < QRY0:
                    c = b - OUT0
                    if c == 0:
                        dve.wait_ge(xres_loaded, 16)
                    for half in range(HALVES):
                        o = xres[:, half, 512 * c:512 * c + 512]
                        ins = tt(o, psum[:, bank_of(b) + half, :], o, ALU.add)
                    ins.then_inc(dveA, 1)
                    return
                else:
                    c = b - QRY0
                    dst, bank = qT[:, 4 * c + 2:4 * c + 4, :], two
                V.tensor_copy(dst, bank).then_inc(dveA, 1)

            def hook(b):
                if b == 3:
                    dve.wait_ge(gfz_ps, 1)
                    dve.wait_ge(late_loaded, 16 * NLATE)
                    tt(gz[:], psum[:, 7, 0:64].rearrange("p (h c) -> p h c", c=32),
                       bias32.unsqueeze(1).to_broadcast([P, HALVES, 32]), ALU.add).then_inc(gz_done, 1)
                    dve.wait_ge(gz_done, 1)
                    f = gz[:, :, NGATE:32]
                    seq(ts(nz[:], f, -1.0, None, ALU.mult))
                    settle()
                    tt(az[:], f, nz[:], ALU.max).then_inc(fx_done, 1)
                    dve.wait_ge(actA, 3)
                    dve.wait_ge(dveA, 3)
                    for kv, pc0 in ((0, KPOS), (1, VPOS)):
                        tok = kvcT[:, kv].rearrange("p g (n r) -> p r g n", r=CMP_STRIDE)
                        for m in range(2):
                            rs = slice(CMP_STRIDE * m, CMP_STRIDE * (m + 1))
                            pe_ = cols[:, pc0 + CMP_STRIDE * m:pc0 + CMP_STRIDE * (m + 1)]
                            for g in range(GROUPS):
                                ins = tt(flat[:, kv, rs, g, :], tok[:, :, g, m:m + NCMP],
                                         pe_.unsqueeze(2).to_broadcast([P, CMP_STRIDE, NCMP]), ALU.add)
                    ins.then_inc(flat_done, 1)
                if b == 4:
                    dve.wait_ge(gt_done, 1)
                    stt(lf[:], gz[:, :, NGATE:32], 0.0, lz[:], ALU.min, ALU.subtract).then_inc(lf_done, 1)
                    seq(ts(gate[:], tg[:], 0.5, 0.5, ALU.mult, ALU.add))
                if b == 5:
                    dve.wait_ge(cum_ps, 1)
                    c_ = psum[:, 5, 0:16].rearrange("p (h c) -> p h c", c=FOX_H)
                    ts(ab[:, 0, :, 0:FOX_H], c_, 1.0 / SCALE, None, ALU.mult)
                    ts(ab[:, 1, :, FOX_H:], c_, -1.0 / SCALE, None, ALU.mult).then_inc(ab_done, 1)
                if b == 6:
                    dve.wait_ge(ga_done, 2)
                    seq(tt(hid1[:], hid[:], hid[:], ALU.mult))
                    settle()
                    seq(ts(hid2[:], hid1[:], GELU_C1, 1.0, ALU.mult, ALU.add))
                    settle()
                    tt(hid1[:], hid2[:], hid[:], ALU.mult).then_inc(gelu_in, 1)
                    dve.wait_ge(gelu_tanh, 1)
                    seq(stt(hid1[:], hid2[:], 1.0, hid[:], ALU.add, ALU.mult))
                    settle()
                    ts(hid2[:], hid1[:], 0.5, None, ALU.mult).then_inc(gy_done, 1)
                if b == 8:
                    dve.wait_ge(kc_done, 1)
                    V.tensor_copy(vc.rearrange("p g d -> p (g d)"), psum[0:NCMP, 6, 256:512]).then_inc(vc_done, 1)
                if b == 9:
                    for f in (2, 3):
                        dve.wait_ge(fill_ps, f + 1)
                        V.tensor_copy(qnT[:, 2 * f:2 * f + 2, :].rearrange("p h t -> p (h t)"), psum[:, 4 + f, :]).then_inc(fillD, 1)
                if b == 10:
                    dve.wait_ge(fill_ps, 6)
                    V.tensor_copy(kswT[:, 1].rearrange("p g t -> p (g t)"), psum[:, 5, :]).then_inc(fillD, 1)

            for b in range(GATES0):
                if b == 0:
                    lo_x(0, MIX_G, 0)
                    scale_rows(x_in, x_in, 0, 2)
                lo_piece(b, 0)
                if b == 0:
                    lo_x(0, MIX_G, 1)
                    scale_rows(x_in, x_in, 0, 3)
                lo_piece(b, 1)
                if b >= 1:
                    evac(b - 1)
                hook(b)
                if b == 0:
                    lo_x(0, MIX_G, 2)
                lo_piece(b, 2)
                if b == 0:
                    lo_x(0, MIX_G, 3)
                lo_piece(b, 3)
                if b == 0:
                    dve.wait_ge(gf_hi_done, 1)
                    tt(gf_lo[:], gf_raw[:], f32(gf_hi[:]), ALU.subtract).then_inc(gf_lo_done, 1)
            evac(GATES0 - 1)

            mask = const("mask")

            def mask_unit(u):
                dve.wait_ge(score_ps, u + 1)
                if u >= P_RING:
                    dve.wait_ge(pT_ps, u - P_RING + 1)
                for half in range(HALVES):
                    cs = slice(0, P) if half == 0 else slice(P, 384)
                    ins = V.tensor_tensor_reduce(out=prob[:, u % P_RING, cs], in0=psum[:, u % 2, cs],
                                                 in1=mask[:, 0:P] if half == 0 else mask[:, P:384],
                                                 scale=-SCALE, scalar=-LOWEST, op0=ALU.add, op1=ALU.min,
                                                 accum_out=negmax[:, u, half:half + 1])
                ins.then_inc(masked, 1)

            def scale_unit(u):
                kind, h = UNITS[u]
                dve.wait_ge(exped, u + 1)
                if kind == "fox":
                    seq(V.reciprocal(pscale[:, u, :], psums[:, u, :]))
                else:
                    seq(V.reciprocal(prec[:, u, :], psums[:, u, :]))
                    settle()
                    col = 3 * h + 1 + ("sel", "win").index(kind)
                    seq(tt(pscale[:, u, :], prec[:, u, :], gate[:, :, col], ALU.mult))
                settle()
                pr = prob[:, u % P_RING, :]
                ts(pr[:, 0:P], pr[:, 0:P], pscale[:, u, 0:1], None, ALU.mult)
                ts(pr[:, P:384], pr[:, P:384], pscale[:, u, 1:2], None, ALU.mult).then_inc(p_ready, 1)

            def head_lo(hs):
                dve.wait_ge(o_hi_done, hs + 1)
                o = o_place(hs)
                tt(o_lo[:, o, :], psum[:, 4 + hs % 2, 0:SEQ], f32(o_hi[:, o, :]), ALU.subtract).then_inc(o_lo_done, 1)

            hn = [P, HALVES, NSA_H, NCMP]

            def over_heads(name):
                return const(name).rearrange("p (h n) -> p h n", n=NCMP).unsqueeze(2).to_broadcast(hn)

            def over_blocks(a):
                return a.rearrange("p (h c) -> p h c", c=NSA_H).unsqueeze(3).to_broadcast(hn)

            def cmp_before_exp():
                dve.wait_ge(cs_ps, 1)
                s_ = psum[:, 7, 0:256].rearrange("p (h c n) -> p h c n", h=HALVES, n=16)[:, :, :, 0:NCMP]
                for half in range(HALVES):
                    cn = over_heads("cneg")[:, half]
                    ins = stt(cp[:, 1, half], s_[:, half], SCALE, cn, ALU.mult, ALU.add)
                seq(ins)
                settle()
                seq(V.tensor_reduce(cmx, cp[:, 1], AX_X, ALU.max))
                settle()
                tt(cp[:, 0], cp[:, 1], over_blocks(cmx), ALU.subtract).then_inc(c2_done, 1)

            def cmp_after_exp():
                dve.wait_ge(ce_done, 1)
                seq(tt(cp[:, 2], cp[:, 1], over_heads("c01"), ALU.mult))
                settle()
                seq(V.tensor_reduce(csum, cp[:, 2], AX_X, ALU.add))
                settle()
                seq(ts(cmx, csum, TINY, None, ALU.max))
                settle()
                seq(V.reciprocal(csum, cmx))
                settle()
                seq(tt(crec.rearrange("p (h c) -> p h c", c=NSA_H), csum.rearrange("p (h c) -> p h c", c=NSA_H),
                       gate[:].rearrange("p h (c b) -> p h c b", b=3)[:, :, :, 0], ALU.mult))
                settle()
                tt(cp[:, 3], cp[:, 2], over_blocks(crec), ALU.mult).then_inc(pc_done, 1)

            done_at = {last_unit(hs) + 4: hs for hs in range(16)}
            lo_piece(GATES0, 0)
            for t in range(NU + 4):
                if t < NU:
                    mask_unit(t)
                if t == NU + 1:
                    lo_piece(GATES0, 1)
                if 1 <= t <= NU:
                    scale_unit(t - 1)
                if t == 1:
                    cmp_before_exp()
                if t == 5:
                    cmp_after_exp()
                if t in done_at:
                    head_lo(done_at[t])

            lo_piece(GATES0, 2)
            lo_piece(GATES0, 3)
            with dve.Fori(1, UPS0 - GATES0) as i:
                for p in range(PIECES):
                    lo_piece(i + GATES0, p)

            def up_out(c):
                b = UPS0 + c
                dve.wait_ge(piece_used, 4 * (b + 1))
                dve.wait_ge(actA, UPS0)
                bank = bank_of(b)
                for x_, o in ((0, up_a), (1, up_b)):
                    ps = psum[:, bank + 2 * x_:bank + 2 * x_ + 2, :].rearrange("p k t -> p (k t)")
                    g = gateT[:, 16 * x_ + 4 * c:16 * x_ + 4 * c + 4, :].rearrange("p k t -> p (k t)")
                    last = stt(o[:].rearrange("p k t -> p (k t)"), g, 1.0, ps, ALU.add, ALU.mult)
                last.then_inc(dveA, 1)
                dve.wait_ge(dveA, b - 7)
                tt(up_a[:], up_a[:], up_b[:], ALU.add).then_inc(up_sum, 1)

            def merged_lo(c):
                dve.wait_ge(mer_hi, c + 1)
                stt(act_lo[:, 4 * c:4 * c + 4, :], up_a[:], 0.5, f32(act_hi[:, 4 * c:4 * c + 4, :]),
                    ALU.mult, ALU.subtract).then_inc(mer_lo, 1)
                dve.wait_ge(mer_lo, c + 1)

            for b in range(UPS0, QRY0):
                lo_piece(b, 0)
                lo_piece(b, 1)
                if b > OUT0:
                    evac(b - 1)
                elif b > UPS0:
                    up_out(b - 1 - UPS0)
                lo_piece(b, 2)
                if UPS0 < b <= OUT0:
                    merged_lo(b - 1 - UPS0)
                lo_piece(b, 3)

            def top16(lists):
                for src, scratch, v, ix in lists:
                    seq(V.max(v[:, 0:8], src))
                settle()
                for src, scratch, v, ix in lists:
                    seq(V.max_index(ix[:, 0:8], v[:, 0:8], src))
                    seq(V.match_replace(scratch, v[:, 0:8], src, LOWEST))
                settle()
                for src, scratch, v, ix in lists:
                    seq(V.max(v[:, 8:16], scratch))
                settle()
                for src, scratch, v, ix in lists:
                    seq(V.max_index(ix[:, 8:16], v[:, 8:16], scratch))

            def top_lists(half, h):
                def scores(j):
                    return psum[:, SCORE_BANKS[half][j // 4], (j % 4) * NKEYS:(j % 4 + 1) * NKEYS]
                top16([(scores(2 * h + l), list2[:, 2 * (h % 2) + l, :], val[:, half, h, l, :], ind[:, half, h, l, :])
                       for l in range(2)])
                settle()
                if h % 2 == 1 and (half == 0 or h == PEER_H - 1):
                    V.sem_inc(topk_read, 1)

            def top_sums(half, h):
                cd = cand[:, h % 2]
                seq(tt(cd, val[:, half, h, 0, :].unsqueeze(2).to_broadcast([P, TOPK, TOPK]),
                       val[:, half, h, 1, :].unsqueeze(1).to_broadcast([P, TOPK, TOPK]), ALU.add))
                settle()
                top16([(cd.rearrange("p a b -> p (a b)"), cand2[:, h % 2, :], top[:, half, h, :], pos[:, half, h, :])])
                settle()

            def topk_end(half, h0, h1):
                nh = h1 - h0
                hs = slice(h0, h1)
                ns = nh * TOPK
                g = gw[:, half, hs]
                tt(g, top[:, half, hs], top[:, half, hs, 0:1].to_broadcast([P, nh, TOPK]), ALU.subtract).then_inc(soft_in, 1)
                seq(ts(pab[:, 0, hs], pos[:, half, hs], 4, None, ALU.logical_shift_right))
                seq(ts(pab[:, 1, hs], pos[:, half, hs], 15, None, ALU.bitwise_and))
                seq(V.tensor_copy(indf[:, hs], ind[:, half, hs]))
                settle()
                seq(V.tensor_copy(pabf[:, :, hs], pab[:, :, hs]))
                settle()
                full = [P, nh, TOPK, TOPK]
                iota = const("iota").unsqueeze(1).to_broadcast([P, ns, TOPK])
                oh = onehot[:, hs].rearrange("p h s c -> p (h s) c")
                ks = slice(h0 * TOPK, h1 * TOPK)
                for l in range(2):
                    seq(tt(oh, pabf[:, l, hs].rearrange("p h s -> p (h s)").unsqueeze(2).to_broadcast([P, ns, TOPK]),
                           iota, ALU.is_equal))
                    settle()
                    seq(tt(onehot[:, hs], onehot[:, hs], indf[:, hs, l, :].unsqueeze(2).to_broadcast(full), ALU.mult))
                    settle()
                    seq(V.tensor_reduce(key12[:, l, ks], oh, AX_X, ALU.add))
                    settle()
                seq(stt(eidf[:, ks], key12[:, 0, ks], float(NKEYS), key12[:, 1, ks], ALU.mult, ALU.add))
                settle()
                V.tensor_copy(eidx[:, half, ks], eidf[:, ks]).then_inc(eidx_done, 1)

            def topk_weights(count, half, h0, h1):
                hs = slice(h0, h1)
                g = gw[:, half, hs]
                dve.wait_ge(soft_exp, count)
                seq(V.tensor_reduce(wsum[:, 0, hs], g, AX_X, ALU.add))
                settle()
                seq(V.reciprocal(wsum[:, 1, hs], wsum[:, 0, hs]))
                settle()
                seq(tt(g, g, wsum[:, 1, hs].unsqueeze(2).to_broadcast([P, h1 - h0, TOPK]), ALU.mult))
                settle()

            lo_piece(QRY0, 0)
            evac(QRY0 - 1)
            dve.wait_ge(part_sums, 4)
            V.tensor_reduce(ss[:, HALVES:2 * HALVES], ss4[:], AX_X, ALU.add).then_inc(ms_done, 1)
            inverse_rms(HALVES, 2)
            scale_rows(xn, xres, HALVES, 0)
            scale_rows(xn, xres, HALVES, 1)
            lo_x(KC, FFN_G, 0)
            scale_rows(xn, xres, HALVES, 2)
            lo_piece(QRY0, 1)
            lo_x(KC, FFN_G, 1)
            scale_rows(xn, xres, HALVES, 3)

            def with_gain(half):
                dve.wait_ge(fin_loaded, 32)
                dve.wait_ge(xT_ps, 2 * KC)
                seq(tt(xn[:, half, :], xn[:, half, :], ffn_row[:], ALU.mult))

            def dot(G, half, s):
                dve.wait_ge(down_in[s % RING], G * 32 + (s // RING + 1) * 16)
                V.tensor_tensor_reduce(out=down_rows[:, s % RING, :], in0=down_rows[:, s % RING, :],
                                       in1=xn[:, half, :], scale=1.0, scalar=0.0, op0=ALU.mult, op1=ALU.add,
                                       accum_out=dots[:, 0, s:s + 1]).then_inc(down_used, 1)

            lo_x(KC, FFN_G, 2)
            lo_piece(QRY0, 2)
            lo_x(KC, FFN_G, 3)
            lo_piece(QRY0, 3)
            with_gain(0)
            for c in (1, 2):
                b = QRY0 + c
                lo_piece(b, 0)
                if c == 2:
                    top_sums(0, 0)
                evac(b - 1)
                lo_piece(b, 1)
                if c == 1:
                    with_gain(1)
                else:
                    top_sums(0, 1)
                    topk_end(0, 0, 2)
                lo_piece(b, 2)
                dve.wait_ge(ks_ps, c)
                top_lists(0, 2 * c - 2)
                lo_piece(b, 3)
                top_lists(0, 2 * c - 1)
            lo_piece(NBLK - 1, 0)
            evac(NBLK - 2)
            lo_piece(NBLK - 1, 1)
            dot(0, 0, 0)
            lo_piece(NBLK - 1, 2)
            dot(0, 0, 1)
            lo_piece(NBLK - 1, 3)
            dot(0, 0, 2)
            dot(0, 0, 3)
            evac(NBLK - 1)
            topk_weights(1, 0, 0, 2)

            def step(G, half, j, loop=False):
                for s in range(GS):
                    if loop or G > 0 or s >= RING:
                        dot(G, half, s)
                a = dots[:, 0, :]
                dve.wait_ge(down_used, G * GS + GS)
                tt(dots[:, 1, :], a, a, ALU.mult).then_inc(ge_sq, 1)
                dve.wait_ge(ge_sq, G + 1)
                ts(dots[:, 2, :], dots[:, 1, :], GELU_C1, 1.0, ALU.mult, ALU.add).then_inc(ge_poly, 1)
                dve.wait_ge(ge_poly, G + 1)
                tt(dots[:, 3, :], dots[:, 2, :], a, ALU.mult).then_inc(ge_in, 1)
                if loop or G > 0:
                    dve.wait_ge(w_ready, G)
                dve.wait_ge(ge_tanh, G + 1)
                stt(dots[:, 5, :], dots[:, 4, :], 1.0, a, ALU.add, ALU.mult).then_inc(ge_y, 1)
                if loop or G > 0:
                    dve.wait_ge(diag_ready, G * GS)
                dve.wait_ge(ge_y, G + 1)
                g = gw[:, half].rearrange("p h s -> p (h s)")
                g = g[:, bass.ds(j * GS, GS)] if loop else g[:, j * GS:j * GS + GS]
                stt(dots[:, 6, :], dots[:, 5, :], 0.5, g, ALU.mult, ALU.mult).then_inc(w_ready, 1)

            def residual(half):
                dve.wait_ge(up_used, SLOTS * (half + 1))
                tt(xres[:, half, :], psum[:, 4 * half:4 * half + 4, :].rearrange("p k n -> p (k n)"),
                   xres[:, half, :], ALU.add).then_inc(x2_done, 1)

            def final(half):
                dve.wait_ge(squares, 3 + half)
                i = 2 * HALVES + half
                seq(V.reciprocal(rstd[:, i:i + 1], rms[:, i:i + 1]))
                settle()
                stt(xn[:, half, :], xres[:, half, :], rstd[:, i:i + 1], final_row[:], ALU.mult, ALU.mult).then_inc(y_done, 1)

            for G in range(GPH // 2):
                step(G, 0, G)
                if G == 0:
                    dve.wait_ge(ks_ps, 4)
                    for h in (4, 5, 6, 7):
                        top_lists(0, h)
                elif G == 1:
                    for h in range(2, PEER_H):
                        top_sums(0, h)
                elif G == 2:
                    topk_end(0, 2, PEER_H)
                    topk_weights(2, 0, 2, PEER_H)
                elif G < 7:
                    dve.wait_ge(ks_ps, 5)
                    for h in (2 * G - 6, 2 * G - 5):
                        top_lists(1, h)
                        top_sums(1, h)
                else:
                    topk_end(1, 0, PEER_H)
                    topk_weights(3, 1, 0, PEER_H)
            with dve.Fori(GPH // 2, GPH) as i:
                step(i, 0, i, True)
            step(GPH, 1, 0)
            step(GPH + 1, 1, 1)
            residual(0)
            final(0)
            with dve.Fori(GPH + 2, NG) as i:
                step(i, 1, i - GPH, True)
            residual(1)
            final(1)


_INS = ['x', 'norm_mix_gain', 'w_in', 'nsa_gate_bias', 'fox_forget_bias', 'merge_gate_bias', 'k_cmp_pos', 'k_cmp_w1',
        'k_cmp_w2', 'v_cmp_pos', 'v_cmp_w1', 'v_cmp_w2', 'w_up_nsa', 'w_up_fox', 'w_out', 'norm_ffn_gain',
        'peer_w_query', 'peer_sub_keys_1', 'peer_sub_keys_2', 'peer_expert_down', 'peer_expert_up',
        'norm_final_gain']


def kernel(**inputs):
    import concourse.bacc as _bacc
    from concourse.bass_utils import run_bass_kernel_spmd as _run

    nc = _bacc.Bacc("TRN2", target_bir_lowering=False, num_devices=1)
    arrays, args = {}, []
    for name in _INS:
        a = np.ascontiguousarray(inputs[name])
        arrays[f"in_{name}_dram"] = a
        args.append(nc.dram_tensor(f"in_{name}_dram", a.shape, mybir.dt.from_np(a.dtype), kind="ExternalInput").ap())
    table = const_table()
    arrays["in_consts_dram"] = table
    args.append(nc.dram_tensor("in_consts_dram", table.shape, F32, kind="ExternalInput").ap())
    args.append(nc.dram_tensor("out_0_dram", (1, SEQ, D), F32, kind="ExternalOutput").ap())
    build(nc, *args)
    r = _run(nc, [arrays], core_ids=[0])
    return r.results[0]["out_0_dram"]
```

```python
from contextlib import ExitStack

import numpy as np

import concourse.bass as bass
from concourse import mybir

F32 = mybir.dt.float32
F32R = mybir.dt.float32r
U32 = mybir.dt.uint32
ALU = mybir.AluOpType
ACT = mybir.ActivationFunctionType
AX_X = mybir.AxisListType.X

P = 128
SEQ = 256
D = 2048
HALVES = SEQ // P
HD = 128
ROT = HD // 2
KC = D // P
NSA_H, GROUPS, HPG = 8, 2, 4
FOX_H = 8
CMP_STRIDE, CMP_BLOCK, CMP_HID = 16, 32, 256
NCMP = SEQ // CMP_STRIDE - CMP_BLOCK // CMP_STRIDE + 1
SCALE = float(HD) ** -0.5
EPS = 1e-6
NEG = -1e30
TINY = 1e-30
GELU_C0, GELU_C1 = 0.7978845608028654, 0.044715
PEER_H, NKEYS, TOPK = 8, 128, 16
SLOTS = PEER_H * TOPK
LOWEST = -3.0e38

Q_N, KV_C, KV_S, KV_W, G_N = 0, 1024, 1536, 2048, 2560
Q_F, V_F, F_F, G_A = 2584, 4632, 5656, 5664
NGATE = 3 * NSA_H

CT = {}


def _columns():
    at = 0
    for name, n in (("ident", P), ("tri", P), ("mask", 384), ("cos", HALVES * ROT), ("sin", HALVES * ROT),
                    ("cosc", ROT), ("sinc", ROT), ("c01", HALVES * NCMP), ("cneg", HALVES * NCMP),
                    ("iota", TOPK), ("augsel", FOX_H)):
        CT[name] = (at, at + n)
        at += n
    return at


NCONST = _columns()


def const_table():
    t = np.zeros((P, NCONST + NKEYS), np.float32)
    t[:, NCONST:] = np.arange(NKEYS)

    def put(name, a):
        lo, hi = CT[name]
        t[:a.shape[0], lo:hi] = a.reshape(a.shape[0], -1)

    i = np.arange(P)
    put("ident", np.eye(P, dtype=np.float32))
    put("tri", (i[:, None] <= i[None, :]).astype(np.float32))
    causal = np.where(i[None, :] <= i[:, None], 0.0, NEG)
    put("mask", np.concatenate([causal, np.zeros((P, P)), causal], axis=1))
    freq = np.float32(10000.0) ** (-np.arange(0, HD, 2, dtype=np.float32) / np.float32(HD))
    ang = np.arange(SEQ, dtype=np.float32)[:, None] * freq[None, :]
    put("cos", np.cos(ang).reshape(HALVES, P, ROT).transpose(1, 0, 2))
    put("sin", np.sin(ang).reshape(HALVES, P, ROT).transpose(1, 0, 2))
    end = np.arange(NCMP) * CMP_STRIDE + CMP_BLOCK - 1
    angc = end.astype(np.float32)[:, None] * freq[None, :]
    put("cosc", np.cos(angc))
    put("sinc", np.sin(angc))
    seen = (end[None, None, :] <= (i[:, None, None] + P * np.arange(HALVES)[None, :, None]))
    put("c01", seen.astype(np.float32))
    put("cneg", np.where(seen, 0.0, NEG))
    put("iota", np.tile(np.arange(TOPK), (P, 1)))
    sel = np.zeros((2 * FOX_H, FOX_H))
    for h in range(FOX_H):
        sel[h, h] = sel[FOX_H + h, h] = 1.0
    put("augsel", sel)
    return t


PIECES = 4
KPP = 4
GATES0, UPS0, OUT0, QRY0, NBLK = 11, 19, 23, 27, 31
CMP_AFTER = 4
W_IN_COL = [Q_N, Q_N + 512, KV_C, KV_S, KV_W, Q_F, Q_F + 512, Q_F + 1024, Q_F + 1536, V_F, V_F + 512]
TRANSPOSED = {2, 5, 6, 7, 8}

UNITS = [("fox", h) for h in range(FOX_H)] + [(b, h) for h in range(NSA_H) for b in ("sel", "win")]
NU = len(UNITS)
NSETUP, NLATE = 6, 6
P_RING = 4

GS = 8
GPH = SLOTS // GS
NG = HALVES * GPH
GPP = 2 * TOPK // GS
RING = 8
BT = 4
NB = P // BT


def build(nc, x, norm_mix_gain, w_in, nsa_gate_bias, fox_forget_bias, merge_gate_bias, k_cmp_pos, k_cmp_w1,
          k_cmp_w2, v_cmp_pos, v_cmp_w1, v_cmp_w2, w_up_nsa, w_up_fox, w_out, norm_ffn_gain, peer_w_query,
          peer_sub_keys_1, peer_sub_keys_2, peer_expert_down, peer_expert_up, norm_final_gain, consts, out):
    with ExitStack() as ctx:
        def sem(name):
            return ctx.enter_context(nc.semaphore(name))

        base = -(-nc.sbuf_base // 512) * 512

        def at(name, shape, kb, dt=F32):
            n = int(np.prod(shape[1:])) * 4
            assert base + kb * 1024 + n <= nc.sbuf_usable_end, name
            return nc.alloc_sbuf_tensor_at(name, shape, dt, offset=int(base + kb * 1024))

        ct = at("ct", [P, NCONST], 0)
        cols = at("cols", [P, P], 4.5)
        rows = at("rows", [64, 2, P], 5)
        ones = at("ones", [P, P], 6)
        small = at("small", [P, 896], 6.5)
        MERGE_B, MIX_G, FFN_G, KPOS, VPOS = 0, 32, 48, 64, 96
        cut = [0]

        def tile(*dims, dt=F32, parts=P):
            n = int(np.prod(dims))
            a = small[0:parts, cut[0]:cut[0] + n]
            cut[0] += n
            assert cut[0] <= 896
            if len(dims) > 1:
                names = "abcd"[:len(dims)]
                a = a.rearrange(f"p ({' '.join(names)}) -> p {' '.join(names)}", **dict(zip(names, dims)))
            return a if dt == F32 else a.bitcast(dt)

        def const(name, parts=P):
            lo, hi = CT[name]
            return ct[0:parts, lo:hi]

        ident = const("ident")
        act_hi = at("act_hi", [P, KC, SEQ], 10, F32R)
        act_lo = at("act_lo", [P, KC, SEQ], 26, F32R)
        raw = at("raw", [P, PIECES, KPP, 512], 42)
        w_hi = at("w_hi", [P, 2, KPP, 512], 74, F32R)
        w_lo = at("w_lo", [P, 2, KPP, 512], 90, F32R)
        qkfT = at("qkfT", [P, 2 * FOX_H, SEQ], 106)
        vf = at("vf", [P, HALVES, 1024], 122)
        kvsw = at("kvsw", [P, HALVES, 2, 4, HD], 130)
        gateT = at("gateT", [P, 32, SEQ], 106)
        keysT = at("keysT", [P, 2 * PEER_H, NKEYS], 106)
        keys = at("keys", [P, 2, PEER_H, HD], 114)
        ffn_row = at("ffn_row", [P, D], 122)
        final_row = at("final_row", [P, D], 10)
        qn = at("qn", [P, HALVES, NSA_H, HD], 138)
        qnT = at("qnT", [P, NSA_H, SEQ], 146)
        kswT = at("kswT", [P, 2, GROUPS, SEQ], 154)
        kvcT = at("kvcT", [P, 2, GROUPS, SEQ], 158)
        pcT = at("pcT", [NCMP, 2, SEQ], 158)
        xres = at("xres", [P, HALVES, D], 138)
        o_hi = at("o_hi", [P, 16, SEQ], 162, F32R)
        o_lo = at("o_lo", [P, 16, SEQ], 178, F32R)
        x_in = at("x_in", [P, HALVES, D], 162)
        rt = at("rt", [P, 2, HALVES, NSA_H, ROT], 178)
        flat = at("flat", [P, 2, CMP_BLOCK, GROUPS, NCMP], 186)
        aug = at("aug", [2 * FOX_H, FOX_H, SEQ], 186)
        xn = at("xn", [P, HALVES, D], 162)
        qT = at("qT", [P, 2 * PEER_H, SEQ], 178)
        prob = at("prob", [P, P_RING, 384], 194)
        pT = at("pT", [P, 2, 384], 200)
        gf_raw = at("gf_raw", [P, KC, 32], 194)
        gf_hi = at("gf_hi", [P, KC, 32], 196, F32R)
        gf_lo = at("gf_lo", [P, KC, 32], 198, F32R)
        gfT = at("gfT", [32, SEQ], 200)
        abT = at("abT", [2 * FOX_H, 2, SEQ], 203)
        w2 = at("w2", [P, 2, 2, HD], 205)
        up_a = at("up_a", [P, 4, SEQ], 194)
        up_b = at("up_b", [P, 4, SEQ], 198)
        sq = at("sq", [P, HALVES, D], 106)
        down_rows = [at(f"down_rows{r}", [P, D], 42 + 8 * r if r < 4 else 8 * r - 22) for r in range(RING)]
        onehot = at("onehot", [P, PEER_H, TOPK, TOPK], 114)
        cand = at("cand", [P, 2, TOPK, TOPK], 154)
        cand2 = at("cand2", [P, 2, TOPK * TOPK], 156)
        list2 = at("list2", [P, 4, NKEYS], 158)
        val = at("val", [P, HALVES, PEER_H, 2, TOPK], 160)
        ind = at("ind", [P, HALVES, PEER_H, 2, TOPK], 198, U32)
        top = at("top", [P, HALVES, PEER_H, TOPK], 200)
        pos = at("pos", [P, HALVES, PEER_H, TOPK], 201, U32)
        gw = at("gw", [P, HALVES, PEER_H, TOPK], 202)
        eidx = at("eidx", [P, HALVES, SLOTS], 203, U32)
        pab = at("pab", [P, 2, PEER_H, TOPK], 204, U32)
        pabf = at("pabf", [P, 2, PEER_H, TOPK], 205)
        indf = at("indf", [P, PEER_H, 2, TOPK], 206)
        acc = at("acc", [P, GS], 207)
        idx_stage = at("idx_stage", [P, 2, GS], 207.25, U32)
        numT = at("numT", [P, HALVES, 2, P], 0.5)
        dots = at("dots", [P, HALVES, SLOTS], 2.5)
        iota128 = at("iota128", [P, NKEYS], 3.5)
        wT = at("wT", [P, P], 4.5)
        W = at("W", [P, HALVES, NKEYS, P], 10)
        oh = [at("oh0", [P, 2, 2, BT, NKEYS], 178), at("oh1", [P, 2, 2, BT, NKEYS], 170)]
        u_raw = at("u_raw", [P, 2, D], 154)
        u_hi = at("u_hi", [P, 2, D], 178, F32R)
        u_lo = [at("u_lo0", [P, D], 194, F32R), at("u_lo1", [P, D], 170, F32R)]
        c_hi = at("c_hi", [P, 2, HALVES, P], 204, F32R)
        c_lo = [at("c_lo0", [P, HALVES, P], 206, F32R), at("c_lo1", [P, HALVES, P], 203, F32R)]
        key12 = at("key12", [P, 2, SLOTS], 5)
        eidf = at("eidf", [P, SLOTS], 6)

        ss = tile(3 * HALVES)
        ss4 = tile(HALVES, 4)
        wsum = tile(2, PEER_H)
        rms = tile(3 * HALVES)
        rstd = tile(3 * HALVES)
        eps = tile(1)
        sqrt_junk = tile(1)
        bias32 = tile(32)
        hbias = tile(32)
        gz = tile(HALVES, 32)
        nz = tile(HALVES, FOX_H)
        az = tile(HALVES, FOX_H)
        ez = tile(HALVES, FOX_H)
        lz = tile(HALVES, FOX_H)
        lf = tile(HALVES, FOX_H)
        tg = tile(HALVES, NGATE)
        gate = tile(HALVES, NGATE)
        ab = tile(2, HALVES, 2 * FOX_H)
        kcT = tile(GROUPS, NCMP)
        negmax = tile(NU, 2)
        psums = tile(NU, 2)
        prec = tile(NU, 2)
        pscale = tile(NU, 2)
        cmx, csum, crec = tile(16), tile(16), tile(16)
        kc = at("kc", [NCMP, GROUPS, HD], 196)
        crt = at("crt", [NCMP, 2, GROUPS, ROT], 197)
        vc = rows[0:NCMP, 0:2, :]
        hid = at("hid", [GROUPS * NCMP, 2, CMP_HID], 194)
        hid1 = at("hid1", [GROUPS * NCMP, 2, CMP_HID], 198)
        hid2 = at("hid2", [GROUPS * NCMP, 2, CMP_HID], 200)
        hidT = at("hidT", [P, 2, 2, GROUPS * NCMP], 202)
        cp = at("cp", [P, 4, HALVES, NSA_H, NCMP], 138)

        psum = ctx.enter_context(nc.psum_tensor("psum", [P, 8, 512], F32))

        x_loaded = [sem(f"x_loaded{half}") for half in range(HALVES)]
        setup_loaded = sem("setup_loaded")
        late_loaded = sem("late_loaded")
        raw_loaded = [sem(f"raw_loaded{p}") for p in range(PIECES)]
        xres_loaded = sem("xres_loaded")
        keys_loaded = sem("keys_loaded")
        fin_loaded = sem("fin_loaded")
        stored = sem("stored")
        dve_seq = sem("dve_seq")
        act_seq = sem("act_seq")
        pool_seq = sem("pool_seq")
        const_done = sem("const_done")
        cols_ps = sem("cols_ps")
        cols_done = sem("cols_done")
        hbias_done = sem("hbias_done")
        half_sum = sem("half_sum")
        part_sums = sem("part_sums")
        ms_done = sem("ms_done")
        squares = sem("squares")
        normed = sem("normed")
        xT_ps = sem("xT_ps")
        act_hi_done = sem("act_hi_done")
        act_lo_done = sem("act_lo_done")
        gf_hi_done = sem("gf_hi_done")
        gf_lo_done = sem("gf_lo_done")
        gf_ps = sem("gf_ps")
        gfT_done = sem("gfT_done")
        gfz_ps = sem("gfz_ps")
        gz_done = sem("gz_done")
        fx_done = sem("fx_done")
        lf_done = sem("lf_done")
        cum_ps = sem("cum_ps")
        ab_done = sem("ab_done")
        ab_ps = sem("ab_ps")
        abT_done = sem("abT_done")
        flat_done = sem("flat_done")
        cmp_used = sem("cmp_used")
        ga_done = sem("ga_done")
        gt_done = sem("gt_done")
        gy_done = sem("gy_done")
        hidT_ps = sem("hidT_ps")
        hidT_done = sem("hidT_done")
        kvc_ps = sem("kvc_ps")
        kc_done = sem("kc_done")
        vc_done = sem("vc_done")
        kcr_done = sem("kcr_done")
        kcT_ps = sem("kcT_ps")
        kcT_done = sem("kcT_done")
        roped = sem("roped")
        fill_ps = sem("fill_ps")
        fillA = sem("fillA")
        fillD = sem("fillD")
        cs_ps = sem("cs_ps")
        c2_done = sem("c2_done")
        ce_done = sem("ce_done")
        pc_done = sem("pc_done")
        hi_done = sem("hi_done")
        lo_done = sem("lo_done")
        piece_used = sem("piece_used")
        actA = sem("actA")
        dveA = sem("dveA")
        score_ps = sem("score_ps")
        masked = sem("masked")
        exped = sem("exped")
        p_ready = sem("p_ready")
        pT_ps = sem("pT_ps")
        pT_done = sem("pT_done")
        pv_done = sem("pv_done")
        o_hi_done = sem("o_hi_done")
        o_lo_done = sem("o_lo_done")
        pcT_ps = sem("pcT_ps")
        pcT_done = sem("pcT_done")
        aug_done = sem("aug_done")
        up_sum = sem("up_sum")
        mer_hi = sem("mer_hi")
        mer_lo = sem("mer_lo")
        keyT_ps = sem("keyT_ps")
        keyT_done = sem("keyT_done")
        ks_ps = sem("ks_ps")
        topk_read = sem("topk_read")
        soft_in = sem("soft_in")
        soft_exp = sem("soft_exp")
        eidx_done = sem("eidx_done")
        idx_copied = sem("idx_copied")
        turn = sem("turn")
        down_in = [sem(f"down_in{r}") for r in range(RING)]
        down_used = sem("down_used")
        gelu_in = sem("gelu_in")
        gelu_tanh = sem("gelu_tanh")
        acc_out = sem("acc_out")
        num_done = sem("num_done")
        num_ps = sem("num_ps")
        numT_done = sem("numT_done")
        inner_done = sem("inner_done")
        tanh_done = sem("tanh_done")
        w_done = sem("w_done")
        w_ps = sem("w_ps")
        wT_done = sem("wT_done")
        dist_done = sem("dist_done")
        oh2_ready = sem("oh2_ready")
        oh_ready = sem("oh_ready")
        W_ps = sem("W_ps")
        W_out = sem("W_out")
        u_loaded = [sem(f"u_loaded{r}") for r in range(2)]
        u_hi_done = sem("u_hi_done")
        u_lo_done = sem("u_lo_done")
        c_hi_done = sem("c_hi_done")
        c_lo_done = sem("c_lo_done")
        half_summed = sem("half_summed")
        chunk_used = sem("chunk_used")
        row_loaded = sem("row_loaded")
        x2_done = sem("x2_done")
        y_done = sem("y_done")

        OUT_COLS = (slice(0, D // 2), slice(D // 2, D))
        ACT_TOKENS = (BT, 1)

        w_in_v = w_in[0].rearrange("(k p) n -> p k n", p=P)
        w_un_v = w_up_nsa[0].rearrange("(k p) n -> p k n", p=P)
        w_uf_v = w_up_fox[0].rearrange("(k p) n -> p k n", p=P)
        w_out_v = w_out[0].rearrange("(k p) n -> p k n", p=P)
        w_q_v = peer_w_query[0].rearrange("(k p) n -> p k n", p=P)
        x_v = x[0].rearrange("(h p) d -> p h d", p=P)
        out_v = out[0].rearrange("(h p) d -> p h d", p=P)

        def f32(a):
            return a.bitcast(F32)

        def bank_of(b):
            if b < UPS0:
                return 2 * (b % 2)
            return 4 * (b % 2)

        X_BANKS = ((2, 3, 4, 5), (2, 3, 6, 7))
        SCORE_BANKS = ((2, 3, 6, 7), (4, 5, 6, 7))

        def uses(b):
            return b + 1 + 2 * (1 if not isinstance(b, int) or b > CMP_AFTER else 0)

        def kT_of(kind, h):
            return qkfT[:, FOX_H + h, :] if kind == "fox" else kswT[:, ("sel", "win").index(kind), h // HPG, :]

        def q_of(kind, h):
            return qkfT[:, h, :] if kind == "fox" else qnT[:, h, :]

        def v_of(kind, h, kb):
            if kind == "fox":
                return vf[:, kb, h * HD:(h + 1) * HD]
            return kvsw[:, kb, ("sel", "win").index(kind), GROUPS + h // HPG, :]

        def head_slot(kind, h):
            return h if kind == "fox" else FOX_H + h

        def o_place(hs):
            return NSA_H + hs if hs < FOX_H else hs - FOX_H

        def last_unit(hs):
            return hs if hs < FOX_H else FOX_H + 2 * (hs - FOX_H) + 1

        block = ctx.enter_context(nc.Block())

        @block.sync
        def _(sp):
            sp.dma_start(x_in[:, 0, :], x_v[:, 0, :]).then_inc(x_loaded[0], 16)
            sp.dma_start(x_in[:, 1, :], x_v[:, 1, :]).then_inc(x_loaded[1], 16)
            for dst, src in ((rows[0:32, 0, :], merge_gate_bias[0].rearrange("(c p) -> c p", p=P)),
                             (rows[32:48, 0, :], norm_mix_gain[0].rearrange("(c p) -> c p", p=P)),
                             (rows[48:64, 0, :], norm_ffn_gain[0].rearrange("(c p) -> c p", p=P)),
                             (rows[0:32, 1, :], k_cmp_pos[0]), (rows[32:64, 1, :], v_cmp_pos[0])):
                sp.dma_start(dst, src).then_inc(setup_loaded, 16)

            def load(b, src, first=False):
                for p in range(PIECES):
                    if not first:
                        sp.wait_ge(lo_done, 4 * (b - 1) + p + 1)
                    sp.dma_start(raw[:, p], src(p)).then_inc(raw_loaded[p], 16)

            def w_in_piece(col):
                return lambda p: w_in_v[:, KPP * p:KPP * p + KPP, col]

            for b in range(GATES0):
                col = W_IN_COL[b]
                if b == CMP_AFTER + 1:
                    for kv, w1 in enumerate((k_cmp_w1, v_cmp_w1)):
                        w1_v = w1[0].rearrange("(r d) h -> d r h", d=HD)
                        for p in range(PIECES):
                            if kv == 0:
                                sp.wait_ge(lo_done, 4 * (b - 1) + p + 1)
                            else:
                                sp.wait_ge(cmp_used, p + 1)
                            sp.dma_start(raw[:, p].rearrange("p k n -> p (k n)").rearrange("p (r h) -> p r h", h=CMP_HID),
                                         w1_v[:, 8 * p:8 * p + 8, :]).then_inc(raw_loaded[p], 16)
                    for p in range(PIECES):
                        sp.wait_ge(cmp_used, PIECES + p + 1)
                        sp.dma_start(raw[:, p], w_in_piece(slice(col, col + 512))(p)).then_inc(raw_loaded[p], 16)
                else:
                    load(b, w_in_piece(slice(col, col + 512)), first=b == 0)
            with sp.Fori(0, UPS0 - GATES0) as i:
                load(i + GATES0, w_in_piece(bass.ds(i * 512 + G_A, 512)))
            for c in range(4):
                cs = slice(512 * c, 512 * c + 512)
                load(UPS0 + c, lambda p: (w_un_v if p < 2 else w_uf_v)[:, KPP * (p % 2):KPP * (p % 2) + KPP, cs])
            sp.wait_ge(o_hi_done, 16)
            sp.dma_start(xres[:], x_v).then_inc(xres_loaded, 16)
            for c in range(4):
                cs = slice(512 * c, 512 * c + 512)
                load(OUT0 + c, lambda p: w_out_v[:, KPP * p:KPP * p + KPP, cs])
            for c in range(4):
                cs = slice(512 * c, 512 * c + 512)
                load(QRY0 + c, lambda p: w_q_v[:, KPP * p:KPP * p + KPP, cs])
            up_v = peer_expert_up[0].rearrange("(c p) d -> p c d", p=P)
            sp.wait_ge(eidx_done, 8)
            sp.wait_ge(down_used, SLOTS)
            for q in range(2):
                sp.dma_start(u_raw[:, q, :], up_v[:, q, :]).then_inc(u_loaded[q], 16)
            with sp.Fori(1, NKEYS // 2) as i:
                for q in range(2):
                    sp.wait_ge(u_lo_done, i * 2 + (q - 1))
                    sp.dma_start(u_raw[:, q, :], up_v[:, bass.ds(i * 2 + q, 1), :].rearrange("p o d -> p (o d)")).then_inc(u_loaded[q], 16)
            sp.dma_start(final_row[:], norm_final_gain.unsqueeze(0).partition_broadcast(P)).then_inc(row_loaded, 16)
            for half in range(HALVES):
                for q, cs in enumerate(OUT_COLS):
                    sp.wait_ge(y_done, 2 * half + q + 1)
                    sp.dma_start(out_v[:, half, cs], xn[:, half, cs]).then_inc(stored, 16)
            sp.wait_ge(stored, 2 * 16 * HALVES)

        @block.tensor
        def _(pe):
            def mm(*a, **k):
                return nc.tensor.matmul(*a, skip_group_check=True, **k)

            pe.wait_ge(setup_loaded, 16 * NSETUP)
            nc.tensor.transpose(psum[:, 7, 0:64], rows[:, 0, :], ident[0:64, 0:64])
            nc.tensor.transpose(psum[:, 7, 64:128], rows[:, 1, :], ident[0:64, 0:64]).then_inc(cols_ps, 1)

            def transpose_x(src, n0, chunks):
                for k in chunks:
                    if k % 4 == 0:
                        pe.wait_ge(normed, (n0 + k) // 4 + 1)
                    if k >= 4:
                        pe.wait_ge(act_lo_done, n0 + k - 3)
                    for half in range(HALVES):
                        ins = nc.tensor.transpose(psum[:, X_BANKS[n0 > 0][k % 4], half * P:(half + 1) * P],
                                                  src[:, half, k * P:(k + 1) * P], ident)
                    ins.then_inc(xT_ps, 1)

            def nat_piece(hi, lo, p, banks, n=512, kpp=KPP, w0=0):
                for k in range(kpp):
                    kk = kpp * p + k
                    for half in range(HALVES):
                        t = slice(half * P, (half + 1) * P)
                        o = banks[half]
                        mm(o, act_hi[:, kk, t], hi[:, k, :], start=kk == 0, stop=False)
                        mm(o, act_hi[:, kk, t], lo[:, k, :], start=False, stop=False)
                        last = mm(o, act_lo[:, kk, t], hi[:, k, :], start=False, stop=kk == KC - 1)
                return last

            def tr_piece(hi, lo, ahi, alo, k0, bank, nk):
                for k in range(KPP):
                    kk = k0 + k
                    for c in range(4):
                        o = psum[:, bank + c // 2, (c % 2) * SEQ:(c % 2 + 1) * SEQ]
                        cs = slice(c * P, (c + 1) * P)
                        first = kk == 0 and c % 2 == 0
                        mm(o, hi[:, k, cs], ahi[:, kk, :], start=first, stop=False)
                        mm(o, hi[:, k, cs], alo[:, kk, :], start=False, stop=False)
                        last = mm(o, lo[:, k, cs], ahi[:, kk, :], start=False, stop=kk == nk - 1)
                return last

            def weight_block(b, par, kind, before=None, behind=None):
                bank = (2 if kind in ("nat", "tr") else 4) * par
                for p in range(PIECES):
                    if before:
                        before(p)
                    pe.wait_ge(lo_done, b * 4 + (p + 1))
                    if kind == "out" and p == PIECES - 1:
                        pe.wait_ge(mer_lo, 4)
                    hi, lo = w_hi[:, p % 2], w_lo[:, p % 2]
                    if kind in ("nat", "out"):
                        last = nat_piece(hi, lo, p, [psum[:, bank, :], psum[:, bank + 1, :]])
                    elif kind in ("tr", "qry"):
                        last = tr_piece(hi, lo, act_hi, act_lo, KPP * p, bank, KC)
                    else:
                        fox = p // 2
                        last = tr_piece(hi, lo, o_hi[:, 8 * fox:8 * fox + 8], o_lo[:, 8 * fox:8 * fox + 8],
                                        KPP * (p % 2), bank + 2 * fox, 2 * KPP)
                    last.then_inc(piece_used, 1)
                    if behind:
                        behind(p)

            def beside_norm(src, n0):
                def before(p):
                    transpose_x(src, n0, range(0, 8) if p == 0 else range(4 * p + 4, 4 * p + 8) if p < 3 else ())
                    pe.wait_ge(act_lo_done, n0 + KPP * (p + 1))
                return before

            def after(b):
                if b == 1:
                    pe.wait_ge(gf_lo_done, 1)
                    pe.wait_ge(cols_done, 1)
                    o = psum[0:32, 7, 0:SEQ]
                    for k in range(KC):
                        mm(o, gf_hi[:, k, :], act_hi[:, k, :], start=k == 0, stop=False)
                        mm(o, gf_hi[:, k, :], act_lo[:, k, :], start=False, stop=False)
                        last = mm(o, gf_lo[:, k, :], act_hi[:, k, :], start=False, stop=k == KC - 1)
                    last.then_inc(gf_ps, 1)
                if b == 2:
                    pe.wait_ge(gfT_done, 1)
                    for half in range(HALVES):
                        ins = nc.tensor.transpose(psum[:, 7, half * 32:half * 32 + 32], gfT[:, half * P:(half + 1) * P],
                                                  ident[0:32, 0:32])
                    ins.then_inc(gfz_ps, 1)
                if b == 4:
                    pe.wait_ge(lf_done, 1)
                    tri = const("tri")
                    mm(psum[:, 5, 0:8], tri, lf[:, 0, :], start=True, stop=True)
                    mm(psum[:, 5, 8:16], ones[:], lf[:, 0, :], start=True, stop=False)
                    mm(psum[:, 5, 8:16], tri, lf[:, 1, :], start=False, stop=True).then_inc(cum_ps, 1)
                    pe.wait_ge(flat_done, 1)
                    pe.wait_ge(gz_done, 1)
                    for kv in range(2):
                        for p in range(PIECES):
                            pe.wait_ge(raw_loaded[p], 16 * (CMP_AFTER + 2 + kv))
                            w1 = raw[:, p].rearrange("p k n -> p (k n)").rearrange("p (r h) -> p r h", h=CMP_HID)
                            for r in range(8):
                                last = mm(psum[0:GROUPS * NCMP, 6 + kv, 0:CMP_HID],
                                          flat[:, kv, 8 * p + r, :, :].rearrange("p g n -> p (g n)"), w1[:, r, :],
                                          start=p == 0 and r == 0, stop=p == PIECES - 1 and r == 7)
                            last.then_inc(cmp_used, 1)
                if b == 5:
                    pe.wait_ge(ab_done, 1)
                    for x_ in range(2):
                        for half in range(HALVES):
                            ins = nc.tensor.transpose(psum[0:16, 4, x_ * SEQ + half * P:x_ * SEQ + (half + 1) * P],
                                                      ab[:, x_, half, :], ident)
                    ins.then_inc(ab_ps, 1)
                if b == 6:
                    pe.wait_ge(gy_done, 1)
                    for kv in range(2):
                        for hc in range(2):
                            c = (2 * kv + hc) * GROUPS * NCMP
                            ins = nc.tensor.transpose(psum[:, 7, c:c + GROUPS * NCMP], hid2[:, kv, hc * P:(hc + 1) * P],
                                                      ident[0:GROUPS * NCMP, 0:GROUPS * NCMP])
                    ins.then_inc(hidT_ps, 1)
                if b == 7:
                    pe.wait_ge(hidT_done, 1)
                    pe.wait_ge(late_loaded, 16 * NLATE)
                    for kv in range(2):
                        for g in range(GROUPS):
                            for hc in range(2):
                                last = mm(psum[0:NCMP, 6, kv * 256 + g * HD:kv * 256 + (g + 1) * HD],
                                          hidT[:, kv, hc, g * NCMP:(g + 1) * NCMP], w2[:, kv, hc, :],
                                          start=hc == 0, stop=hc == 1)
                    last.then_inc(kvc_ps, 1)
                if b == 8:
                    pe.wait_ge(roped, 1)
                    pe.wait_ge(ab_ps, 1)
                    pe.wait_ge(abT_done, 1)
                    pe.wait_ge(ab_done, 1)
                    pe.wait_ge(kc_done, 1)
                    pe.wait_ge(vc_done, 1)
                    pe.wait_ge(hidT_done, 1)
                    for f in range(4):
                        for hh in range(2):
                            for half in range(HALVES):
                                ins = nc.tensor.transpose(
                                    psum[:, 4 + f, hh * SEQ + half * P:hh * SEQ + (half + 1) * P],
                                    qn[:, half, 2 * f + hh, :], ident)
                        ins.then_inc(fill_ps, 1)
                if b == 9:
                    pe.wait_ge(roped, 3)
                    for f in range(2):
                        pe.wait_ge(fillA, 2)
                        for g in range(GROUPS):
                            for half in range(HALVES):
                                ins = nc.tensor.transpose(
                                    psum[:, 4 + f, g * SEQ + half * P:g * SEQ + (half + 1) * P],
                                    kvsw[:, half, f, g, :], ident)
                        ins.then_inc(fill_ps, 1)
                    pe.wait_ge(kcr_done, 1)
                    pe.wait_ge(fillD, 2)
                    for g in range(GROUPS):
                        ins = nc.tensor.transpose(psum[:, 6, g * NCMP:(g + 1) * NCMP], kc[:, g, :],
                                                  ident[0:NCMP, 0:NCMP])
                    ins.then_inc(kcT_ps, 1)
                if b == 10:
                    pe.wait_ge(kcT_done, 1)
                    pe.wait_ge(fillA, 3)
                    pe.wait_ge(fillD, 3)
                    for half in range(HALVES):
                        for h in range(NSA_H):
                            last = mm(psum[:, 7, (half * NSA_H + h) * 16:(half * NSA_H + h) * 16 + NCMP],
                                      qnT[:, h, half * P:(half + 1) * P], kcT[:, h // HPG, :],
                                      start=half == 0 and h == 0, stop=True)
                    last.then_inc(cs_ps, 1)

            for b in range(GATES0):
                if b >= 2:
                    pe.wait_ge(actA, b - 1)
                    pe.wait_ge(dveA, b - 1)
                weight_block(b, b % 2, "tr" if b in TRANSPOSED else "nat",
                             before=beside_norm(x_in, 0) if b == 0 else None)
                after(b)

            def score(u):
                kind, h = UNITS[u]
                if u >= 2:
                    pe.wait_ge(masked, u - 1)
                q, k = q_of(kind, h), kT_of(kind, h)
                if kind == "fox":
                    pe.wait_ge(aug_done, h + 1)
                S = psum[:, u % 2, :]
                for half in range(HALVES):
                    n = P * (half + 1)
                    o = S[:, P * half:P * half + n]
                    last = mm(o, q[:, half * P:(half + 1) * P], k[:, 0:n], start=True, stop=kind != "fox")
                    if kind == "fox":
                        last = mm(o, aug[:, h, half * P:(half + 1) * P], abT[:, 1, 0:n], start=False, stop=True)
                last.then_inc(score_ps, 1)

            def trans(u):
                pe.wait_ge(p_ready, u + 1)
                if u >= 2:
                    pe.wait_ge(pT_done, u - 1)
                for j in range(3):
                    ins = nc.tensor.transpose(psum[:, 2 + u % 2, j * P:(j + 1) * P],
                                              prob[:, u % P_RING, j * P:(j + 1) * P], ident)
                ins.then_inc(pT_ps, 1)

            def cmp_trans(h):
                if h == 0:
                    pe.wait_ge(pc_done, 1)
                if h >= 1:
                    pe.wait_ge(pcT_done, h)
                for half in range(HALVES):
                    ins = nc.tensor.transpose(psum[0:NCMP, 6, half * P:(half + 1) * P],
                                              cp[:, 3, half, h, :], ident)
                ins.then_inc(pcT_ps, 1)

            def pv(u):
                kind, h = UNITS[u]
                hs = head_slot(kind, h)
                o = psum[:, 4 + hs % 2, 0:SEQ]
                begins = kind != "win"
                if begins and hs >= 2:
                    pe.wait_ge(o_lo_done, hs - 1)
                if kind == "sel":
                    pe.wait_ge(pcT_done, h + 1)
                    mm(o, vc[:, h // HPG, :], pcT[:, h % 2, :], start=True, stop=False)
                pe.wait_ge(pT_done, u + 1)
                pt = pT[:, u % 2, :]
                mm(o, v_of(kind, h, 0), pt[:, 0:SEQ], start=kind == "fox", stop=False)
                mm(o[:, P:SEQ], v_of(kind, h, 1), pt[:, SEQ:SEQ + P], start=False,
                   stop=kind != "sel").then_inc(pv_done, 1)

            pe.wait_ge(actA, GATES0)
            pe.wait_ge(dveA, GATES0)
            pe.wait_ge(abT_done, 1)
            for t in range(NU + 3):
                if t < NU:
                    score(t)
                    kind, h = UNITS[t]
                    if kind == "sel":
                        cmp_trans(h)
                if 2 <= t < NU + 2:
                    trans(t - 2)
                if t >= 3:
                    pv(t - 3)

            pe.wait_ge(masked, NU)
            pe.wait_ge(pT_done, NU)
            with pe.Fori(0, (UPS0 - GATES0) // 2) as i:
                for q in range(2):
                    b = i * 2 + (GATES0 + q)
                    pe.wait_ge(actA, i * 2 + (GATES0 + q - 1))
                    weight_block(b, (GATES0 + q) % 2, "tr")
            pe.wait_ge(o_lo_done, 16)
            with pe.Fori(0, 2) as i:
                for q in range(2):
                    if q == 1:
                        pe.wait_ge(actA, UPS0)
                    pe.wait_ge(dveA, i * 2 + (UPS0 + q - 9))
                    weight_block(i * 2 + (UPS0 + q), (UPS0 + q) % 2, "ups")
            pe.wait_ge(mer_lo, 3)
            with pe.Fori(0, 2) as i:
                for q in range(2):
                    pe.wait_ge(dveA, i * 2 + (OUT0 + q - 9))
                    weight_block(i * 2 + (OUT0 + q), (OUT0 + q) % 2, "out")

            pe.wait_ge(keys_loaded, 32)
            pe.wait_ge(dveA, QRY0 - 12)
            for f in range(4):
                if f >= 2:
                    pe.wait_ge(keyT_done, f - 1)
                for c in range(4):
                    j = 4 * f + c
                    ins = nc.tensor.transpose(psum[:, 6 + f % 2, c * P:(c + 1) * P], keys[:, j % 2, j // 2, :], ident)
                ins.then_inc(keyT_ps, 1)

            pe.wait_ge(keyT_done, 4)

            def key_scores(half, pair):
                for j in range(4 * pair, 4 * pair + 4):
                    last = mm(psum[:, SCORE_BANKS[half][pair], (j % 4) * NKEYS:(j % 4 + 1) * NKEYS],
                              qT[:, j, half * P:(half + 1) * P], keysT[:, j, :], start=True, stop=True)
                return last

            def scores_behind(c):
                def behind(p):
                    if p == 0:
                        pe.wait_ge(actA, QRY0 + c - 8)
                        pe.wait_ge(dveA, QRY0 + c - 8)
                        key_scores(0, c - 1).then_inc(ks_ps, 1)
                return behind

            for c in range(4):
                pe.wait_ge(dveA, QRY0 + c - 9)
                if c >= 2:
                    pe.wait_ge(actA, QRY0 + c - 9)
                weight_block(QRY0 + c, (QRY0 + c) % 2, "qry", before=beside_norm(xn, KC) if c == 0 else None,
                             behind=scores_behind(c) if c > 0 else None)
            pe.wait_ge(actA, NBLK - 8)
            pe.wait_ge(dveA, NBLK - 8)
            key_scores(0, 3).then_inc(ks_ps, 1)

            pe.wait_ge(topk_read, 4)
            for pair in range(4):
                last = key_scores(1, pair)
            last.then_inc(ks_ps, 1)

            def numbers_T(half):
                pe.wait_ge(num_done, half + 1)
                if half > 0:
                    pe.wait_ge(numT_done, half)
                for l in range(2):
                    ins = nc.tensor.transpose(psum[:, 0, l * P:(l + 1) * P], key12[:, l, :], ident)
                ins.then_inc(num_ps, 1)

            def weights_T(half):
                pe.wait_ge(w_done, half + 1)
                if half > 0:
                    pe.wait_ge(wT_done, half)
                nc.tensor.transpose(psum[:, 1, 0:P], gw[:, half].rearrange("p h s -> p (h s)"), ident).then_inc(w_ps, 1)

            def spread(b, half, par, first=False):
                pe.wait_ge(oh_ready, b + 1)
                pe.wait_ge(oh2_ready, b + 1)
                if not first:
                    pe.wait_ge(W_out, b - 1)
                for q in range(BT):
                    ins = mm(psum[:, 2 + par, q * P:(q + 1) * P], oh[half][:, 0, par, q, :], oh[half][:, 1, par, q, :],
                             start=True, stop=True)
                ins.then_inc(W_ps, 1)

            numbers_T(0)
            weights_T(0)
            numbers_T(1)
            spread(0, 0, 0, first=True)
            spread(1, 0, 1, first=True)
            with pe.Fori(1, NB // 2) as i:
                for q in range(2):
                    spread(i * 2 + q, 0, q)
            weights_T(1)
            with pe.Fori(NB // 2, NB) as i:
                for q in range(2):
                    spread(i * 2 + q, 1, q)

            pe.wait_ge(W_out, 2 * NB)
            pe.wait_ge(wT_done, 2)
            pe.wait_ge(topk_read, 5)

            def up_chunk(i, q, first=False, end=False):
                pe.wait_ge(u_lo_done, i + 1)
                pe.wait_ge(c_lo_done, i + 1)
                for half in range(HALVES):
                    hi, lo = c_hi[:, q, 1 - half, :], c_lo[q][:, 1 - half, :]
                    for c in range(4):
                        o, n = psum[:, 4 * half + c, :], slice(512 * c, 512 * c + 512)
                        mm(o, hi, u_hi[:, q, n], start=first, stop=False)
                        mm(o, hi, u_lo[q][:, n], start=False, stop=False)
                        last = mm(o, lo, u_hi[:, q, n], start=False, stop=end)
                    last.then_inc(half_summed if half == 0 else chunk_used, 1)

            up_chunk(0, 0, first=True)
            up_chunk(1, 1)
            with pe.Fori(1, NKEYS // 2 - 1) as i:
                for q in range(2):
                    up_chunk(i * 2 + q, q)
            up_chunk(NKEYS - 2, 0)
            up_chunk(NKEYS - 1, 1, end=True)

        @block.gpsimd
        def _(pool):
            n = [0]

            def seq(ins):
                ins.then_inc(pool_seq, 1)
                n[0] += 1

            def rope(x1, x2, cos, sin, t1, t2, done, count):
                tt = nc.gpsimd.tensor_tensor
                seq(tt(t1, x1, sin, ALU.mult))
                seq(tt(t2, x2, sin, ALU.mult))
                pool.wait_ge(pool_seq, n[0])
                seq(tt(x1, x1, cos, ALU.mult))
                seq(tt(x2, x2, cos, ALU.mult))
                pool.wait_ge(pool_seq, n[0])
                seq(tt(x1, x1, t2, ALU.subtract))
                pool.wait_ge(pool_seq, n[0])
                tt(x2, x2, t1, ALU.add).then_inc(done, 1)
                pool.wait_ge(done, count)

            def table(name, heads):
                t = const(name).rearrange("p (h r) -> p h r", h=HALVES)
                return t.unsqueeze(2).to_broadcast([P, HALVES, heads, ROT])

            pool.wait_ge(setup_loaded, 16 * NSETUP)
            pool.wait_ge(actA, 2)
            pool.wait_ge(dveA, 2)
            rope(qn[:, :, :, 0:ROT], qn[:, :, :, ROT:HD], table("cos", NSA_H), table("sin", NSA_H),
                 rt[:, 0], rt[:, 1], roped, 1)
            pool.wait_ge(actA, 5)
            pool.wait_ge(dveA, 5)
            for sw in range(2):
                rope(kvsw[:, :, sw, 0:GROUPS, 0:ROT], kvsw[:, :, sw, 0:GROUPS, ROT:HD], table("cos", GROUPS),
                     table("sin", GROUPS), rt[:, 0, :, 0:GROUPS], rt[:, 1, :, 0:GROUPS], roped, sw + 2)

            def ctable(name):
                return const(name, NCMP).unsqueeze(1).to_broadcast([NCMP, GROUPS, ROT])

            pool.wait_ge(kc_done, 1)
            rope(kc[:, :, 0:ROT], kc[:, :, ROT:HD], ctable("cosc"), ctable("sinc"), crt[:, 0], crt[:, 1], kcr_done, 1)

            pool.wait_ge(abT_done, 1)
            pool.wait_ge(cmp_used, 8)
            asel = const("augsel", 2 * FOX_H)
            for h in range(FOX_H):
                nc.gpsimd.tensor_scalar(aug[:, h, :], abT[:, 0, :], asel[:, h:h + 1], None, ALU.mult).then_inc(aug_done, 1)

            places = eidx[:].rearrange("p h s -> p (h s)")

            def gather_group(G, par, first=False):
                for s in range(GS):
                    if not first:
                        pool.wait_ge(down_used, G * GS + (s - RING + 1))
                        pool.sem_inc(turn, 1)
                    elif s < 4:
                        pool.wait_ge(lo_done, 4 * (NBLK - 1) + s + 1)
                    else:
                        pool.wait_ge(piece_used, 4 * NBLK)
                    if s == 0:
                        nc.gpsimd.tensor_copy(idx_stage[:, par], places[:, 0:GS] if first else
                                              places[:, bass.ds(G * GS, GS)]).then_inc(idx_copied, 1)
                        pool.wait_ge(idx_copied, G + 1)
                        if not first:
                            pool.sem_inc(turn, 1)
                    nc.gpsimd.indirect_dma_start(
                        down_rows[s][:], None, peer_expert_down[0],
                        bass.IndirectOffsetOnAxis(ap=idx_stage[:, par, s:s + 1], axis=0)).then_inc(down_in[s], 16)

            for pair in range(HALVES * PEER_H // 2):
                pool.wait_ge(eidx_done, pair + 1)
                if pair == 0:
                    gather_group(0, 0, first=True)
                    gather_group(1, 1)
                with pool.Fori(max(GPP * pair // 2, 1), GPP * (pair + 1) // 2) as i:
                    for q in range(2):
                        gather_group(i * 2 + q, q)

        @block.scalar
        def _(act):
            A = nc.scalar.activation
            n = [0]

            def seq(ins):
                ins.then_inc(act_seq, 1)
                n[0] += 1

            act.dma_start(ct[:], consts[:, 0:NCONST]).then_inc(setup_loaded, 16)

            def sqrt_table():
                A(sqrt_junk, eps[:, 0:1], ACT.Sqrt)

            def norm_stats(src, junk, i, half):
                seq(A(junk[:, half, :], src[:, half, :], ACT.Square, accum_out=ss[:, i:i + 1]))
                act.wait_ge(act_seq, n[0])
                A(rms[:, i:i + 1], ss[:, i:i + 1], ACT.Sqrt, bias=eps[:, 0:1], scale=1.0 / D).then_inc(squares, 1)

            def split_x(n0, gain, q):
                for k in range(4 * q, 4 * q + 4):
                    act.wait_ge(xT_ps, n0 + k + 1)
                    A(act_hi[:, k, :], psum[:, X_BANKS[n0 > 0][k % 4], 0:SEQ], ACT.Copy,
                      scale=cols[:, gain + k:gain + k + 1]).then_inc(act_hi_done, 1)

            act.wait_ge(const_done, 1)
            sqrt_table()
            act.wait_ge(x_loaded[0], 16)
            seq(A(sq[:, 0, :], x_in[:, 0, :], ACT.Square, accum_out=ss[:, 0:1]))
            def ld(dst, src):
                act.dma_start(dst, src).then_inc(late_loaded, 16)

            ld(bias32[:, 0:NGATE], nsa_gate_bias.partition_broadcast(P))
            ld(bias32[:, NGATE:32], fox_forget_bias.partition_broadcast(P))
            ld(gf_raw[:, :, 0:NGATE], w_in_v[:, :, G_N:G_N + NGATE])
            ld(gf_raw[:, :, NGATE:32], w_in_v[:, :, F_F:F_F + FOX_H])
            ld(w2[:, 0], k_cmp_w2[0].rearrange("(c p) d -> p c d", p=P))
            ld(w2[:, 1], v_cmp_w2[0].rearrange("(c p) d -> p c d", p=P))

            act.wait_ge(half_sum, 1)
            act.wait_ge(act_seq, n[0])
            A(rms[:, 0:HALVES], ss[:, 0:HALVES], ACT.Sqrt, bias=eps[:, 0:1], scale=1.0 / D).then_inc(squares, 1)
            act.wait_ge(cols_ps, 1)
            nc.scalar.copy(cols[:], psum[:, 7, 0:P]).then_inc(cols_done, 1)
            act.wait_ge(cols_done, 1)

            def hi_piece(b, p):
                act.wait_ge(raw_loaded[p], uses(b) * 16)
                if not (isinstance(b, int) and b == 0 and p < 2):
                    act.wait_ge(piece_used, b * 4 + (p - 1))
                nc.scalar.copy(w_hi[:, p % 2], raw[:, p]).then_inc(hi_done, 1)

            def evac(b):
                act.wait_ge(piece_used, 4 * (b + 1))
                bank = psum[:, bank_of(b), :]
                two = bank.rearrange("p (c t) -> p c t", t=SEQ)
                if b < 2:
                    dst = qn[:, 0, 4 * b:4 * b + 4, :].rearrange("p h d -> p (h d)")
                elif b == 2:
                    dst, bank = kvcT[:, 0], two
                elif b < 5:
                    dst = kvsw[:, 0, b - 3].rearrange("p h d -> p (h d)")
                elif b < 9:
                    dst, bank = qkfT[:, 4 * (b - 5):4 * (b - 5) + 2, :], two
                elif b < 11:
                    dst = vf[:, 0, 512 * (b - 9):512 * (b - 9) + 512]
                else:
                    c = b - QRY0
                    dst, bank = qT[:, 4 * c:4 * c + 2, :], psum[:, 4 * (b % 2), :].rearrange("p (c t) -> p c t", t=SEQ)
                nc.scalar.copy(dst, bank).then_inc(actA, 1)

            def hook(b):
                if b == 2:
                    act.wait_ge(gf_ps, 1)
                    nc.scalar.copy(gfT[:], psum[0:32, 7, 0:SEQ]).then_inc(gfT_done, 1)
                if b == 3:
                    act.wait_ge(fx_done, 1)
                    seq(A(ez[:], az[:], ACT.Exp, scale=-1.0))
                    seq(A(tg[:], gz[:, :, 0:NGATE], ACT.Tanh, scale=0.5))
                    act.wait_ge(act_seq, n[0])
                    A(lz[:], ez[:], ACT.Ln, bias=1.0).then_inc(gt_done, 1)
                if b == 5:
                    act.wait_ge(cmp_used, 8)
                    for kv in range(2):
                        nc.scalar.copy(hid[:, kv, :], psum[0:GROUPS * NCMP, 6 + kv, 0:CMP_HID]).then_inc(ga_done, 1)
                if b == 6:
                    act.wait_ge(ab_ps, 1)
                    nc.scalar.copy(abT[:].rearrange("p x t -> p (x t)"), psum[0:2 * FOX_H, 4, :]).then_inc(abT_done, 1)
                    act.wait_ge(gelu_in, 1)
                    A(hid2[:], hid1[:], ACT.Tanh, scale=GELU_C0).then_inc(gelu_tanh, 1)
                if b == 7:
                    act.wait_ge(hidT_ps, 1)
                    nc.scalar.copy(hidT[:].rearrange("p v c n -> p (v c n)"), psum[:, 7, 0:4 * GROUPS * NCMP]).then_inc(hidT_done, 1)
                if b == 8:
                    act.wait_ge(kvc_ps, 1)
                    nc.scalar.copy(kc[:].rearrange("p g d -> p (g d)"), psum[0:NCMP, 6, 0:256]).then_inc(kc_done, 1)
                if b == 9:
                    for f in range(2):
                        act.wait_ge(fill_ps, f + 1)
                        nc.scalar.copy(qnT[:, 2 * f:2 * f + 2, :].rearrange("p h t -> p (h t)"), psum[:, 4 + f, :]).then_inc(fillA, 1)
                if b == 10:
                    act.wait_ge(fill_ps, 5)
                    nc.scalar.copy(kswT[:, 0].rearrange("p g t -> p (g t)"), psum[:, 4, :]).then_inc(fillA, 1)
                    act.wait_ge(kcT_ps, 1)
                    nc.scalar.copy(kcT.rearrange("p g n -> p (g n)"), psum[:, 6, 0:2 * NCMP]).then_inc(kcT_done, 1)

            for b in range(GATES0):
                hi_piece(b, 0)
                if b == 0:
                    split_x(0, MIX_G, 0)
                if b == 0:
                    split_x(0, MIX_G, 1)
                hi_piece(b, 1)
                if b >= 1:
                    evac(b - 1)
                hook(b)
                if b == 0:
                    split_x(0, MIX_G, 2)
                hi_piece(b, 2)
                if b == 0:
                    split_x(0, MIX_G, 3)
                hi_piece(b, 3)
                if b == 0:
                    act.wait_ge(late_loaded, 16 * NLATE)
                    nc.scalar.copy(gf_hi[:], gf_raw[:]).then_inc(gf_hi_done, 1)
            evac(GATES0 - 1)

            def exp_unit(u):
                act.wait_ge(masked, u + 1)
                pr = prob[:, u % P_RING, :]
                A(pr[:, 0:P], pr[:, 0:P], ACT.Exp, bias=negmax[:, u, 0:1], scale=-1.0, accum_out=psums[:, u, 0:1])
                A(pr[:, P:384], pr[:, P:384], ACT.Exp, bias=negmax[:, u, 1:2], scale=-1.0,
                  accum_out=psums[:, u, 1:2]).then_inc(exped, 1)

            def pT_out(u):
                act.wait_ge(pT_ps, u + 1)
                if u >= 2:
                    act.wait_ge(pv_done, u - 1)
                nc.scalar.copy(pT[:, u % 2, :], psum[:, 2 + u % 2, 0:384]).then_inc(pT_done, 1)

            def head_hi(hs):
                act.wait_ge(pv_done, last_unit(hs) + 1)
                nc.scalar.copy(o_hi[:, o_place(hs), :], psum[:, 4 + hs % 2, 0:SEQ]).then_inc(o_hi_done, 1)

            done_at = {last_unit(hs) + 3: hs for hs in range(16)}
            hi_piece(GATES0, 0)
            for t in range(NU + 4):
                if 2 <= t < NU + 2:
                    pT_out(t - 2)
                if t == NU:
                    hi_piece(GATES0, 1)
                if t < NU:
                    exp_unit(t)
                    kind, h = UNITS[t]
                    if kind == "sel":
                        act.wait_ge(pcT_ps, h + 1)
                        if h >= 2:
                            act.wait_ge(pv_done, FOX_H + 2 * (h - 2) + 1)
                        nc.scalar.copy(pcT[:, h % 2, :], psum[0:NCMP, 6, 0:SEQ]).then_inc(pcT_done, 1)
                if t == 3:
                    act.wait_ge(c2_done, 1)
                    A(cp[:, 1], cp[:, 0], ACT.Exp).then_inc(ce_done, 1)
                if t - 1 in done_at:
                    head_hi(done_at[t - 1])

            def gate_evac(b, par):
                g = b - GATES0
                for c in range(4):
                    src = psum[:, 2 * par + c // 2, (c % 2) * SEQ:(c % 2 + 1) * SEQ]
                    if isinstance(b, int):
                        dst, bias = gateT[:, 4 * g + c, :], hbias[:, 4 * g + c:4 * g + c + 1]
                    else:
                        dst = gateT[:, bass.ds(g * 4 + c, 1), :].rearrange("p o t -> p (o t)")
                        bias = hbias[:, bass.ds(g * 4 + c, 1)]
                    ins = A(dst, src, ACT.Tanh, bias=bias, scale=0.5)
                ins.then_inc(actA, 1)

            def hi4(b, middle):
                hi_piece(b, 0)
                hi_piece(b, 1)
                middle()
                hi_piece(b, 2)
                hi_piece(b, 3)

            def gates_block(b, par):
                def middle():
                    act.wait_ge(piece_used, b * 4)
                    gate_evac(b - 1, 1 - par)
                hi4(b, middle)

            act.wait_ge(hbias_done, 1)
            act.wait_ge(pv_done, NU)
            hi_piece(GATES0, 2)
            hi_piece(GATES0, 3)
            with act.Fori(0, (UPS0 - GATES0) // 2 - 1) as i:
                for q in range(2):
                    gates_block(i * 2 + (GATES0 + 1 + q), (GATES0 + 1 + q) % 2)
            gates_block(UPS0 - 1, (UPS0 - 1) % 2)

            def merged_hi(c):
                act.wait_ge(up_sum, c + 1)
                A(act_hi[:, 4 * c:4 * c + 4, :], up_a[:], ACT.Copy, scale=0.5).then_inc(mer_hi, 1)

            gates_block(UPS0, UPS0 % 2)
            for c in range(1, 5):
                for p in range(3):
                    hi_piece(UPS0 + c, p)
                merged_hi(c - 1)
                hi_piece(UPS0 + c, 3)
            act.dma_start(keys[:, 0], peer_sub_keys_1[0].rearrange("h k d -> k h d")).then_inc(keys_loaded, 16)
            act.dma_start(keys[:, 1], peer_sub_keys_2[0].rearrange("h k d -> k h d")).then_inc(keys_loaded, 16)
            act.dma_start(ffn_row[:], norm_ffn_gain.partition_broadcast(P)).then_inc(fin_loaded, 16)
            act.wait_ge(kcr_done, 1)
            act.dma_start(iota128[:], consts[:, NCONST:NCONST + NKEYS]).then_inc(fin_loaded, 16)
            def part_squares(c):
                act.wait_ge(dveA, OUT0 + c - 7)
                for half in range(HALVES):
                    ins = A(xn[:, half, 512 * c:512 * c + 512], xres[:, half, 512 * c:512 * c + 512], ACT.Square,
                            accum_out=ss4[:, half, c:c + 1])
                ins.then_inc(part_sums, 1)

            for c in range(1, 4):
                hi4(OUT0 + c, lambda: None)
                part_squares(c - 1)
            hi_piece(QRY0, 0)
            sqrt_table()
            for f in range(4):
                act.wait_ge(keyT_ps, f + 1)
                nc.scalar.copy(keysT[:, 4 * f:4 * f + 4, :].rearrange("p j k -> p (j k)"), psum[:, 6 + f % 2, :]).then_inc(keyT_done, 1)
            part_squares(3)
            act.wait_ge(ms_done, 1)
            A(rms[:, HALVES:2 * HALVES], ss[:, HALVES:2 * HALVES], ACT.Sqrt, bias=eps[:, 0:1],
              scale=1.0 / D).then_inc(squares, 1)
            hi_piece(QRY0, 1)
            split_x(KC, FFN_G, 0)
            split_x(KC, FFN_G, 1)
            for c in range(4):
                b = QRY0 + c
                if c > 0:
                    hi_piece(b, 0)
                    hi_piece(b, 1)
                    evac(b - 1)
                else:
                    split_x(KC, FFN_G, 2)
                hi_piece(b, 2)
                if c == 0:
                    split_x(KC, FFN_G, 3)
                hi_piece(b, 3)
            evac(NBLK - 1)

            def soft_exp_of(i, half, h0, h1):
                act.wait_ge(soft_in, i)
                A(gw[:, half, h0:h1], gw[:, half, h0:h1], ACT.Exp).then_inc(soft_exp, 1)

            def final_stats(half):
                act.wait_ge(x2_done, half + 1)
                norm_stats(xres, xn, 2 * HALVES + half, half)

            def soft_pairs(pairs):
                for k in pairs:
                    half, h = k // 4, 2 * (k % 4)
                    soft_exp_of(k + 1, half, h, h + 2)

            def numbers_out(half):
                act.wait_ge(num_ps, half + 1)
                nc.scalar.copy(numT[:, half].rearrange("p l t -> p (l t)"), psum[:, 0, 0:2 * P]).then_inc(numT_done, 1)

            def gelu_tanh_of(half):
                act.wait_ge(inner_done, half + 1)
                A(pabf[:, 1], pabf[:, 0], ACT.Tanh, scale=GELU_C0).then_inc(tanh_done, 1)

            def weights_out(half):
                act.wait_ge(w_ps, half + 1)
                nc.scalar.copy(wT[:], psum[:, 1, 0:P]).then_inc(wT_done, 1)

            def one_hots(b, half, par, t0, first=False):
                if not first:
                    act.wait_ge(W_ps, b - 1)
                qs = range(BT - ACT_TOKENS[half], BT)
                for q in qs:
                    A(oh[half][:, 0, par, q, :], iota128[:], ACT.Abs, bias=numT[:, half, 1, bass.ds(t0 + q, 1)],
                      scale=-1.0).then_inc(dist_done, 1)
                for q in qs:
                    before = b * ACT_TOKENS[0] if half == 0 else b * ACT_TOKENS[1] + NB * (ACT_TOKENS[0] - ACT_TOKENS[1])
                    act.wait_ge(dist_done, before + (q - qs[0] + 1))
                    ins = A(oh[half][:, 0, par, q, :], oh[half][:, 0, par, q, :], ACT.Relu, bias=1.0, scale=-1.0)
                ins.then_inc(oh2_ready, 1)

            def spread_out(b, half, par, t0):
                act.wait_ge(W_ps, b + 1)
                nc.scalar.copy(W[:, 1 - half, :, bass.ds(t0, BT)].rearrange("p i t -> p t i"),
                               psum[:, 2 + par, :].rearrange("p (t i) -> p t i", i=NKEYS)).then_inc(W_out, 1)

            soft_pairs(range(0, 4))
            numbers_out(0)
            soft_pairs(range(4, 6))
            gelu_tanh_of(0)
            weights_out(0)
            soft_pairs(range(6, 8))
            numbers_out(1)
            for q in range(2):
                one_hots(q, 0, q, BT * q, first=True)
            with act.Fori(0, NB // 2 - 1) as i:
                for q in range(2):
                    spread_out(i * 2 + q, 0, q, i * (2 * BT) + BT * q)
                    one_hots(i * 2 + (q + 2), 0, q, i * (2 * BT) + BT * (q + 2))
            for q in range(2):
                spread_out(NB - 2 + q, 0, q, P - 2 * BT + BT * q)

            def u_high(i, q, turn_, first=False):
                act.wait_ge(u_loaded[q], turn_ * 16)
                if not first:
                    act.wait_ge(chunk_used, i - 1)
                nc.scalar.copy(u_hi[:, q, :], u_raw[:, q, :]).then_inc(u_hi_done, 1)

            def c_high(i, q):
                w = W[:, :, bass.ds(i, 1), :].rearrange("p h o t -> p h (o t)")
                nc.scalar.copy(c_hi[:, q], w).then_inc(c_hi_done, 1)

            act.wait_ge(ks_ps, 5)
            u_high(0, 0, 1, first=True)
            u_high(1, 1, 1, first=True)
            gelu_tanh_of(1)
            weights_out(1)
            for q in range(2):
                one_hots(NB + q, 1, q, BT * q)
            with act.Fori(NB // 2, NB - 1) as i:
                for q in range(2):
                    spread_out(i * 2 + q, 1, q, i * (2 * BT) + (BT * q - P))
                    one_hots(i * 2 + (q + 2), 1, q, i * (2 * BT) + (BT * (q + 2) - P))
            for q in range(2):
                spread_out(2 * NB - 2 + q, 1, q, P - 2 * BT + BT * q)
            act.wait_ge(W_out, 2 * NB)
            c_high(0, 0)
            c_high(1, 1)
            with act.Fori(1, NKEYS // 2) as i:
                for q in range(2):
                    act.wait_ge(chunk_used, i * 2 + (q - 1))
                    c_high(i * 2 + q, q)
                    u_high(i * 2 + q, q, i + 1)
            sqrt_table()
            for half in range(HALVES):
                final_stats(half)

        @block.vector
        def _(dve):
            V = nc.vector
            tt, ts, stt = V.tensor_tensor, V.tensor_scalar, V.scalar_tensor_tensor
            n = [0]

            def seq(ins):
                ins.then_inc(dve_seq, 1)
                n[0] += 1

            def settle():
                dve.wait_ge(dve_seq, n[0])

            V.memset(ones[:], 1.0)
            V.memset(ab[:, 0, :, FOX_H:], 1.0)
            V.memset(ab[:, 1, :, 0:FOX_H], 1.0)
            V.memset(eps, EPS).then_inc(const_done, 1)

            def inverse_rms(i0, count):
                dve.wait_ge(squares, count)
                seq(V.reciprocal(rstd[:, i0:i0 + HALVES], rms[:, i0:i0 + HALVES]))
                settle()

            def scale_rows(dst, src, i0, q):
                cs = slice(512 * q, 512 * q + 512)
                for half in range(HALVES):
                    ins = ts(dst[:, half, cs], src[:, half, cs], rstd[:, i0 + half:i0 + half + 1], None, ALU.mult)
                ins.then_inc(normed, 1)

            def lo_x(n0, gain, q):
                for k in range(4 * q, 4 * q + 4):
                    dve.wait_ge(act_hi_done, n0 + k + 1)
                    stt(act_lo[:, k, :], psum[:, X_BANKS[n0 > 0][k % 4], 0:SEQ], cols[:, gain + k:gain + k + 1],
                        f32(act_hi[:, k, :]), ALU.mult, ALU.subtract).then_inc(act_lo_done, 1)

            dve.wait_ge(x_loaded[1], 16)
            V.tensor_tensor_reduce(out=sq[:, 1, :], in0=x_in[:, 1, :], in1=x_in[:, 1, :], scale=1.0, scalar=0.0,
                                   op0=ALU.mult, op1=ALU.add, accum_out=ss[:, 1:2]).then_inc(half_sum, 1)
            inverse_rms(0, 1)
            scale_rows(x_in, x_in, 0, 0)
            scale_rows(x_in, x_in, 0, 1)
            dve.wait_ge(cols_done, 1)
            ts(hbias, cols[:, MERGE_B:MERGE_B + 32], 0.5, None, ALU.mult).then_inc(hbias_done, 1)

            def lo_piece(b, p):
                dve.wait_ge(hi_done, b * 4 + (p + 1))
                tt(w_lo[:, p % 2], raw[:, p], f32(w_hi[:, p % 2]), ALU.subtract).then_inc(lo_done, 1)

            def evac(b):
                dve.wait_ge(piece_used, 4 * (b + 1))
                bank = psum[:, bank_of(b) + 1, :]
                two = bank.rearrange("p (c t) -> p c t", t=SEQ)
                if b < 2:
                    dst = qn[:, 1, 4 * b:4 * b + 4, :].rearrange("p h d -> p (h d)")
                elif b == 2:
                    dst, bank = kvcT[:, 1], two
                elif b < 5:
                    dst = kvsw[:, 1, b - 3].rearrange("p h d -> p (h d)")
                elif b < 9:
                    dst, bank = qkfT[:, 4 * (b - 5) + 2:4 * (b - 5) + 4, :], two
                elif b < 11:
                    dst = vf[:, 1, 512 * (b - 9):512 * (b - 9) + 512]
                elif b < QRY0:
                    c = b - OUT0
                    if c == 0:
                        dve.wait_ge(xres_loaded, 16)
                    for half in range(HALVES):
                        o = xres[:, half, 512 * c:512 * c + 512]
                        ins = tt(o, psum[:, bank_of(b) + half, :], o, ALU.add)
                    ins.then_inc(dveA, 1)
                    return
                else:
                    c = b - QRY0
                    dst, bank = qT[:, 4 * c + 2:4 * c + 4, :], two
                V.tensor_copy(dst, bank).then_inc(dveA, 1)

            def hook(b):
                if b == 3:
                    dve.wait_ge(gfz_ps, 1)
                    dve.wait_ge(late_loaded, 16 * NLATE)
                    tt(gz[:], psum[:, 7, 0:64].rearrange("p (h c) -> p h c", c=32),
                       bias32.unsqueeze(1).to_broadcast([P, HALVES, 32]), ALU.add).then_inc(gz_done, 1)
                    dve.wait_ge(gz_done, 1)
                    f = gz[:, :, NGATE:32]
                    seq(ts(nz[:], f, -1.0, None, ALU.mult))
                    settle()
                    tt(az[:], f, nz[:], ALU.max).then_inc(fx_done, 1)
                    dve.wait_ge(actA, 3)
                    dve.wait_ge(dveA, 3)
                    for kv, pc0 in ((0, KPOS), (1, VPOS)):
                        tok = kvcT[:, kv].rearrange("p g (n r) -> p r g n", r=CMP_STRIDE)
                        for m in range(2):
                            rs = slice(CMP_STRIDE * m, CMP_STRIDE * (m + 1))
                            pe_ = cols[:, pc0 + CMP_STRIDE * m:pc0 + CMP_STRIDE * (m + 1)]
                            for g in range(GROUPS):
                                ins = tt(flat[:, kv, rs, g, :], tok[:, :, g, m:m + NCMP],
                                         pe_.unsqueeze(2).to_broadcast([P, CMP_STRIDE, NCMP]), ALU.add)
                    ins.then_inc(flat_done, 1)
                if b == 4:
                    dve.wait_ge(gt_done, 1)
                    stt(lf[:], gz[:, :, NGATE:32], 0.0, lz[:], ALU.min, ALU.subtract).then_inc(lf_done, 1)
                    seq(ts(gate[:], tg[:], 0.5, 0.5, ALU.mult, ALU.add))
                if b == 5:
                    dve.wait_ge(cum_ps, 1)
                    c_ = psum[:, 5, 0:16].rearrange("p (h c) -> p h c", c=FOX_H)
                    ts(ab[:, 0, :, 0:FOX_H], c_, 1.0 / SCALE, None, ALU.mult)
                    ts(ab[:, 1, :, FOX_H:], c_, -1.0 / SCALE, None, ALU.mult).then_inc(ab_done, 1)
                if b == 6:
                    dve.wait_ge(ga_done, 2)
                    seq(tt(hid1[:], hid[:], hid[:], ALU.mult))
                    settle()
                    seq(ts(hid2[:], hid1[:], GELU_C1, 1.0, ALU.mult, ALU.add))
                    settle()
                    tt(hid1[:], hid2[:], hid[:], ALU.mult).then_inc(gelu_in, 1)
                    dve.wait_ge(gelu_tanh, 1)
                    seq(stt(hid1[:], hid2[:], 1.0, hid[:], ALU.add, ALU.mult))
                    settle()
                    ts(hid2[:], hid1[:], 0.5, None, ALU.mult).then_inc(gy_done, 1)
                if b == 8:
                    dve.wait_ge(kc_done, 1)
                    V.tensor_copy(vc.rearrange("p g d -> p (g d)"), psum[0:NCMP, 6, 256:512]).then_inc(vc_done, 1)
                if b == 9:
                    for f in (2, 3):
                        dve.wait_ge(fill_ps, f + 1)
                        V.tensor_copy(qnT[:, 2 * f:2 * f + 2, :].rearrange("p h t -> p (h t)"), psum[:, 4 + f, :]).then_inc(fillD, 1)
                if b == 10:
                    dve.wait_ge(fill_ps, 6)
                    V.tensor_copy(kswT[:, 1].rearrange("p g t -> p (g t)"), psum[:, 5, :]).then_inc(fillD, 1)

            for b in range(GATES0):
                lo_piece(b, 0)
                if b == 0:
                    lo_x(0, MIX_G, 0)
                    scale_rows(x_in, x_in, 0, 2)
                if b == 0:
                    lo_x(0, MIX_G, 1)
                    scale_rows(x_in, x_in, 0, 3)
                lo_piece(b, 1)
                if b >= 1:
                    evac(b - 1)
                hook(b)
                if b == 0:
                    lo_x(0, MIX_G, 2)
                lo_piece(b, 2)
                if b == 0:
                    lo_x(0, MIX_G, 3)
                lo_piece(b, 3)
                if b == 0:
                    dve.wait_ge(gf_hi_done, 1)
                    tt(gf_lo[:], gf_raw[:], f32(gf_hi[:]), ALU.subtract).then_inc(gf_lo_done, 1)
            evac(GATES0 - 1)

            mask = const("mask")

            def mask_unit(u):
                dve.wait_ge(score_ps, u + 1)
                if u >= P_RING:
                    dve.wait_ge(pT_ps, u - P_RING + 1)
                for half in range(HALVES):
                    cs = slice(0, P) if half == 0 else slice(P, 384)
                    ins = V.tensor_tensor_reduce(out=prob[:, u % P_RING, cs], in0=psum[:, u % 2, cs],
                                                 in1=mask[:, 0:P] if half == 0 else mask[:, P:384],
                                                 scale=-SCALE, scalar=-LOWEST, op0=ALU.add, op1=ALU.min,
                                                 accum_out=negmax[:, u, half:half + 1])
                ins.then_inc(masked, 1)

            def scale_unit(u):
                kind, h = UNITS[u]
                dve.wait_ge(exped, u + 1)
                if kind == "fox":
                    seq(V.reciprocal(pscale[:, u, :], psums[:, u, :]))
                else:
                    seq(V.reciprocal(prec[:, u, :], psums[:, u, :]))
                    settle()
                    col = 3 * h + 1 + ("sel", "win").index(kind)
                    seq(tt(pscale[:, u, :], prec[:, u, :], gate[:, :, col], ALU.mult))
                settle()
                pr = prob[:, u % P_RING, :]
                ts(pr[:, 0:P], pr[:, 0:P], pscale[:, u, 0:1], None, ALU.mult)
                ts(pr[:, P:384], pr[:, P:384], pscale[:, u, 1:2], None, ALU.mult).then_inc(p_ready, 1)

            def head_lo(hs):
                dve.wait_ge(o_hi_done, hs + 1)
                o = o_place(hs)
                tt(o_lo[:, o, :], psum[:, 4 + hs % 2, 0:SEQ], f32(o_hi[:, o, :]), ALU.subtract).then_inc(o_lo_done, 1)

            hn = [P, HALVES, NSA_H, NCMP]

            def over_heads(name):
                return const(name).rearrange("p (h n) -> p h n", n=NCMP).unsqueeze(2).to_broadcast(hn)

            def over_blocks(a):
                return a.rearrange("p (h c) -> p h c", c=NSA_H).unsqueeze(3).to_broadcast(hn)

            def cmp_before_exp():
                dve.wait_ge(cs_ps, 1)
                s_ = psum[:, 7, 0:256].rearrange("p (h c n) -> p h c n", h=HALVES, n=16)[:, :, :, 0:NCMP]
                for half in range(HALVES):
                    cn = over_heads("cneg")[:, half]
                    ins = stt(cp[:, 1, half], s_[:, half], SCALE, cn, ALU.mult, ALU.add)
                seq(ins)
                settle()
                seq(V.tensor_reduce(cmx, cp[:, 1], AX_X, ALU.max))
                settle()
                tt(cp[:, 0], cp[:, 1], over_blocks(cmx), ALU.subtract).then_inc(c2_done, 1)

            def cmp_after_exp():
                dve.wait_ge(ce_done, 1)
                seq(tt(cp[:, 2], cp[:, 1], over_heads("c01"), ALU.mult))
                settle()
                seq(V.tensor_reduce(csum, cp[:, 2], AX_X, ALU.add))
                settle()
                seq(ts(cmx, csum, TINY, None, ALU.max))
                settle()
                seq(V.reciprocal(csum, cmx))
                settle()
                seq(tt(crec.rearrange("p (h c) -> p h c", c=NSA_H), csum.rearrange("p (h c) -> p h c", c=NSA_H),
                       gate[:].rearrange("p h (c b) -> p h c b", b=3)[:, :, :, 0], ALU.mult))
                settle()
                tt(cp[:, 3], cp[:, 2], over_blocks(crec), ALU.mult).then_inc(pc_done, 1)

            done_at = {last_unit(hs) + 4: hs for hs in range(16)}
            lo_piece(GATES0, 0)
            for t in range(NU + 4):
                if t < NU:
                    mask_unit(t)
                if t == NU + 1:
                    lo_piece(GATES0, 1)
                if 1 <= t <= NU:
                    scale_unit(t - 1)
                if t == 1:
                    cmp_before_exp()
                if t == 5:
                    cmp_after_exp()
                if t in done_at:
                    head_lo(done_at[t])

            lo_piece(GATES0, 2)
            lo_piece(GATES0, 3)
            with dve.Fori(1, UPS0 - GATES0) as i:
                for p in range(PIECES):
                    lo_piece(i + GATES0, p)

            def up_out(c):
                b = UPS0 + c
                dve.wait_ge(piece_used, 4 * (b + 1))
                dve.wait_ge(actA, UPS0)
                bank = bank_of(b)
                for x_, o in ((0, up_a), (1, up_b)):
                    ps = psum[:, bank + 2 * x_:bank + 2 * x_ + 2, :].rearrange("p k t -> p (k t)")
                    g = gateT[:, 16 * x_ + 4 * c:16 * x_ + 4 * c + 4, :].rearrange("p k t -> p (k t)")
                    last = stt(o[:].rearrange("p k t -> p (k t)"), g, 1.0, ps, ALU.add, ALU.mult)
                last.then_inc(dveA, 1)
                dve.wait_ge(dveA, b - 7)
                tt(up_a[:], up_a[:], up_b[:], ALU.add).then_inc(up_sum, 1)

            def merged_lo(c):
                dve.wait_ge(mer_hi, c + 1)
                stt(act_lo[:, 4 * c:4 * c + 4, :], up_a[:], 0.5, f32(act_hi[:, 4 * c:4 * c + 4, :]),
                    ALU.mult, ALU.subtract).then_inc(mer_lo, 1)
                dve.wait_ge(mer_lo, c + 1)

            for b in range(UPS0, QRY0):
                lo_piece(b, 0)
                lo_piece(b, 1)
                if b > OUT0:
                    evac(b - 1)
                elif b > UPS0:
                    up_out(b - 1 - UPS0)
                lo_piece(b, 2)
                if UPS0 < b <= OUT0:
                    merged_lo(b - 1 - UPS0)
                lo_piece(b, 3)

            def top16(lists):
                for src, scratch, v, ix in lists:
                    seq(V.max(v[:, 0:8], src))
                settle()
                for src, scratch, v, ix in lists:
                    seq(V.max_index(ix[:, 0:8], v[:, 0:8], src))
                    seq(V.match_replace(scratch, v[:, 0:8], src, LOWEST))
                settle()
                for src, scratch, v, ix in lists:
                    seq(V.max(v[:, 8:16], scratch))
                settle()
                for src, scratch, v, ix in lists:
                    seq(V.max_index(ix[:, 8:16], v[:, 8:16], scratch))

            def top_lists(half, h):
                def scores(j):
                    return psum[:, SCORE_BANKS[half][j // 4], (j % 4) * NKEYS:(j % 4 + 1) * NKEYS]
                top16([(scores(2 * h + l), list2[:, 2 * (h % 2) + l, :], val[:, half, h, l, :], ind[:, half, h, l, :])
                       for l in range(2)])
                settle()
                if h % 2 == 1 and (half == 0 or h == PEER_H - 1):
                    V.sem_inc(topk_read, 1)

            def top_sums(half, h):
                cd = cand[:, h % 2]
                seq(tt(cd, val[:, half, h, 0, :].unsqueeze(2).to_broadcast([P, TOPK, TOPK]),
                       val[:, half, h, 1, :].unsqueeze(1).to_broadcast([P, TOPK, TOPK]), ALU.add))
                settle()
                top16([(cd.rearrange("p a b -> p (a b)"), cand2[:, h % 2, :], top[:, half, h, :], pos[:, half, h, :])])
                settle()

            def topk_end(half, h0, h1):
                nh = h1 - h0
                hs = slice(h0, h1)
                ns = nh * TOPK
                g = gw[:, half, hs]
                tt(g, top[:, half, hs], top[:, half, hs, 0:1].to_broadcast([P, nh, TOPK]), ALU.subtract).then_inc(soft_in, 1)
                if half == 1 and h0 == 0:
                    dve.wait_ge(num_ps, 1)
                seq(ts(pab[:, 0, hs], pos[:, half, hs], 4, None, ALU.logical_shift_right))
                seq(ts(pab[:, 1, hs], pos[:, half, hs], 15, None, ALU.bitwise_and))
                seq(V.tensor_copy(indf[:, hs], ind[:, half, hs]))
                settle()
                seq(V.tensor_copy(pabf[:, :, hs], pab[:, :, hs]))
                settle()
                full = [P, nh, TOPK, TOPK]
                iota = const("iota").unsqueeze(1).to_broadcast([P, ns, TOPK])
                oh = onehot[:, hs].rearrange("p h s c -> p (h s) c")
                ks = slice(h0 * TOPK, h1 * TOPK)
                for l in range(2):
                    seq(tt(oh, pabf[:, l, hs].rearrange("p h s -> p (h s)").unsqueeze(2).to_broadcast([P, ns, TOPK]),
                           iota, ALU.is_equal))
                    settle()
                    seq(tt(onehot[:, hs], onehot[:, hs], indf[:, hs, l, :].unsqueeze(2).to_broadcast(full), ALU.mult))
                    settle()
                    seq(V.tensor_reduce(key12[:, l, ks], oh, AX_X, ALU.add))
                    settle()
                seq(stt(eidf[:, ks], key12[:, 0, ks], float(NKEYS), key12[:, 1, ks], ALU.mult, ALU.add))
                settle()
                V.tensor_copy(eidx[:, half, ks], eidf[:, ks]).then_inc(eidx_done, 1)
                if h1 == PEER_H:
                    V.sem_inc(num_done, 1)

            def topk_weights(count, half, h0, h1):
                hs = slice(h0, h1)
                g = gw[:, half, hs]
                dve.wait_ge(soft_exp, count)
                seq(V.tensor_reduce(wsum[:, 0, hs], g, AX_X, ALU.add))
                settle()
                seq(V.reciprocal(wsum[:, 1, hs], wsum[:, 0, hs]))
                settle()
                seq(tt(g, g, wsum[:, 1, hs].unsqueeze(2).to_broadcast([P, h1 - h0, TOPK]), ALU.mult))
                settle()

            lo_piece(QRY0, 0)
            evac(QRY0 - 1)
            dve.wait_ge(part_sums, 4)
            V.tensor_reduce(ss[:, HALVES:2 * HALVES], ss4[:], AX_X, ALU.add).then_inc(ms_done, 1)
            inverse_rms(HALVES, 2)
            scale_rows(xn, xres, HALVES, 0)
            scale_rows(xn, xres, HALVES, 1)
            lo_x(KC, FFN_G, 0)
            scale_rows(xn, xres, HALVES, 2)
            lo_piece(QRY0, 1)
            lo_x(KC, FFN_G, 1)
            scale_rows(xn, xres, HALVES, 3)

            def with_gain(half):
                dve.wait_ge(fin_loaded, 32)
                dve.wait_ge(xT_ps, 2 * KC)
                seq(tt(xn[:, half, :], xn[:, half, :], ffn_row[:], ALU.mult))

            def dot(G, half, s):
                dve.wait_ge(down_in[s], G * 16 + 16)
                V.tensor_tensor_reduce(out=down_rows[s][:], in0=down_rows[s][:],
                                       in1=xn[:, half, :], scale=1.0, scalar=0.0, op0=ALU.mult, op1=ALU.add,
                                       accum_out=acc[:, s:s + 1]).then_inc(down_used, 1)

            lo_x(KC, FFN_G, 2)
            lo_piece(QRY0, 2)
            lo_x(KC, FFN_G, 3)
            lo_piece(QRY0, 3)
            with_gain(0)
            for c in (1, 2):
                b = QRY0 + c
                lo_piece(b, 0)
                if c == 2:
                    top_sums(0, 0)
                evac(b - 1)
                lo_piece(b, 1)
                if c == 1:
                    with_gain(1)
                else:
                    top_sums(0, 1)
                    topk_end(0, 0, 2)
                lo_piece(b, 2)
                dve.wait_ge(ks_ps, c)
                top_lists(0, 2 * c - 2)
                lo_piece(b, 3)
                top_lists(0, 2 * c - 1)
            lo_piece(NBLK - 1, 0)
            evac(NBLK - 2)
            lo_piece(NBLK - 1, 1)
            dot(0, 0, 0)
            lo_piece(NBLK - 1, 2)
            dot(0, 0, 1)
            lo_piece(NBLK - 1, 3)
            dot(0, 0, 2)
            dot(0, 0, 3)
            evac(NBLK - 1)
            topk_weights(1, 0, 0, 2)

            all_dots = dots[:].rearrange("p h s -> p (h s)")

            def group(G, half, begun=0):
                if begun == 0:
                    dve.wait_ge(acc_out, G)
                for s in range(begun, GS):
                    dot(G, half, s)
                dve.wait_ge(down_used, G * GS + GS)
                V.tensor_copy(all_dots[:, bass.ds(G * GS, GS)], acc[:]).then_inc(acc_out, 1)

            def weights(half):
                dve.wait_ge(acc_out, GPH * (half + 1))
                a = dots[:, half, :].rearrange("p (h s) -> p h s", s=TOPK)
                g1, g2 = pabf[:, 0], pabf[:, 1]
                seq(tt(g1, a, a, ALU.mult))
                settle()
                seq(ts(g2, g1, GELU_C1, 1.0, ALU.mult, ALU.add))
                settle()
                tt(g1, g2, a, ALU.mult).then_inc(inner_done, 1)
                dve.wait_ge(tanh_done, half + 1)
                seq(stt(g1, g2, 1.0, a, ALU.add, ALU.mult))
                settle()
                stt(gw[:, half], g1, 0.5, gw[:, half], ALU.mult, ALU.mult).then_inc(w_done, 1)

            def one_hots(b, half, par, t0, first=False):
                mine = BT - ACT_TOKENS[half]
                if not first:
                    dve.wait_ge(W_ps, b - 1)
                if mine:
                    n2 = numT[:, half, 1, bass.ds(t0, mine)].unsqueeze(2).to_broadcast([P, mine, NKEYS])
                    tt(oh[half][:, 0, par, 0:mine], iota128[:].unsqueeze(1).to_broadcast([P, mine, NKEYS]), n2, ALU.is_equal)
                for q in range(BT):
                    ins = ts(oh[half][:, 1, par, q, :], iota128[:], numT[:, half, 0, bass.ds(t0 + q, 1)],
                             wT[:, bass.ds(t0 + q, 1)], ALU.is_equal, ALU.mult)
                ins.then_inc(oh_ready, 1)

            def u_low(i, q):
                dve.wait_ge(u_hi_done, i + 1)
                tt(u_lo[q][:], u_raw[:, q, :], f32(u_hi[:, q, :]), ALU.subtract).then_inc(u_lo_done, 1)

            def c_low(i, q):
                dve.wait_ge(c_hi_done, i + 1)
                w = W[:, :, bass.ds(i, 1), :].rearrange("p h o t -> p h (o t)")
                tt(c_lo[q][:], w, f32(c_hi[:, q]), ALU.subtract).then_inc(c_lo_done, 1)

            def residual(half):
                dve.wait_ge(half_summed if half == 0 else chunk_used, NKEYS)
                tt(xres[:, half, :], psum[:, 4 * half:4 * half + 4, :].rearrange("p k n -> p (k n)"),
                   xres[:, half, :], ALU.add).then_inc(x2_done, 1)

            def final(half):
                dve.wait_ge(squares, 3 + half)
                i = 2 * HALVES + half
                seq(V.reciprocal(rstd[:, i:i + 1], rms[:, i:i + 1]))
                settle()
                dve.wait_ge(row_loaded, 16)
                for cs in OUT_COLS:
                    stt(xn[:, half, cs], xres[:, half, cs], rstd[:, i:i + 1], final_row[:, cs], ALU.mult, ALU.mult).then_inc(y_done, 1)

            def between(G):
                if G < 2:
                    k, part = 1, G + 1
                else:
                    k, part = ((G - 2) // 3 + 2, (G - 2) % 3) if G < 8 else ((G - 8) // 3 + 4, (G - 8) % 3)
                half, h = k // 4, 2 * (k % 4)
                if part == 0:
                    dve.wait_ge(ks_ps, 4 if half == 0 else 5)
                    top_lists(half, h)
                    top_lists(half, h + 1)
                elif part == 1:
                    top_sums(half, h)
                    top_sums(half, h + 1)
                else:
                    topk_end(half, h, h + 2)
                    topk_weights(k + 1, half, h, h + 2)

            for G in range(20):
                group(G, G // GPH, begun=4 if G == 0 else 0)
                if G == GPH - 1:
                    between(G)
                    weights(0)
                else:
                    between(G)
            dve.wait_ge(numT_done, 2)
            dve.wait_ge(wT_done, 1)
            group(20, 1)
            for q in range(4):
                one_hots(q, 0, q % 2, BT * q, first=q < 2)
            with dve.Fori(21, 28) as i:
                group(i, 1)
                for q in range(4):
                    one_hots(i * 4 + (q - 80), 0, q % 2, i * (4 * BT) + (BT * q - 20 * 4 * BT))
            with dve.Fori(28, NG - 1) as i:
                group(i, 1)
            u_low(0, 0)
            group(NG - 1, 1)
            weights(1)
            dve.wait_ge(wT_done, 2)
            with dve.Fori(NB // 2, NB) as i:
                for q in range(2):
                    one_hots(i * 2 + q, 1, q, i * (2 * BT) + (BT * q - P))
            dve.wait_ge(W_ps, 2 * NB)
            c_low(0, 0)
            u_low(1, 1)
            c_low(1, 1)
            with dve.Fori(1, NKEYS // 2) as i:
                for q in range(2):
                    c_low(i * 2 + q, q)
                    u_low(i * 2 + q, q)
            for half in range(HALVES):
                residual(half)
            for half in range(HALVES):
                final(half)


_INS = ['x', 'norm_mix_gain', 'w_in', 'nsa_gate_bias', 'fox_forget_bias', 'merge_gate_bias', 'k_cmp_pos', 'k_cmp_w1',
        'k_cmp_w2', 'v_cmp_pos', 'v_cmp_w1', 'v_cmp_w2', 'w_up_nsa', 'w_up_fox', 'w_out', 'norm_ffn_gain',
        'peer_w_query', 'peer_sub_keys_1', 'peer_sub_keys_2', 'peer_expert_down', 'peer_expert_up',
        'norm_final_gain']


def kernel(**inputs):
    import concourse.bacc as _bacc
    from concourse.bass_utils import run_bass_kernel_spmd as _run

    nc = _bacc.Bacc("TRN2", target_bir_lowering=False, num_devices=1)
    arrays, args = {}, []
    for name in _INS:
        a = np.ascontiguousarray(inputs[name])
        arrays[f"in_{name}_dram"] = a
        args.append(nc.dram_tensor(f"in_{name}_dram", a.shape, mybir.dt.from_np(a.dtype), kind="ExternalInput").ap())
    table = const_table()
    arrays["in_consts_dram"] = table
    args.append(nc.dram_tensor("in_consts_dram", table.shape, F32, kind="ExternalInput").ap())
    args.append(nc.dram_tensor("out_0_dram", (1, SEQ, D), F32, kind="ExternalOutput").ap())
    build(nc, *args)
    r = _run(nc, [arrays], core_ids=[0])
    return r.results[0]["out_0_dram"]
```
